# Optimizing a Trainium2 kernel written in Bass

```python
import jax, jax.numpy as jnp
from jax import lax
import numpy as np

D_MODEL = 1024
BATCH = 1
SEQ = 256
DEPTH = 2

N_MIXERS = 2
N_NSA_LAYERS = (DEPTH + 1) // 2
N_HG_LAYERS = DEPTH // 2
EPS = 1e-6
ROPE_THETA = 10000.0

NSA_HEADS = 16
NSA_KV_GROUPS = 4
NSA_HPG = NSA_HEADS // NSA_KV_GROUPS
NSA_HEAD_DIM = D_MODEL // NSA_HEADS
NSA_Q_W = NSA_HEADS * NSA_HEAD_DIM
NSA_KV_W = NSA_KV_GROUPS * NSA_HEAD_DIM
NSA_IN = 2 * NSA_Q_W + 6 * NSA_KV_W + 3 * NSA_HEADS
CMP_BLOCK = 32
CMP_STRIDE = 16
CMP_HIDDEN = 4 * NSA_HEAD_DIM
SEL_BLOCK = 64
SEL_TOPK = 16
WINDOW = 512
NSA_QBLOCK = 128

HG_EXPAND = 128
HG_HEADS = D_MODEL // HG_EXPAND
HG_KDIM = HG_EXPAND
HG_VDIM = D_MODEL // HG_HEADS
HG_K_W = HG_HEADS * HG_KDIM
HG_V_W = HG_HEADS * HG_VDIM
HG_IN = 2 * HG_K_W + 2 * HG_V_W
HG_CHUNK = 64

kernel_name = "nsa_hgrn2_interleaved_hybrid"

def rms_norm(x, g):
    xf = x.astype(jnp.float32)
    y = xf * lax.rsqrt(jnp.mean(xf * xf, axis=-1, keepdims=True) + EPS)
    return (y * g.astype(jnp.float32)).astype(x.dtype)

def rope(x, pos):
    half = x.shape[-1] // 2
    inv = ROPE_THETA ** (-jnp.arange(half, dtype=jnp.float32) / half)
    ang = pos.astype(jnp.float32)[:, None] * inv[None, :]
    cos = jnp.cos(ang)[:, None, :]
    sin = jnp.sin(ang)[:, None, :]
    xf = x.astype(jnp.float32)
    x1, x2 = xf[..., :half], xf[..., half:]
    return jnp.concatenate([x1 * cos - x2 * sin, x2 * cos + x1 * sin], axis=-1).astype(x.dtype)

def masked_softmax(s, mask):
    p = jax.nn.softmax(jnp.where(mask, s, -1e30), axis=-1)
    return jnp.where(mask, p, 0.0)

def split_cols(a, sizes):
    offs = np.cumsum(sizes)[:-1].tolist()
    return jnp.split(a, offs, axis=-1)

def compress(kv, pe, w1, w2):
    B, S, G, hd = kv.shape
    n_cmp = (S - CMP_BLOCK) // CMP_STRIDE + 1
    idx = jnp.arange(n_cmp)[:, None] * CMP_STRIDE + jnp.arange(CMP_BLOCK)[None, :]
    blocks = kv[:, idx] + pe[:, None, :]
    flat = jnp.moveaxis(blocks, 3, 2).reshape(B, n_cmp, G, CMP_BLOCK * hd)
    return jax.nn.silu(flat @ w1) @ w2

def nsa_mixer(h, w_in, pe_k, pe_v, wk1, wk2, wv1, wv2, w_out):
    B, S, _ = h.shape
    H, G, R, hd = NSA_HEADS, NSA_KV_GROUPS, NSA_HPG, NSA_HEAD_DIM
    QB = NSA_QBLOCK
    scale = hd ** -0.5
    pos = jnp.arange(S)
    proj = h @ w_in
    q, kc, vc, ks, vs, kw, vw, gl, z = split_cols(proj, [NSA_Q_W] + [NSA_KV_W] * 6 + [3 * H, NSA_Q_W])
    q = rope(q.reshape(B, S, H, hd), pos).reshape(B, S, G, R, hd)
    gates = jax.nn.sigmoid(gl.astype(jnp.float32)).reshape(B, S, G, R, 3)
    kv = lambda a: a.reshape(B, S, G, hd)

    v_cmp = compress(kv(vc), pe_v, wv1, wv2)
    k_raw = compress(kv(kc), pe_k, wk1, wk2)
    n_cmp = k_raw.shape[1]
    cmp_start = jnp.arange(n_cmp) * CMP_STRIDE
    cmp_end = cmp_start + CMP_BLOCK - 1
    k_cmp = rope(k_raw, cmp_end)

    n_sel = S // SEL_BLOCK
    n_top = min(SEL_TOPK, n_sel)
    ks_blk = rope(kv(ks), pos).reshape(B, n_sel, SEL_BLOCK, G, hd).transpose(0, 3, 1, 2, 4)
    vs_blk = kv(vs).reshape(B, n_sel, SEL_BLOCK, G, hd).transpose(0, 3, 1, 2, 4)
    sel_start = jnp.arange(n_sel) * SEL_BLOCK
    overlap = ((cmp_start[:, None] < sel_start[None, :] + SEL_BLOCK)
               & (cmp_start[:, None] + CMP_BLOCK > sel_start[None, :])).astype(jnp.float32)
    bidx = jnp.arange(B)[:, None, None, None]
    gidx = jnp.arange(G)[None, None, :, None]
    sel_ids = jnp.arange(n_sel)

    pad = ((0, 0), (WINDOW, 0), (0, 0), (0, 0))
    kw_p = jnp.pad(rope(kv(kw), pos), pad)
    vw_p = jnp.pad(kv(vw), pad)

    def block_fn(s0):
        t = s0 + jnp.arange(QB)
        qb = lax.dynamic_slice_in_dim(q, s0, QB, axis=1)
        gb = lax.dynamic_slice_in_dim(gates, s0, QB, axis=1)
        sc = jnp.einsum('bqgrd,bngd->bqgrn', qb, k_cmp).astype(jnp.float32) * scale
        m_c = (cmp_end[None, :] <= t[:, None])[None, :, None, None, :]
        p_c = masked_softmax(sc, m_c)
        o_c = jnp.einsum('bqgrn,bngd->bqgrd', p_c.astype(v_cmp.dtype), v_cmp)
        imp = jnp.einsum('bqgrn,nj->bqgj', p_c, overlap)
        cur = t // SEL_BLOCK
        valid = sel_ids[None, :] <= cur[:, None]
        forced = (sel_ids[None, :] == 0) | (sel_ids[None, :] == cur[:, None]) | (sel_ids[None, :] == cur[:, None] - 1)
        score = jnp.where(forced[None, :, None, :], jnp.inf,
                          jnp.where(valid[None, :, None, :], imp, -jnp.inf))
        _, idx = lax.top_k(score, n_top)
        k_sel = ks_blk[bidx, gidx, idx].reshape(B, QB, G, n_top * SEL_BLOCK, hd)
        v_sel = vs_blk[bidx, gidx, idx].reshape(B, QB, G, n_top * SEL_BLOCK, hd)
        pos_sel = (idx[..., None] * SEL_BLOCK + jnp.arange(SEL_BLOCK)).reshape(B, QB, G, 1, n_top * SEL_BLOCK)
        m_s = pos_sel <= t[None, :, None, None, None]
        ss = jnp.einsum('bqgrd,bqgmd->bqgrm', qb, k_sel).astype(jnp.float32) * scale
        p_s = masked_softmax(ss, m_s)
        o_s = jnp.einsum('bqgrm,bqgmd->bqgrd', p_s.astype(v_sel.dtype), v_sel)
        kwb = lax.dynamic_slice_in_dim(kw_p, s0, WINDOW + QB, axis=1)
        vwb = lax.dynamic_slice_in_dim(vw_p, s0, WINDOW + QB, axis=1)
        pos_w = s0 - WINDOW + jnp.arange(WINDOW + QB)
        dlt = t[:, None] - pos_w[None, :]
        m_w = ((pos_w[None, :] >= 0) & (dlt >= 0) & (dlt < WINDOW))[None, :, None, None, :]
        sw = jnp.einsum('bqgrd,bkgd->bqgrk', qb, kwb).astype(jnp.float32) * scale
        p_w = masked_softmax(sw, m_w)
        o_w = jnp.einsum('bqgrk,bkgd->bqgrd', p_w.astype(vwb.dtype), vwb)
        o = gb[..., 0:1] * o_c + gb[..., 1:2] * o_s + gb[..., 2:3] * o_w
        return o.astype(h.dtype)

    o = lax.map(block_fn, jnp.arange(S // QB) * QB)
    o = o.transpose(1, 0, 2, 3, 4, 5).reshape(B, S, NSA_Q_W)
    return (o * jax.nn.silu(z)) @ w_out

def hgrn2_mixer(h, w_in, lb, g_norm, w_out):
    B, S, _ = h.shape
    H, dk, dv, C = HG_HEADS, HG_KDIM, HG_VDIM, HG_CHUNK
    NC = S // C
    proj = h @ w_in
    q_raw, f_raw, i_in, z = split_cols(proj, [HG_K_W, HG_K_W, HG_V_W, HG_V_W])
    q = jax.nn.silu(q_raw.astype(jnp.float32)).reshape(B, S, H, dk)
    f = lb[None, None, :] + (1.0 - lb[None, None, :]) * jax.nn.sigmoid(f_raw.astype(jnp.float32))
    k = (1.0 - f).reshape(B, S, H, dk)
    logf = jnp.log(f).reshape(B, S, H, dk)
    v = i_in.astype(jnp.float32).reshape(B, S, H, dv)
    to_chunks = lambda a: a.reshape(B, NC, C, H, a.shape[-1]).transpose(1, 0, 3, 2, 4)
    causal = jnp.tril(jnp.ones((C, C), dtype=bool))

    def step(state, inp):
        qc, kc, vc, lfc = inp
        b = jnp.cumsum(lfc, axis=2)
        o_inter = jnp.einsum('bhtk,bhkv->bhtv', qc * jnp.exp(b), state)
        diff = b[:, :, :, None, :] - b[:, :, None, :, :]
        decay = jnp.exp(jnp.where(causal[:, :, None], diff, -jnp.inf))
        att = jnp.einsum('bhtk,bhsk,bhtsk->bhts', qc, kc, decay)
        o = o_inter + jnp.einsum('bhts,bhsv->bhtv', att, vc)
        b_last = b[:, :, -1:, :]
        new_state = jnp.exp(b_last[:, :, 0, :])[..., None] * state + jnp.einsum(
            'bhsk,bhsv->bhkv', kc * jnp.exp(b_last - b), vc)
        return new_state, o

    state0 = jnp.zeros((B, H, dk, dv), jnp.float32)
    _, o = lax.scan(step, state0, (to_chunks(q), to_chunks(k), to_chunks(v), to_chunks(logf)))
    o = o.transpose(1, 0, 3, 2, 4).reshape(B, S, H, dv)
    o = o * lax.rsqrt(jnp.mean(o * o, axis=-1, keepdims=True) + EPS)
    o = (o.reshape(B, S, HG_V_W) * g_norm.astype(jnp.float32)).astype(h.dtype)
    return (o * jax.nn.silu(z)) @ w_out

def setup_inputs(seed: int = 0) -> dict:
    key = jax.random.key(seed)
    ks = jax.random.split(key, 16)
    nrm = lambda k, shape: jax.random.normal(k, shape, jnp.float32)
    w = lambda k, shape, fan_in: nrm(k, shape) * fan_in ** -0.5
    hd = NSA_HEAD_DIM
    return {
        "x": nrm(ks[0], (BATCH, SEQ, D_MODEL)),
        "norm_w": 1.0 + 0.01 * nrm(ks[1], (DEPTH, D_MODEL)),
        "nsa_w_in": w(ks[2], (N_NSA_LAYERS, D_MODEL, NSA_IN), D_MODEL),
        "nsa_pe_k": 0.02 * nrm(ks[3], (N_NSA_LAYERS, CMP_BLOCK, hd)),
        "nsa_pe_v": 0.02 * nrm(ks[4], (N_NSA_LAYERS, CMP_BLOCK, hd)),
        "nsa_wk1": w(ks[5], (N_NSA_LAYERS, CMP_BLOCK * hd, CMP_HIDDEN), CMP_BLOCK * hd),
        "nsa_wk2": w(ks[6], (N_NSA_LAYERS, CMP_HIDDEN, hd), CMP_HIDDEN),
        "nsa_wv1": w(ks[7], (N_NSA_LAYERS, CMP_BLOCK * hd, CMP_HIDDEN), CMP_BLOCK * hd),
        "nsa_wv2": w(ks[8], (N_NSA_LAYERS, CMP_HIDDEN, hd), CMP_HIDDEN),
        "nsa_w_out": w(ks[9], (N_NSA_LAYERS, NSA_Q_W, D_MODEL), NSA_Q_W),
        "hg_w_in": w(ks[10], (N_HG_LAYERS, D_MODEL, HG_IN), D_MODEL),
        "hg_lb_logits": 0.5 * nrm(ks[11], (DEPTH, HG_K_W)),
        "hg_norm": 1.0 + 0.01 * nrm(ks[12], (N_HG_LAYERS, HG_V_W)),
        "hg_w_out": w(ks[13], (N_HG_LAYERS, HG_V_W, D_MODEL), HG_V_W),
        "final_norm": 1.0 + 0.01 * nrm(ks[14], (D_MODEL,)),
    }

def reference(x, norm_w, nsa_w_in, nsa_pe_k, nsa_pe_v, nsa_wk1, nsa_wk2, nsa_wv1, nsa_wv2,
              nsa_w_out, hg_w_in, hg_lb_logits, hg_norm, hg_w_out, final_norm):
    p = jax.nn.softmax(hg_lb_logits.astype(jnp.float32), axis=0)
    lower_bounds = jnp.cumsum(p, axis=0) - p[0]
    for i in range(DEPTH):
        h = rms_norm(x, norm_w[i])
        j = i // N_MIXERS
        if i % N_MIXERS == 0:
            y = nsa_mixer(h, nsa_w_in[j], nsa_pe_k[j], nsa_pe_v[j], nsa_wk1[j], nsa_wk2[j],
                          nsa_wv1[j], nsa_wv2[j], nsa_w_out[j])
        else:
            y = hgrn2_mixer(h, hg_w_in[j], lower_bounds[i], hg_norm[j], hg_w_out[j])
        x = x + y.astype(x.dtype)
    return rms_norm(x, final_norm)


_drawn_inputs = setup_inputs


def setup_inputs(seed=0):
    import zlib

    import numpy as np

    out = dict(_drawn_inputs(seed))
    spreads = {}
    factors = {'norm_w': 6.819,
     'nsa_pe_k': 8.0,
     'nsa_pe_v': 32.893,
     'hg_norm': 60.462,
     'final_norm': 33.144}
    for name, (base, spread) in spreads.items():
        noise = np.random.default_rng([zlib.crc32(name.encode()), seed]).standard_normal(out[name].shape)
        drawn = base * np.exp(spread * noise) if base else spread * noise
        out[name] = __import__('jax').numpy.asarray(drawn.astype(out[name].dtype))
    for name, factor in factors.items():
        out[name] = (out[name] * factor).astype(out[name].dtype)
    return out
```

```python
from contextlib import ExitStack

import numpy as np

import concourse.bass as bass
from concourse import mybir

P = 128
D = 1024
S = 256
KT = D // P
TT = S // P
UW = 512
H, G, R, HD = 16, 4, 4, 64
CB, CS, NC, NP_ = 32, 16, 15, 32
CH = 256
HH = 8
EPS = 1e-6
NEG = -1e30
NQ = 4
LEVELS = [1, 2, 4, 8, 16, 32, 64]

F32 = mybir.dt.float32
FR = mybir.dt.float32r
BF16 = mybir.dt.bfloat16
U8 = mybir.dt.uint8
ALU = mybir.AluOpType
ACT = mybir.ActivationFunctionType
AX = mybir.AxisListType

NSA_Q, NSA_KC, NSA_KS, NSA_KW, NSA_GL, NSA_Z = 0, 1024, 1536, 2048, 2560, 2608
UNITS = [("nsa", NSA_KS), ("nsa", NSA_KW), ("nsa", NSA_KC), ("nsa", NSA_Q), ("nsa", NSA_Q + UW),
         ("nsa", NSA_Z), ("nsa", NSA_Z + UW), ("nsa_out", 0), ("nsa_out", UW),
         ("hg", 2048), ("hg", 2560), ("hg", 1024), ("hg", 0), ("hg", 1536), ("hg", 512),
         ("hg", 3072), ("hg", 3584), ("hg_out", 0), ("hg_out", UW)]
U_KS, U_KW, U_KC, U_Q0, U_Q1, U_Z0, U_Z1, U_O0, U_O1 = range(9)
V_V0, V_V1, V_F0, V_Q0, V_F1, V_Q1, V_Z0, V_Z1, V_O0, V_O1 = range(9, 19)
RAW = [0, 1, 2, 3, "k", 4, "v"] + list(range(5, len(UNITS)))
NRAW = 2
RAW_AT = {item: n for n, item in enumerate(RAW)}

ITEMS = [(0, gp, 2 * gp + g2, rp, None) for gp in range(2) for g2 in range(2) for rp in range(2)]
ITEMS += [(1, gp, 2 * gp + g2, rp, b) for gp in range(2) for g2 in range(2) for rp in range(2)
          for b in range(2)]
NI = len(ITEMS)
JOBS = [(i, gp) for i in range(2) for gp in range(2)]
ITEM_JOB = [JOBS.index((it[0], it[1])) for it in ITEMS]
JOB_LAST = [max(n for n in range(NI) if ITEM_JOB[n] == j) for j in range(4)]
JOB_FIRST = [min(n for n in range(NI) if ITEM_JOB[n] == j) for j in range(4)]
STEPS_L = ["diag"] + LEVELS


def schedule():
    out = []

    def add(*step, banks=()):
        out.append((step, tuple(banks)))

    def pa(u, t, bank, slices=range(4)):
        for sl in slices:
            add("pa", u, t, sl, banks=(bank,))

    def pb(u, m2, bank, slices=range(4)):
        for sl in slices:
            add("pb", u, m2, sl, banks=(bank,))

    def stage(j):
        for half in range(2):
            add("stage", j, half, banks=(4 + half,))

    for t in range(TT):
        add("hT", 0, t, 0, banks=(4 + 2 * t,))
        add("hT", 0, t, 1, banks=(5 + 2 * t,))
        pa(U_KS, t, 2 * t)
        if t == 1:
            stage(0)
        pa(U_KW, t, 2 * t + 1)
    stage(1)
    pb(U_KC, 0, 0)
    pb(U_KC, 1, 1)
    pa(U_Q0, 0, 2)
    stage(2)
    pa(U_Q0, 1, 3)
    stage(3)
    add("cmp1", 0, banks=(6,))
    add("gl", banks=(7,))
    add("cmpT", 0, banks=(6,))
    pa(U_Q1, 0, 0)
    add("glT", banks=(7,))
    add("cmp2", 0, banks=(6,))
    stage(4)
    pa(U_Q1, 1, 1)
    add("kcT", banks=(7,))
    stage(5)
    add("cmp1", 1, banks=(6,))
    stage(6)
    add("cmpT", 1, banks=(6,))
    z = [(u, m2, sl) for u in (U_Z0, U_Z1) for m2 in range(2) for sl in range(4)]
    fill = [(("pb",) + s, 2 + s[1]) for s in z]
    fill += [(("pa", u, 0, sl), 2 + (u - U_O0)) for u in (U_O0, U_O1) for sl in range(4)]

    def filler(n):
        for _ in range(n):
            if fill:
                step, bank = fill.pop(0)
                add(*step, banks=(bank,))

    filler(1)
    stage(7)
    add("cmp2", 1, banks=(6,))
    for i in range(2):
        add("sc", i, banks=(7,))
        filler(1)
        add("scT", i, banks=(7,))
        filler(1)
    for i in range(2):
        add("s", i, banks=(4 + i,))
    for i in range(2):
        add("pcT", i, banks=(7,))
        filler(1)
    for n in range(NI):
        add("pt", n, banks=(6 + (n + 1) % 2,))
        if n + 2 < NI:
            add("s", n + 2, banks=(4 + n % 2,))
        if n >= 1:
            add("pv", n - 1, banks=(ITEM_JOB[n - 1] % 2,))
        if n % 8 != 7:
            filler(1)
    add("pv", NI - 1, banks=(ITEM_JOB[NI - 1] % 2,))
    filler(len(fill))
    pa(U_O0, 1, 4)
    pa(U_O1, 1, 5)
    add("hT", 1, 0, 0, banks=(0,))
    add("hT", 1, 0, 1, banks=(1,))
    pa(V_V0, 0, 2)
    pa(V_V1, 0, 3)
    add("hT", 1, 1, 0, banks=(6,))
    add("hT", 1, 1, 1, banks=(7,))
    pa(V_V0, 1, 0)
    pa(V_V1, 1, 1)
    for hh, (uf, uq) in enumerate(((V_F0, V_Q0), (V_F1, V_Q1))):
        pb(uf, 0, 2)
        pb(uf, 1, 3)
        pb(uq, 0, 0)
        pb(uq, 1, 1)
    zs = [(("pa", u, t, sl), 2 * (u - V_Z0) + t) for u in (V_Z0, V_Z1) for t in range(2) for sl in range(4)]
    for lv in range(len(STEPS_L)):
        for hh in range(2):
            for c in range(TT):
                add("lev", lv, hh, c, banks=(4 + 2 * hh + c,))
            for _ in range(1):
                if zs:
                    step, bank = zs.pop(0)
                    add(*step, banks=(bank,))
    for hh in range(2):
        add("cross", hh, banks=(4 + 2 * hh,))
    for c in range(TT):
        for hh in range(2):
            add("o", c, hh, banks=((0, 1, 2, 3)[2 * c + hh],))
    for c in range(TT):
        add("yT", c, 0, banks=(4 + 2 * c,))
        add("yT", c, 1, banks=(5 + 2 * c,))
        pa(V_O0, c, 2 * c)
        pa(V_O1, c, 2 * c + 1)
    return out


def bank_key(step):
    if step[0] in ("pa", "pb"):
        return step[:3]
    if step[0] == "pv":
        return ("pv", ITEM_JOB[step[1]])
    return step


SCHEDULE = schedule()


def bank_uses():
    uses, filled, last = {}, [0] * 8, {}
    open_ = {}
    for n, (step, banks) in enumerate(SCHEDULE):
        for b in banks:
            key = bank_key(step)
            if key not in uses:
                uses[key] = (b, filled[b])
                filled[b] += 1
            assert uses[key][0] == b and (b not in open_ or open_[b] == key or filled[b] == uses[key][1] + 1), step
            assert filled[b] == uses[key][1] + 1, step
            open_[b] = key
            last[key] = n
    return uses, last


USES, LAST = bank_uses()
UNIT_LAST = {}
for _n, (_step, _) in enumerate(SCHEDULE):
    if _step[0] in ("pa", "pb"):
        UNIT_LAST[_step[1]] = _n


def program(nc, t_in, out):
    with ExitStack() as ctx:
        def sb(name, shape, dt=F32, scope=ctx):
            return scope.enter_context(nc.sbuf_tensor(name, shape, dt))

        raw = sb("raw", [P, NRAW, KT, UW])
        w_hi = sb("w_hi", [P, 2, KT, UW], FR)
        w_lo = sb("w_lo", [P, 2, KT, UW], FR)
        x = sb("x_res", [P, TT, D])
        h_hi = sb("h_hi", [P, KT, S], FR)
        h_lo = sb("h_lo", [P, KT, S], FR)
        g_row = sb("g_row", [P, D])
        ident = sb("ident", [P, P])
        ident_r = sb("ident_r", [P, P], FR)
        ident_b = sb("ident_b", [P, P], BF16)
        tri_b = sb("tri_b", [P, P], BF16)
        rope = sb("rope", [P, 4, TT, HD])
        rope_c = sb("rope_c", [P, 2, HD])
        c_mask = sb("c_mask", [P, TT, NP_])
        c_valid = sb("c_valid", [P, TT])
        l_mask = sb("l_mask", [P, len(LEVELS), P], U8)
        pe_t = sb("pe_t", [P, 2, CS])
        w2 = sb("w2", [P, 2, 2, HD])
        lbl = sb("lbl", [P, 2, HH])
        lb = sb("lb", [P, 6, HH])
        stat = sb("stat", [P, 3, 3, TT])
        eps_t = sb("eps_t", [P, 1])
        nmax = sb("nmax", [P, NI, 4])
        rsum = sb("rsum", [P, NI, 4])
        rrec = sb("rrec", [P, NI, 4])
        scl = sb("scl", [P, NI, 4])
        gate = sb("gate", [P, TT, 48])
        ostat = sb("ostat", [P, 4, 4, 4])

        nsa = ExitStack()
        q2 = sb("q2", [P, H, S], FR, nsa)
        k2 = sb("k2", [P, 2, 2, G, S], FR, nsa)
        v_tok = sb("v_tok", [P, TT, 2, G, HD], F32, nsa)
        l_land = v_tok[:].rearrange("p t b g d -> p (t b g d)")[:, 0:len(LEVELS) * P]
        kc_pad = sb("kc_pad", [P, 2, G, P], FR, nsa)
        vc_bd = sb("vc_bd", [P, 2, P], F32, nsa)
        zT = sb("zT", [P, KT, S], F32, nsa)
        xn = zT[:].rearrange("p k s -> p (k s)").rearrange("p (t d) -> p t d", t=TT)
        flat = zT[:].rearrange("p k s -> p (k s)").rearrange("p (v j g n) -> p v j g n", v=2, j=CS, g=G)
        pre = ExitStack()
        stg = sb("stg", [P, 2, 8, P], FR, pre)
        rp = sb("rp", [P, 3, UW], F32, pre)
        hid = sb("hid", [G * CS, CH], F32, pre)
        hidT = sb("hidT", [P, 2, 2, P], F32, pre)
        kcr = sb("kcr", [P, 3, HD], F32, pre)
        tri = kcr[:, 0:2].rearrange("p a d -> p (a d)")
        kcs = sb("kcs", [P, 2, P], FR, pre)
        wg = sb("wg", [P, KT, 48], F32, pre)
        wg_hi = sb("wg_hi", [P, KT, 48], FR, pre)
        wg_lo = sb("wg_lo", [P, KT, 48], FR, pre)
        gT = sb("gT", [48, S], F32, pre)
        pre.close()
        att = ExitStack()
        prob = sb("prob", [P, 2, 512], F32, att)
        prob_s = sb("prob_s", [P, 2, 512], F32, att)
        prob_t = sb("prob_t", [P, 2, 512], F32, att)
        oT = sb("oT", [P, KT, S], F32, att)
        p_ct = sb("p_ct", [P, 2, 512], F32, att)
        cst = sb("cst", [P, 2, 3, 16], F32, att)
        att.close()
        s_ct = oT[:].rearrange("p k s -> p (k s)")[:, 0:512]
        s_c = oT[:].rearrange("p k s -> p (k s)")[:, 512:1536].rearrange("p (i c) -> p i c", i=TT)
        nsa.close()

        hg = ExitStack()
        qa = sb("qa", [P, HH, S], F32, hg)
        kb = sb("kb", [P, HH, S], F32, hg)
        fg = sb("fg", [P, HH, S], F32, hg)
        ft = sb("ft", [P, HH, S], F32, hg)
        attn = sb("attn", [P, TT, HH, P], F32, hg)
        attx = sb("attx", [P, HH, P], F32, hg)
        v_hg = sb("v_hg", [P, TT, D], F32, hg)
        z_hg = sb("z_hg", [P, TT, D], F32, hg)
        y_hg = sb("y_hg", [P, TT, D], F32, hg)
        junk = sb("junk", [P, D], BF16, hg)
        hg.close()

        bank = [ctx.enter_context(nc.psum_tensor(f"bank{b}", [P, 512], F32)) for b in range(8)]

        def sem(name):
            return ctx.enter_context(nc.semaphore(name))

        raw_in = [sem(f"raw_in{i}") for i in range(NRAW)]
        x_in = [sem(f"x_in{t}") for t in range(TT)]
        const_in = sem("const_in")
        wg_in = sem("wg_in")
        g_in = [sem(f"g_in{i}") for i in range(4)]
        hi_done = sem("hi_done")
        lo_done = sem("lo_done")
        ident_in = sem("ident_in")
        pv_done = sem("pv_done")
        vec_step = sem("vec_step")
        act_step = sem("act_step")
        pool_step = sem("pool_step")
        filled = [sem(f"filled{b}") for b in range(8)]
        drained = [sem(f"drained{b}") for b in range(8)]
        taken_hi = sem("taken_hi")
        idents = sem("idents")
        eps_set = sem("eps_set")
        sumsq = sem("sumsq")
        root = sem("root")
        rstd = sem("rstd")
        normed = sem("normed")
        r_ab = sem("r_ab")
        r_sum = sem("r_sum")
        r_hi = sem("r_hi")
        r_lo = sem("r_lo")
        flat_zero = sem("flat_zero")
        hid_done = sem("hid_done")
        kc_v = sem("kc_v")
        zeros = sem("zeros")
        wg_hi_d = sem("wg_hi_d")
        wg_lo_d = sem("wg_lo_d")
        gate_v = sem("gate_v")
        cmp_v = sem("cmp_v")
        cmp_exp = sem("cmp_exp")
        cmp_scaled = sem("cmp_scaled")
        rowmax = sem("rowmax")
        expd = sem("expd")
        recip_d = sem("recip_d")
        scale_d = sem("scale_d")
        scaled = sem("scaled")
        z_silu = sem("z_silu")
        y_mul = sem("y_mul")
        y_hi = sem("y_hi")
        y_lo = sem("y_lo")
        lb_v = sem("lb_v")
        lb_e = sem("lb_e")
        f_lin = sem("f_lin")
        k_lin = sem("k_lin")
        q_f = sem("q_f")
        qa_up = sem("qa_up")
        kb_up = sem("kb_up")
        ft_up = sem("ft_up")
        z_g = sem("z_g")
        o_sq = sem("o_sq")
        o_sum = sem("o_sum")
        o_root = sem("o_root")
        o_rstd = sem("o_rstd")
        o_norm = sem("o_norm")
        done_row = sem("done_row")
        out_done = sem("out_done")

        def wait_full(eng, key):
            b, k = USES[key]
            eng.wait_ge(filled[b], k + 1)

        def wait_taken(eng, key):
            b, k = USES[key]
            eng.wait_ge(drained[b], k + 1)

        def full(key):
            return filled[USES[key][0]]

        def taken(key):
            return drained[USES[key][0]]

        def bk(key):
            return bank[USES[key][0]]

        def wait_residual(eng, u, t):
            wait_taken(eng, ("pa", u, t))
            wait_taken(eng, ("pa", u + 1, t))

        def wait_unit_used(eng, u):
            wait_full(eng, bank_key(SCHEDULE[UNIT_LAST[u]][0]))

        def wait_pv(eng, it):
            if it == JOB_LAST[ITEM_JOB[it]]:
                wait_full(eng, ("pv", ITEM_JOB[it]))
            else:
                eng.wait_ge(pv_done, it + 1 - sum(j < it for j in JOB_LAST))

        def bc(ap, n, at):
            shape = list(ap.shape)
            return ap.unsqueeze(at).broadcast_to(shape[:at] + [n] + shape[at:])


        def level_totals(s, hh):
            hs = slice(4 * hh, 4 * hh + 4)
            if s == 1:
                return fg[:, hs]
            at = S - 2 * S // s
            return ft[:, hs, at:at + S // s]

        def totals(s, hh):
            return level_totals(s, hh).rearrange("p h (b u) -> p h b u", u=2)

        def scale_item(pool, it):
            pool.wait_ge(scale_d, it + 1)
            if it >= 2:
                wait_full(pool, ("pt", it - 2))
            nb = 4 if ITEMS[it][0] == 0 else 2
            v = lambda ap: ap.rearrange("p (a b) -> p a b", a=nb)
            nc.gpsimd.tensor_tensor(v(prob_s[:, it % 2]), v(prob[:, it % 2]), bc(scl[:, it, 0:nb], 512 // nb, 2),
                                    ALU.mult).then_inc(scaled, 1)

        def split_parts(u, q):
            if u not in (U_Z0, U_Z1):
                sl = slice(2 * q, 2 * q + 2)
                return [(w_hi[:, u % 2, sl], raw[:, RAW_AT[u] % NRAW, sl], w_lo[:, u % 2, sl])]
            tile = lambda w, kk: w[:, u % 2, kk].rearrange("p (r g d) -> p r g d", r=R, d=HD)
            return [(tile(w_hi, kk), raw[:, RAW_AT[u] % NRAW, kk].rearrange("p (g r d) -> p r g d", r=R, d=HD), tile(w_lo, kk))
                    for kk in (2 * q, 2 * q + 1)]

        CONST_LOADS = [(rope[:], t_in["c_rope"]), (rope_c[:], t_in["c_rope_c"]), (c_mask[:], t_in["c_mask"]),
                       (c_valid[:], t_in["c_valid"]), (tri, t_in["c_tri"]), (l_land, t_in["c_levels"].rearrange("p l q -> p (l q)")),
                       (pe_t[:], t_in["pe"]), (lbl[:], t_in["lb"]),
                       (w2[:, 0], t_in["w2k"].rearrange("(c p) d -> p c d", p=P)),
                       (w2[:, 1], t_in["w2v"].rearrange("(c p) d -> p c d", p=P))]
        N_CONST = len(CONST_LOADS)

        STAGE = [(U_KS, 0), (U_KW, 0), (U_KS, 1), (U_KW, 1), (U_Q0, 0), (U_Q0, 1), (U_Q1, 0), (U_Q1, 1)]
        block = ctx.enter_context(nc.Block())

        @block.sync
        def _(sp):
            for n, item in enumerate(RAW):
                if n >= NRAW:
                    old = RAW[n - NRAW]
                    if old == "k" or old == "v":
                        wait_full(sp, ("cmp1", "kv".index(old)))
                    else:
                        sp.wait_ge(lo_done, NQ * (old + 1))
                dst = raw[:, n % NRAW]
                if item in ("k", "v"):
                    w1 = t_in["w1" + item].rearrange("(a j d) h -> a d j h", a=2, d=HD)
                    for a in range(2):
                        sp.dma_start(dst[a * HD:(a + 1) * HD].rearrange("p k n -> p (k n)").rearrange(
                            "p (j h) -> p j h", h=CH), w1[a]).then_inc(raw_in[n % NRAW], 16)
                    continue
                kind, col = UNITS[item]
                w = t_in[kind][:, col:col + UW]
                if kind == "nsa_out":
                    w = w.rearrange("(gp g2 r d) n -> g2 d gp r n", gp=2, g2=2, r=R)
                    for g2 in range(2):
                        for gp in range(2):
                            sp.dma_start(dst[g2 * HD:(g2 + 1) * HD, gp * R:(gp + 1) * R], w[g2][:, gp]).then_inc(raw_in[n % NRAW], 16)
                else:
                    w = w.rearrange("(k p) n -> p k n", p=P)
                    for half in range(2):
                        sp.dma_start(dst[:, 4 * half:4 * half + 4], w[:, 4 * half:4 * half + 4]).then_inc(raw_in[n % NRAW], 16)
            for t in range(TT):
                sp.wait_ge(done_row, t + 1)
                sp.dma_start(out[t * P:(t + 1) * P, :], y_hg[:, t]).then_inc(out_done, 16)
            sp.wait_ge(out_done, 16 * TT)

        def raw_count(item):
            n = RAW_AT[item]
            c = 0
            for m in range(n % NRAW, n + 1, NRAW):
                it = RAW[m]
                c += 4 if it not in ("k", "v") and UNITS[it][0] == "nsa_out" else 2
            return 16 * c

        @block.tensor
        def _(pe):
            def mm(o, lhsT, rhs, start, stop):
                return nc.tensor.matmul(o, lhsT, rhs, start=start, stop=stop, skip_group_check=True)

            def parts(u, sl_first, kk):
                pe.wait_ge(lo_done, NQ * u + kk // 2 + 1)

            def act_ready(L, t, u):
                if u in (U_O0, U_O1):
                    pe.wait_ge(y_lo, 2 * t + 2)
                elif u in (V_O0, V_O1):
                    for q in range(2):
                        wait_taken(pe, ("yT", t, q))
                else:
                    for q in range(2):
                        wait_taken(pe, ("hT", L, t, q))

            for n, (step, banks) in enumerate(SCHEDULE):
                kind = step[0]
                key = bank_key(step)
                b, k = USES[key]
                ps = bank[b]
                first = not any(bank_key(s) == key for s, _ in SCHEDULE[:n])
                last_of_bank = LAST[key] == n
                if first and k > 0:
                    pe.wait_ge(drained[b], k)
                if kind == "hT":
                    _, L, t, q = step
                    pe.wait_ge(normed, TT * L + t + 1)
                    if n == 0:
                        pe.wait_ge(ident_in, 16)
                    src = xn if L == 0 else y_hg
                    for j in range(4):
                        c = (4 * q + j) * P
                        m = nc.tensor.transpose(ps[:, j * P:(j + 1) * P], src[:, t, c:c + P], ident[:])
                elif kind == "pa":
                    _, u, t, sl = step
                    if sl == 0:
                        act_ready(0 if u <= U_O1 else 1, t, u)
                    for kk in (2 * sl, 2 * sl + 1):
                        parts(u, sl, kk)
                        hi = h_hi[:, kk, t * P:(t + 1) * P]
                        mm(ps[:], hi, w_hi[:, u % 2, kk], kk == 0, False)
                        mm(ps[:], hi, w_lo[:, u % 2, kk], False, False)
                        m = mm(ps[:], h_lo[:, kk, t * P:(t + 1) * P], w_hi[:, u % 2, kk], False, kk == KT - 1)
                elif kind == "pb":
                    _, u, m2, sl = step
                    if m2 == 0 and sl == 0:
                        for t in range(TT):
                            act_ready(0 if u <= U_O1 else 1, t, u)
                    j = 2 * m2 + sl // 2
                    for kk in range(4 * (sl % 2), 4 * (sl % 2) + 4):
                        parts(u, sl, kk)
                        o = ps[:, (j % 2) * S:(j % 2 + 1) * S]
                        cols = lambda w: w[:, u % 2, kk, j * P:(j + 1) * P]
                        mm(o, cols(w_hi), h_hi[:, kk], kk == 0, False)
                        mm(o, cols(w_hi), h_lo[:, kk], False, False)
                        m = mm(o, cols(w_lo), h_hi[:, kk], False, kk == KT - 1)
                elif kind == "stage":
                    _, j, half = step
                    pe.wait_ge(r_lo, j + 1)
                    if j == 0 and half == 0:
                        pe.wait_ge(idents, 1)
                    for c in range(4):
                        m = nc.tensor.transpose(ps[:, c * P:(c + 1) * P].bitcast(FR), stg[:, j % 2, 4 * half + c], ident_r[:])
                elif kind == "cmp1":
                    kv = step[1]
                    wait_taken(pe, ("pb", U_KC, kv))
                    pe.wait_ge(flat_zero, 1)
                    item = "kv"[kv]
                    pe.wait_ge(raw_in[RAW_AT[item] % NRAW], raw_count(item))
                    w1 = raw[:, RAW_AT[item] % NRAW].rearrange("p k n -> p (k n)").rearrange("p (j h) -> p j h", h=CH)
                    for j in range(CS):
                        m = mm(ps[0:G * CS, 0:CH], flat[:, kv, j].rearrange("p g n -> p (g n)"), w1[:, j], j == 0, j == CS - 1)
                elif kind == "cmpT":
                    kv = step[1]
                    wait_taken(pe, ("cmp1", kv))
                    for c in range(2):
                        m = nc.tensor.transpose(ps[:, c * HD:(c + 1) * HD], hid[:, c * P:(c + 1) * P], ident[0:HD, 0:HD])
                elif kind == "cmp2":
                    kv = step[1]
                    if kv == 0:
                        pe.wait_ge(const_in, 16 * N_CONST)
                    wait_taken(pe, ("cmpT", kv))
                    for c in range(2):
                        m = mm(ps[:, 0:HD], hidT[:, kv, c], w2[:, kv, c], c == 0, c == 1)
                elif kind == "kcT":
                    pe.wait_ge(kc_v, 1)
                    for c in range(2):
                        m = nc.tensor.transpose(ps[:, c * P:(c + 1) * P].bitcast(FR), kcs[:, c], ident_r[:])
                elif kind == "gl":
                    pe.wait_ge(wg_lo_d, 1)
                    for kk in range(KT):
                        mm(ps[0:48, 0:S], wg_hi[:, kk], h_hi[:, kk], kk == 0, False)
                        mm(ps[0:48, 0:S], wg_hi[:, kk], h_lo[:, kk], False, False)
                        m = mm(ps[0:48, 0:S], wg_lo[:, kk], h_hi[:, kk], False, kk == KT - 1)
                elif kind == "glT":
                    wait_taken(pe, ("gl",))
                    for t in range(TT):
                        m = nc.tensor.transpose(ps[:, t * 48:(t + 1) * 48], gT[:, t * P:(t + 1) * P], ident[0:48, 0:48])
                elif kind == "sc":
                    i = step[1]
                    wait_taken(pe, ("kcT",))
                    for j in range(4 + i, 8, 2):
                        for half in range(2):
                            wait_taken(pe, ("stage", j, half))
                    for g in range(G):
                        for part in range(2):
                            m = mm(ps[:], kc_pad[:, part, g], q2[:, g * R:(g + 1) * R, i * P:(i + 1) * P],
                                   g == 0 and part == 0, g == G - 1 and part == 1)
                elif kind == "scT":
                    i = step[1]
                    wait_taken(pe, ("sc", i))
                    for r in range(R):
                        m = nc.tensor.transpose(ps[:, r * P:(r + 1) * P], s_ct[:, r * P:(r + 1) * P], ident[:])
                elif kind == "pcT":
                    i = step[1]
                    pe.wait_ge(cmp_scaled, i + 1)
                    for r in range(R):
                        m = nc.tensor.transpose(ps[:, r * P:(r + 1) * P], s_c[:, i, r * P:(r + 1) * P], ident[:])
                elif kind == "s":
                    i, gp, g, rp_, br = ITEMS[step[1]]
                    if step[1] == 0:
                        for j in range(8):
                            for half in range(2):
                                wait_taken(pe, ("stage", j, half))
                        pe.wait_ge(idents, 3)
                    for r2 in range(2):
                        h = g * R + 2 * rp_ + r2
                        for part in range(2):
                            keys = k2[:, part, :, g, 0:P] if i == 0 else k2[:, part, br, g]
                            mm(ps[:, r2 * S:(r2 + 1) * S], q2[:, h, i * P:(i + 1) * P], keys, r2 == 0 and part == 0, False)
                    if i == 0:
                        m = mm(ps[:], ident_b[:], bc(tri_b[:], 4, 1), False, True)
                    else:
                        m = mm(ps[:].rearrange("p (r k q) -> p r k q", r=2, k=2)[:, :, 1], ident_b[:], bc(tri_b[:], 2, 1), False, True)
                elif kind == "pt":
                    it = step[1]
                    pe.wait_ge(scaled, it + 1)
                    for c in range(4):
                        m = nc.tensor.transpose(ps[:, c * P:(c + 1) * P], prob_s[:, it % 2, c * P:(c + 1) * P], ident[:])
                elif kind == "pv":
                    it = step[1]
                    i, gp, g, rp_, br = ITEMS[it]
                    if first:
                        wait_taken(pe, ("cmp2", 1))
                        wait_taken(pe, ("pcT", i))
                        mm(ps[:], vc_bd[:, gp], p_ct[:, i], True, False)
                    wait_taken(pe, ("pt", it))
                    for c in range(4):
                        r2, c2 = c // 2, c % 2
                        vb, kt = (c2, 0) if i == 0 else (br, c2)
                        r = 2 * rp_ + r2
                        o = ps[(g % 2) * HD:(g % 2 + 1) * HD, r * P:(r + 1) * P]
                        m = mm(o, v_tok[:, kt, vb, g], prob_t[:, it % 2, c * P:(c + 1) * P], False, last_of_bank)
                elif kind == "lev":
                    _, lv, hh, c = step
                    if lv == 0:
                        for m2 in range(2):
                            wait_taken(pe, ("pb", (V_Q0, V_Q1)[hh], m2))
                        pe.wait_ge(k_lin, hh + 1)
                    elif lv == 1:
                        pe.wait_ge(q_f, hh + 1)
                    else:
                        pe.wait_ge(qa_up, 2 * (lv - 2) + hh + 1)
                        pe.wait_ge(kb_up, 2 * (lv - 2) + hh + 1)
                    for j in range(4):
                        h = 4 * hh + j
                        m = mm(ps[:, j * P:(j + 1) * P], kb[:, h, c * P:(c + 1) * P], qa[:, h, c * P:(c + 1) * P], j == 0, j == 3)
                elif kind == "cross":
                    hh = step[1]
                    lv = len(STEPS_L)
                    pe.wait_ge(qa_up, 2 * (lv - 2) + hh + 1)
                    pe.wait_ge(kb_up, 2 * (lv - 2) + hh + 1)
                    for j in range(4):
                        h = 4 * hh + j
                        m = mm(ps[:, j * P:(j + 1) * P], kb[:, h, 0:P], qa[:, h, P:2 * P], j == 0, j == 3)
                elif kind == "o":
                    _, c, hh = step
                    wait_taken(pe, ("lev", len(STEPS_L) - 1, hh, c))
                    if c == 1:
                        wait_taken(pe, ("cross", hh))
                    for j in range(4):
                        h = 4 * hh + j
                        o = ps[:, j * P:(j + 1) * P]
                        m = mm(o, attn[:, c, h], v_hg[:, c, h * P:(h + 1) * P], j == 0, c == 0 and j == 3)
                        if c == 1:
                            m = mm(o, attx[:, h], v_hg[:, 0, h * P:(h + 1) * P], False, j == 3)
                elif kind == "yT":
                    _, c, q = step
                    pe.wait_ge(o_norm, 2 * c + q + 1)
                    for j in range(4):
                        col = (4 * q + j) * P
                        m = nc.tensor.transpose(ps[:, j * P:(j + 1) * P], y_hg[:, c, col:col + P], ident[:])
                if last_of_bank:
                    m.then_inc(filled[b], 1)
                elif kind == "pv":
                    m.then_inc(pv_done, 1)

        HI_KEYS = [step for step, _ in SCHEDULE if step[0] in ("hT", "yT")]

        def squares(act, norm, t):
            unused = stg[:, 0].rearrange("p c q -> p (c q)") if norm == 0 else junk[:]
            nc.scalar.activation(unused, x[:, t], ACT.Square, accum_out=stat[:, norm, 0, t:t + 1]).then_inc(sumsq, 1)
            act.wait_ge(sumsq, TT * norm + t + 1)
            act.wait_ge(eps_set, 1)
            nc.scalar.activation(stat[:, norm, 1, t:t + 1], stat[:, norm, 0, t:t + 1], ACT.Sqrt,
                                 scale=1.0 / D, bias=eps_t[:]).then_inc(root, 1)

        @block.scalar
        def _(act):
            def split_hi(u):
                if u >= 2:
                    wait_unit_used(act, u - 2)
                act.wait_ge(raw_in[RAW_AT[u] % NRAW], raw_count(u))
                for q in range(NQ):
                    for dst, src, _ in split_parts(u, q):
                        m = nc.scalar.activation(dst, src, ACT.Copy)
                    m.then_inc(hi_done, 1)

            act.dma_start(x[:, 0], t_in["x"][0:P, :]).then_inc(x_in[0], 16)
            act.dma_start(ident[:], t_in["ident"]).then_inc(ident_in, 16)
            act.dma_start(x[:, 1], t_in["x"][P:2 * P, :]).then_inc(x_in[1], 16)
            act.dma_start(wg[:], t_in["nsa"][:, NSA_GL:NSA_Z].rearrange("(k p) n -> p k n", p=P)).then_inc(wg_in, 16)
            for dst, src in CONST_LOADS:
                act.dma_start(dst, src).then_inc(const_in, 16)
            act.wait_ge(ident_in, 16)
            nc.scalar.activation(ident_r[:], ident[:], ACT.Copy).then_inc(idents, 1)
            nc.scalar.activation(ident_b[:], ident[:], ACT.Copy).then_inc(idents, 1)
            for t in range(TT):
                act.wait_ge(x_in[t], 16)
                if t:
                    act.wait_ge(root, t)
                squares(act, 0, t)
            split_hi(0)
            split_hi(1)
            act.wait_ge(const_in, 16 * N_CONST)
            nc.scalar.activation(tri_b[:], tri, ACT.Copy).then_inc(idents, 1)
            nc.scalar.activation(l_mask[:].rearrange("p l q -> p (l q)"), l_land, ACT.Copy).then_inc(idents, 1)
            act.wait_ge(wg_in, 16)
            nc.scalar.activation(wg_hi[:], wg[:], ACT.Copy).then_inc(wg_hi_d, 1)

            for n, (step, _) in enumerate(SCHEDULE):
                kind, key = step[0], bank_key(step)
                if LAST[key] == n:
                    ps = bk(key)
                    if kind == "hT" or kind == "yT":
                        t, q = (step[2], step[3]) if kind == "hT" else (step[1], step[2])
                        wait_full(act, key)
                        nc.scalar.activation(h_hi[:, 4 * q:4 * q + 4, t * P:(t + 1) * P],
                                             ps[:].rearrange("p (k s) -> p k s", k=4), ACT.Copy).then_inc(taken_hi, 1)
                    elif kind == "pa" and step[1] in (U_KS, U_KW, U_Q0, U_Q1):
                        j = STAGE.index(step[1:3])
                        if j >= 2:
                            wait_full(act, ("stage", j - 2, 1))
                        act.wait_ge(r_sum, j + 1)
                        if step[1] in (U_KS, U_KW):
                            nc.scalar.activation(stg[:, j % 2, 0:4].rearrange("p g (u d) -> p g u d", u=2),
                                                 bc(rp[:, 2, 0:G * HD].rearrange("p (g d) -> p g d", d=HD), 2, 2), ACT.Copy).then_inc(r_hi, 1)
                        else:
                            nc.scalar.activation(stg[:, j % 2, :, 0:HD], rp[:, 2].rearrange("p (h d) -> p h d", d=HD), ACT.Copy).then_inc(r_hi, 1)
                    elif kind == "stage":
                        _, j, half = step
                        u, t = STAGE[j]
                        wait_full(act, key)
                        if u in (U_KS, U_KW):
                            dst = k2[:, half, (U_KS, U_KW).index(u), :, t * P:(t + 1) * P]
                        else:
                            h0 = 8 * (u - U_Q0) + 4 * half
                            dst = q2[:, h0:h0 + 4, t * P:(t + 1) * P]
                        nc.scalar.activation(dst, ps[:].rearrange("p (k s) -> p k s", k=4), ACT.Copy).then_inc(taken(key), 1)
                    elif kind == "cmp1":
                        if step[1]:
                            wait_full(act, ("cmpT", 0))
                        wait_full(act, key)
                        nc.scalar.activation(hid[:], ps[0:G * CS, 0:CH], ACT.Silu).then_inc(taken(key), 1)
                    elif kind == "cmpT":
                        act.wait_ge(zeros, 3)
                        wait_full(act, key)
                        nc.scalar.activation(hidT[:, step[1]].rearrange("p c (g n) -> p (c g) n", g=G)[:, :, 0:CS],
                                             ps[:, 0:2 * HD].rearrange("p (c n) -> p c n", n=CS), ACT.Copy).then_inc(taken(key), 1)
                    elif kind == "gl":
                        wait_full(act, key)
                        nc.scalar.activation(gT[:], ps[0:48, 0:S], ACT.Sigmoid).then_inc(taken(key), 1)
                    elif kind == "glT":
                        wait_full(act, key)
                        nc.scalar.activation(gate[:], ps[:, 0:TT * 48].rearrange("p (t c) -> p t c", t=TT), ACT.Copy).then_inc(taken(key), 1)
                    elif kind == "kcT":
                        act.wait_ge(zeros, 3)
                        wait_full(act, key)
                        for part in range(2):
                            for g in range(G):
                                m = nc.scalar.activation(kc_pad[:, part, g, g * NP_:(g + 1) * NP_],
                                                         ps[:, part * P + g * NP_:part * P + (g + 1) * NP_], ACT.Copy)
                                if part == 1 and g == G - 1:
                                    m.then_inc(taken(key), 1)
                    elif kind == "sc":
                        wait_full(act, key)
                        nc.scalar.activation(s_ct, ps[:], ACT.Copy).then_inc(taken(key), 1)
                        if step[1] == 0:
                            act.wait_ge(lb_v, 1)
                            nc.scalar.activation(lb[:, 1:3], lb[:, 1:3], ACT.Exp).then_inc(lb_e, 1)
                    elif kind == "scT":
                        act.wait_ge(cmp_v, step[1] + 1)
                        nc.scalar.activation(s_c[:, step[1]], s_c[:, step[1]], ACT.Exp).then_inc(cmp_exp, 1)
                    elif kind == "pcT":
                        wait_full(act, key)
                        nc.scalar.activation(p_ct[:, step[1]], ps[:], ACT.Copy).then_inc(taken(key), 1)
                    elif kind == "s":
                        it = step[1]
                        i = ITEMS[it][0]
                        if it >= 2:
                            act.wait_ge(scaled, it - 1)
                        act.wait_ge(rowmax, it + 1)
                        nb = 4 if i == 0 else 2
                        w = 512 // nb
                        for c in range(nb):
                            m = nc.scalar.activation(prob[:, it % 2, c * w:(c + 1) * w], ps[:, c * w:(c + 1) * w], ACT.Exp,
                                                     bias=nmax[:, it, c:c + 1], accum_out=rsum[:, it, c:c + 1])
                        m.then_inc(taken(key), 1)
                    elif kind == "pb" and step[1] in (U_Z0, U_Z1):
                        u, m2 = step[1], step[2]
                        if u == U_Z0 and m2 == 0:
                            wait_full(act, ("hT", 0, 1, 1))
                        wait_full(act, key)
                        r0 = 4 * (u - U_Z0) + 2 * m2
                        nc.scalar.activation(zT[:, r0:r0 + 2], ps[:].rearrange("p (k s) -> p k s", k=2), ACT.Copy).then_inc(taken(key), 1)
                        if u == U_Z1 and m2 == 1:
                            wait_taken(act, key)
                            wait_taken(act, ("pb", U_Z1, 0))
                            nc.scalar.activation(zT[:], zT[:], ACT.Silu).then_inc(z_silu, 1)
                    elif kind == "pa" and step[1] in (V_V0, V_V1):
                        u, t = step[1], step[2]
                        wait_full(act, key)
                        nc.scalar.activation(v_hg[:, t, (u - V_V0) * UW:(u - V_V0 + 1) * UW], ps[:], ACT.Copy).then_inc(taken(key), 1)
                    elif kind == "pb" and step[1] in (V_F0, V_F1, V_Q0, V_Q1):
                        u, m2 = step[1], step[2]
                        is_f = u in (V_F0, V_F1)
                        h0 = 4 * (u in (V_F1, V_Q1)) + 2 * m2
                        wait_full(act, key)
                        nc.scalar.activation((fg if is_f else qa)[:, h0:h0 + 2], ps[:].rearrange("p (k s) -> p k s", k=2),
                                             ACT.Sigmoid if is_f else ACT.Silu).then_inc(taken(key), 1)
                    elif kind == "pa" and step[1] in (V_Z0, V_Z1):
                        u, t = step[1], step[2]
                        wait_full(act, key)
                        nc.scalar.activation(z_hg[:, t, (u - V_Z0) * UW:(u - V_Z0 + 1) * UW], ps[:], ACT.Silu).then_inc(taken(key), 1)
                    elif kind == "o":
                        _, c, hh = step
                        o = 2 * c + hh
                        wait_full(act, key)
                        sq = fg[:].rearrange("p h s -> p (h s)")[:, o * 512:(o + 1) * 512]
                        nc.scalar.activation(sq, ps[:], ACT.Square).then_inc(o_sq, 1)
                        act.wait_ge(o_sum, o + 1)
                        nc.scalar.activation(ostat[:, o, 1], ostat[:, o, 0], ACT.Sqrt, scale=1.0 / P, bias=eps_t[:]).then_inc(o_root, 1)
                    elif kind == "pv" and key[1] >= 2:
                        wait_taken(act, key)
                        gp = key[1] - 2
                        nc.scalar.activation(h_hi[:, 4 * gp:4 * gp + 4, P:S], oT[:, 4 * gp:4 * gp + 4, P:S], ACT.Copy).then_inc(y_hi, 1)
                    if key == ("pb", U_Z1, 1):
                        for gp in range(2):
                            act.wait_ge(y_mul, gp + 1)
                            nc.scalar.activation(h_hi[:, 4 * gp:4 * gp + 4, 0:P], oT[:, 4 * gp:4 * gp + 4, 0:P], ACT.Copy).then_inc(y_hi, 1)
                    if key == ("pv", 3):
                        act.wait_ge(y_lo, 4)
                        wait_residual(act, U_O0, 0)
                        squares(act, 1, 0)
                    if key == ("pa", U_O1, 1):
                        act.wait_ge(root, TT + 1)
                        wait_residual(act, U_O0, 1)
                        squares(act, 1, 1)
                    if kind == "pa" and step[1] == V_O1:
                        t = step[2]
                        act.wait_ge(root, 2 * TT + t)
                        wait_residual(act, V_O0, t)
                        squares(act, 2, t)
                if kind in ("pa", "pb") and UNIT_LAST[step[1]] == n and step[1] + 2 < len(UNITS):
                    split_hi(step[1] + 2)

        @block.vector
        def _(dve):
            steps = [0]

            def step_(ins):
                ins.then_inc(vec_step, 1)
                steps[0] += 1

            def settled():
                dve.wait_ge(vec_step, steps[0])

            V = nc.vector

            def split_lo(u):
                for q in range(NQ):
                    dve.wait_ge(hi_done, NQ * u + q + 1)
                    for hi, src, lo in split_parts(u, q):
                        m = V.tensor_tensor(lo, src, hi.bitcast(F32), ALU.subtract)
                    m.then_inc(lo_done, 1)

            def norm(nrm, t, dst, g_n, sig):
                dve.wait_ge(root, TT * nrm + t + 1)
                V.reciprocal(stat[:, nrm, 2, t:t + 1], stat[:, nrm, 1, t:t + 1]).then_inc(rstd, 1)
                dve.wait_ge(rstd, TT * nrm + t + 1)
                dve.wait_ge(g_in[g_n], 16)
                V.scalar_tensor_tensor(dst, x[:, t], stat[:, nrm, 2, t:t + 1], g_row[:], ALU.mult, ALU.mult).then_inc(sig, 1)

            def item_scale(it):
                i, gp, g, rp_, br = ITEMS[it]
                nb = 4 if i == 0 else 2
                wait_taken(dve, ("s", it))
                V.reciprocal(rrec[:, it, 0:nb], rsum[:, it, 0:nb]).then_inc(recip_d, 1)
                dve.wait_ge(recip_d, it + 1)
                h0 = g * R + 2 * rp_
                gv = gate[:, i].rearrange("p (h b) -> p h b", b=3)[:, h0:h0 + 2]
                if i == 0:
                    V.tensor_tensor(scl[:, it].rearrange("p (r b) -> p r b", r=2), rrec[:, it].rearrange("p (r b) -> p r b", r=2),
                                    gv[:, :, 1:3], ALU.mult).then_inc(scale_d, 1)
                else:
                    V.tensor_tensor(scl[:, it, 0:2], rrec[:, it, 0:2], gv[:, :, 1 + br], ALU.mult).then_inc(scale_d, 1)

            V.memset(eps_t[:], EPS).then_inc(eps_set, 1)
            for t in range(TT):
                norm(0, t, xn[:, t], 0, normed)
            rope_uses = 0
            for n, (step, _) in enumerate(SCHEDULE):
                kind, key = step[0], bank_key(step)
                if LAST[key] == n:
                    ps = bk(key)
                    if kind == "hT" or kind == "yT":
                        t, q = (step[2], step[3]) if kind == "hT" else (step[1], step[2])
                        dve.wait_ge(taken_hi, HI_KEYS.index(step) + 1)
                        hs = (slice(None), slice(4 * q, 4 * q + 4), slice(t * P, (t + 1) * P))
                        V.tensor_tensor(h_lo[hs], ps[:].rearrange("p (k s) -> p k s", k=4), h_hi[hs].bitcast(F32),
                                        ALU.subtract).then_inc(taken(key), 1)
                        if step == ("hT", 0, 1, 1):
                            V.memset(flat[HD:P, :, :, :, NC:CS], 0.0).then_inc(flat_zero, 1)
                        if step == ("hT", 0, 0, 1):
                            split_lo(0)
                            split_lo(1)
                            dve.wait_ge(wg_hi_d, 1)
                            V.tensor_tensor(wg_lo[:], wg[:], wg_hi[:].bitcast(F32), ALU.subtract).then_inc(wg_lo_d, 1)
                            dve.wait_ge(const_in, 16 * N_CONST)
                            step_(V.tensor_tensor(lb[:, 0], lbl[:, 0], lbl[:, 1], ALU.max))
                            settled()
                            V.tensor_tensor(lb[:, 1:3], lbl[:], bc(lb[:, 0], 2, 1), ALU.subtract).then_inc(lb_v, 1)
                    elif kind == "pa" and step[1] in (U_KS, U_KW, U_Q0, U_Q1):
                        u, t = step[1], step[2]
                        j = STAGE.index((u, t))
                        is_k = u in (U_KS, U_KW)
                        nh = G if is_k else 8
                        if j == 0:
                            dve.wait_ge(const_in, 16 * N_CONST)
                        else:
                            dve.wait_ge(r_sum, j)
                        wait_full(dve, key)
                        xin = ps[:, 0:nh * HD].rearrange("p (h d) -> p h d", d=HD)
                        a = rp[:, 0, 0:nh * HD].rearrange("p (h d) -> p h d", d=HD)
                        b_ = rp[:, 1, 0:nh * HD].rearrange("p (h d) -> p h d", d=HD)
                        co, si = (rope[:, 2, t], rope[:, 3, t]) if is_k else (rope[:, 0, t], rope[:, 1, t])
                        hf = HD // 2
                        V.tensor_tensor(a, xin, bc(co, nh, 1), ALU.mult)
                        V.tensor_tensor(b_[:, :, 0:hf], xin[:, :, hf:HD], bc(si[:, 0:hf], nh, 1), ALU.mult)
                        if is_k:
                            V.tensor_tensor(b_[:, :, hf:HD], xin[:, :, 0:hf], bc(si[:, hf:HD], nh, 1), ALU.mult).then_inc(r_ab, 1)
                            dve.wait_ge(idents, 4)
                            V.tensor_copy(v_tok[:, t, (U_KS, U_KW).index(u)].rearrange("p g d -> p (g d)"), ps[:, G * HD:UW]).then_inc(taken(key), 1)
                        else:
                            V.tensor_tensor(b_[:, :, hf:HD], xin[:, :, 0:hf], bc(si[:, hf:HD], nh, 1), ALU.mult).then_inc(taken(key), 1)
                    elif key[0:2] == ("pb", U_KC):
                        kv = step[2]
                        wait_full(dve, key)
                        for g in range(G):
                            src = ps[(g % 2) * HD:(g % 2 + 1) * HD, (g // 2) * S:(g // 2 + 1) * S].rearrange("p (n j) -> p j n", j=CS)
                            V.tensor_tensor(flat[0:HD, kv, :, g], src, bc(pe_t[0:HD, kv], CS, 2), ALU.add)
                            m = V.tensor_tensor(flat[HD:P, kv, :, g, 0:NC], src[:, :, 1:CS], bc(pe_t[HD:P, kv], NC, 2), ALU.add)
                        m.then_inc(taken(key), 1)
                    elif kind == "cmp2" and step[1] == 0:
                        wait_full(dve, key)
                        hf = HD // 2
                        dve.wait_ge(idents, 3)
                        step_(V.tensor_tensor(kcr[:, 0], ps[:, 0:HD], rope_c[:, 0], ALU.mult))
                        step_(V.tensor_tensor(kcr[:, 1, 0:hf], ps[:, hf:HD], rope_c[:, 1, 0:hf], ALU.mult))
                        V.tensor_tensor(kcr[:, 1, hf:HD], ps[:, 0:hf], rope_c[:, 1, hf:HD], ALU.mult).then_inc(taken(key), 1)
                        wait_taken(dve, key)
                        step_(V.tensor_tensor(kcr[:, 2], kcr[:, 0], kcr[:, 1], ALU.add))
                        settled()
                        hi2 = kcs[:, 0].rearrange("p (u d) -> p u d", u=2)
                        lo2 = kcs[:, 1].rearrange("p (u d) -> p u d", u=2)
                        step_(V.tensor_copy(hi2, bc(kcr[:, 2], 2, 1)))
                        settled()
                        V.tensor_tensor(lo2, bc(kcr[:, 2], 2, 1), hi2.bitcast(F32), ALU.subtract).then_inc(kc_v, 1)
                    elif kind == "cmp2":
                        dve.wait_ge(zeros, 3)
                        wait_full(dve, key)
                        for g in range(G):
                            m = V.tensor_copy(vc_bd[g * NP_:(g + 1) * NP_, g // 2, (g % 2) * HD:(g % 2 + 1) * HD],
                                              ps[g * NP_:(g + 1) * NP_, 0:HD])
                        m.then_inc(taken(key), 1)
                    elif kind == "glT":
                        wait_taken(dve, key)
                        gc = gate[:].rearrange("p t (h b) -> p t h b", b=3)[:, :, :, 0]
                        V.tensor_tensor(gc, gc, bc(c_valid[:], H, 2), ALU.mult).then_inc(gate_v, 1)
                    elif kind == "scT":
                        i = step[1]
                        sc = s_c[:, i].rearrange("p (a n) -> p a n", n=NP_)
                        wait_full(dve, key)
                        V.tensor_tensor(sc, ps[:].rearrange("p (a n) -> p a n", n=NP_), bc(c_mask[:, i], H, 1), ALU.add).then_inc(taken(key), 1)
                        wait_taken(dve, key)
                        step_(V.tensor_reduce(cst[:, i, 0], sc, AX.X, ALU.max, negate=True))
                        settled()
                        V.tensor_tensor(sc, sc, bc(cst[:, i, 0], NP_, 2), ALU.add).then_inc(cmp_v, 1)
                        dve.wait_ge(cmp_exp, i + 1)
                        step_(V.tensor_reduce(cst[:, i, 1], sc, AX.X, ALU.add))
                        settled()
                        step_(V.reciprocal(cst[:, i, 2], cst[:, i, 1]))
                        settled()
                        dve.wait_ge(gate_v, 1)
                        gc = gate[:, i].rearrange("p (g r b) -> p r g b", g=G, b=3)[:, :, :, 0]
                        step_(V.tensor_tensor(cst[:, i, 0].rearrange("p (r g) -> p r g", g=G),
                                              cst[:, i, 2].rearrange("p (r g) -> p r g", g=G), gc, ALU.mult))
                        settled()
                        V.tensor_tensor(sc, sc, bc(cst[:, i, 0], NP_, 2), ALU.mult).then_inc(cmp_scaled, 1)
                        if i == 1:
                            dve.wait_ge(lb_e, 1)
                            for ins in (lambda: V.tensor_tensor(lb[:, 0], lb[:, 1], lb[:, 2], ALU.add),
                                        lambda: V.reciprocal(lb[:, 3], lb[:, 0]),
                                        lambda: V.tensor_tensor(lb[:, 1:3], lb[:, 1:3], bc(lb[:, 3], 2, 1), ALU.mult),
                                        lambda: V.tensor_tensor(lb[:, 3], lb[:, 1], lb[:, 2], ALU.add),
                                        lambda: V.tensor_tensor(lb[:, 4], lb[:, 3], lb[:, 1], ALU.subtract),
                                        lambda: V.tensor_scalar(lb[:, 5], lb[:, 4], -1.0, 1.0, ALU.mult, ALU.add)):
                                step_(ins())
                                settled()
                    elif kind == "s":
                        it = step[1]
                        nb = 4 if ITEMS[it][0] == 0 else 2
                        wait_full(dve, key)
                        V.tensor_reduce(nmax[:, it, 0:nb], ps[:].rearrange("p (a b) -> p a b", a=nb), AX.X, ALU.max,
                                        negate=True).then_inc(rowmax, 1)
                        if it >= 1:
                            item_scale(it - 1)
                    elif kind == "pt":
                        it = step[1]
                        if it == NI - 2:
                            item_scale(NI - 1)
                        if it >= 2:
                            wait_pv(dve, it - 2)
                        wait_full(dve, key)
                        V.tensor_copy(prob_t[:, it % 2], ps[:]).then_inc(taken(key), 1)
                    elif kind == "pv":
                        job = key[1]
                        i, gp = JOBS[job]
                        dst = oT[:, 4 * gp:4 * gp + 4, i * P:(i + 1) * P]
                        src = ps[:].rearrange("p (k s) -> p k s", k=4)
                        wait_full(dve, key)
                        if i == 0:
                            V.tensor_copy(dst, src).then_inc(taken(key), 1)
                        else:
                            dve.wait_ge(z_silu, 1)
                            V.tensor_tensor(dst, src, zT[:, 4 * gp:4 * gp + 4, P:S], ALU.mult).then_inc(taken(key), 1)
                            dve.wait_ge(y_hi, job + 1)
                            hs = (slice(None), slice(4 * gp, 4 * gp + 4), slice(P, S))
                            V.tensor_tensor(h_lo[hs], oT[hs], h_hi[hs].bitcast(F32), ALU.subtract).then_inc(y_lo, 1)
                    elif kind == "pa" and step[1] in (U_O0, U_O1, V_O0, V_O1):
                        u, t = step[1], step[2]
                        c = (u - (U_O0 if u <= U_O1 else V_O0)) * UW
                        wait_full(dve, key)
                        V.tensor_tensor(x[:, t, c:c + UW], x[:, t, c:c + UW], ps[:], ALU.add).then_inc(taken(key), 1)
                    elif kind == "pb" and step[1] in (V_F0, V_F1) and step[2] == 1:
                        hh = int(step[1] == V_F1)
                        for m2 in range(2):
                            wait_taken(dve, ("pb", step[1], m2))
                        for h in range(4 * hh, 4 * hh + 4):
                            m = V.tensor_scalar(fg[:, h], fg[:, h], lb[:, 5, h:h + 1], lb[:, 4, h:h + 1], ALU.mult, ALU.add)
                        m.then_inc(f_lin, 1)
                        dve.wait_ge(f_lin, hh + 1)
                        V.tensor_scalar(kb[:, 4 * hh:4 * hh + 4], fg[:, 4 * hh:4 * hh + 4], -1.0, 1.0, ALU.mult, ALU.add).then_inc(k_lin, 1)
                    elif kind == "lev":
                        _, lv, hh, c = step
                        dst = attn[:, c, 4 * hh:4 * hh + 4]
                        src = ps[:].rearrange("p (h t) -> p h t", h=4)
                        wait_full(dve, key)
                        if lv == 0:
                            V.tensor_tensor(dst, src, bc(ident[:], 4, 1), ALU.mult).then_inc(taken(key), 1)
                        else:
                            s = LEVELS[lv - 1]
                            cut = lambda ap: ap.rearrange("p h (b u s) -> p h b u s", u=2, s=s)[:, :, :, 1]
                            dve.wait_ge(idents, 4)
                            V.copy_predicated(cut(dst), cut(bc(l_mask[:, lv - 1], 4, 1)), cut(src)).then_inc(taken(key), 1)
                        if c == 1:
                            hs = slice(4 * hh, 4 * hh + 4)
                            if lv == 0:
                                V.tensor_tensor(qa[:, hs], qa[:, hs], fg[:, hs], ALU.mult).then_inc(q_f, 1)
                            else:
                                half = qa[:, hs].rearrange("p h (b u s) -> p h b u s", u=2, s=s)[:, :, :, 1]
                                if lv == 1:
                                    dve.wait_ge(q_f, hh + 1)
                                else:
                                    dve.wait_ge(qa_up, 2 * (lv - 2) + hh + 1)
                                    dve.wait_ge(ft_up, 7 * hh + lv - 1)
                                V.tensor_tensor(half, half, bc(totals(s, hh)[:, :, :, 0], s, 3), ALU.mult).then_inc(qa_up, 1)
                    elif kind == "cross":
                        hh = step[1]
                        wait_full(dve, key)
                        V.tensor_copy(attx[:, 4 * hh:4 * hh + 4], ps[:].rearrange("p (h t) -> p h t", h=4)).then_inc(taken(key), 1)
                    elif kind == "o":
                        _, c, hh = step
                        o = 2 * c + hh
                        ys = y_hg[:, c, hh * UW:(hh + 1) * UW]
                        sq = fg[:].rearrange("p h s -> p (h s)")[:, o * 512:(o + 1) * 512]
                        dve.wait_ge(o_sq, o + 1)
                        V.tensor_reduce(ostat[:, o, 0], sq.rearrange("p (h v) -> p h v", h=4), AX.X, ALU.add).then_inc(o_sum, 1)
                        dve.wait_ge(z_g, 2 * hh + c + 1)
                        V.tensor_tensor(ys, ps[:], z_hg[:, c, hh * UW:(hh + 1) * UW], ALU.mult).then_inc(taken(key), 1)
                        dve.wait_ge(o_root, o + 1)
                        V.reciprocal(ostat[:, o, 2], ostat[:, o, 1]).then_inc(o_rstd, 1)
                        dve.wait_ge(o_rstd, o + 1)
                        wait_taken(dve, key)
                        y4 = ys.rearrange("p (h v) -> p h v", h=4)
                        V.tensor_tensor(y4, y4, bc(ostat[:, o, 2], P, 2), ALU.mult).then_inc(o_norm, 1)
                    if key == ("pb", U_Z1, 1):
                        dve.wait_ge(z_silu, 1)
                        for gp in range(2):
                            wait_taken(dve, ("pv", gp))
                            hs = (slice(None), slice(4 * gp, 4 * gp + 4), slice(0, P))
                            V.tensor_tensor(oT[hs], oT[hs], zT[hs], ALU.mult).then_inc(y_mul, 1)
                        for gp in range(2):
                            hs = (slice(None), slice(4 * gp, 4 * gp + 4), slice(0, P))
                            dve.wait_ge(y_hi, gp + 1)
                            V.tensor_tensor(h_lo[hs], oT[hs], h_hi[hs].bitcast(F32), ALU.subtract).then_inc(y_lo, 1)
                    if key == ("pv", 3):
                        norm(1, 0, y_hg[:, 0], 2, normed)
                    if key == ("pa", U_O1, 1):
                        norm(1, 1, y_hg[:, 1], 2, normed)
                    if kind == "pa" and step[1] == V_O1:
                        norm(2, step[2], y_hg[:, step[2]], 3, done_row)
                if kind in ("pa", "pb") and UNIT_LAST[step[1]] == n and step[1] + 2 < len(UNITS):
                    split_lo(step[1] + 2)

        @block.gpsimd
        def _(pool):
            GP = nc.gpsimd
            row = lambda ap: ap.unsqueeze(0).broadcast_to([P, D])
            pool.dma_start(g_row[:], row(t_in["norm_w"][0])).then_inc(g_in[0], 16)
            GP.memset(hidT[:], 0.0).then_inc(zeros, 1)
            GP.memset(kc_pad[:].bitcast(F32), 0.0).then_inc(zeros, 1)
            GP.memset(vc_bd[:], 0.0).then_inc(zeros, 1)
            pool.wait_ge(normed, TT)
            pool.dma_start(g_row[:], row(t_in["norm_w"][1])).then_inc(g_in[2], 16)

            for n, (step, _) in enumerate(SCHEDULE):
                kind, key = step[0], bank_key(step)
                if LAST[key] == n:
                    if kind == "pa" and step[1] in (U_KS, U_KW, U_Q0, U_Q1):
                        u, t = step[1], step[2]
                        j = STAGE.index((u, t))
                        is_k = u in (U_KS, U_KW)
                        w = (G if is_k else 8) * HD
                        if is_k:
                            pool.wait_ge(r_ab, j + 1)
                        else:
                            wait_taken(pool, key)
                        if j:
                            pool.wait_ge(r_lo, j)
                        GP.tensor_tensor(rp[:, 2, 0:w], rp[:, 0, 0:w], rp[:, 1, 0:w], ALU.add).then_inc(r_sum, 1)
                        pool.wait_ge(r_hi, j + 1)
                        if is_k:
                            v = lambda ap: ap.rearrange("p g (u d) -> p g u d", u=2)
                            GP.tensor_tensor(v(stg[:, j % 2, 4:8]), bc(rp[:, 2, 0:w].rearrange("p (g d) -> p g d", d=HD), 2, 2),
                                             v(stg[:, j % 2, 0:4]).bitcast(F32), ALU.subtract).then_inc(r_lo, 1)
                        else:
                            GP.tensor_tensor(stg[:, j % 2, :, HD:P], rp[:, 2].rearrange("p (h d) -> p h d", d=HD),
                                             stg[:, j % 2, :, 0:HD].bitcast(F32), ALU.subtract).then_inc(r_lo, 1)
                    elif kind == "pt":
                        it = step[1]
                        if it == 0:
                            scale_item(pool, 0)
                            scale_item(pool, 1)
                        if it + 2 < NI:
                            scale_item(pool, it + 2)
                    elif kind == "pb" and step[1] in (V_F0, V_F1) and step[2] == 1:
                        hh = int(step[1] == V_F1)
                        pool.wait_ge(f_lin, hh + 1)
                        for lv, s in enumerate(LEVELS):
                            if lv:
                                pool.wait_ge(ft_up, 7 * hh + lv)
                            tt = totals(s, hh)
                            GP.tensor_tensor(level_totals(2 * s, hh), tt[:, :, :, 0], tt[:, :, :, 1], ALU.mult).then_inc(ft_up, 1)
                    elif kind == "lev" and step[1] >= 1 and step[3] == 1:
                        _, lv, hh, c = step
                        s = LEVELS[lv - 1]
                        wait_full(pool, key)
                        if lv == 1:
                            pool.wait_ge(k_lin, hh + 1)
                            pool.wait_ge(f_lin, hh + 1)
                        else:
                            pool.wait_ge(kb_up, 2 * (lv - 2) + hh + 1)
                            pool.wait_ge(ft_up, 7 * hh + lv - 1)
                        half = kb[:, 4 * hh:4 * hh + 4].rearrange("p h (b u s) -> p h b u s", u=2, s=s)[:, :, :, 0]
                        GP.tensor_tensor(half, half, bc(totals(s, hh)[:, :, :, 1], s, 3), ALU.mult).then_inc(kb_up, 1)
                    elif kind == "pa" and step[1] in (V_Z0, V_Z1):
                        u, t = step[1], step[2]
                        wait_taken(pool, key)
                        pool.wait_ge(g_in[1], 16)
                        zs = z_hg[:, t, (u - V_Z0) * UW:(u - V_Z0 + 1) * UW]
                        GP.tensor_tensor(zs, zs, g_row[:, (u - V_Z0) * UW:(u - V_Z0 + 1) * UW], ALU.mult).then_inc(z_g, 1)
                        if u == V_Z1 and t == 1:
                            pool.wait_ge(z_g, 4)
                            pool.dma_start(g_row[:], row(t_in["final_norm"])).then_inc(g_in[3], 16)
                    if key == ("hT", 1, 1, 1):
                        pool.wait_ge(normed, 2 * TT)
                        pool.dma_start(g_row[:], row(t_in["hg_norm"])).then_inc(g_in[1], 16)


def shape_constants():
    f = np.float32
    half = HD // 2
    inv = (f(10000.0) ** (-np.arange(half, dtype=f) / f(half))).astype(f)

    def table(pos, scale):
        ang = pos.astype(f)[:, None] * inv[None, :]
        co, si = np.cos(ang), np.sin(ang)
        return np.concatenate([co, co], 1) * f(scale), np.concatenate([-si, si], 1) * f(scale)

    pos = np.arange(S)
    q, k = table(pos, HD ** -0.5), table(pos, 1.0)
    rope = np.stack([q[0], q[1], k[0], k[1]]).astype(f)
    rope = rope.reshape(4, TT, P, HD).transpose(2, 0, 1, 3)
    end = np.arange(NP_) * CS + CB - 1
    c = table(end, 1.0)
    rope_c = np.tile(np.stack(c, 1), (G, 1, 1)).astype(f)
    seen = (end[None, :] <= pos[:, None]) & (np.arange(NP_) < NC)[None, :]
    c_mask = np.where(seen, 0.0, NEG).astype(f).reshape(TT, P, NP_).transpose(1, 0, 2)
    c_valid = seen.any(1).astype(f).reshape(TT, P).T
    a = np.arange(P)
    tri = np.where(a[None, :] <= a[:, None], 0.0, NEG).astype(f)
    lm = np.stack([(a[:, None] // (2 * s) == a[None, :] // (2 * s)) & (a[:, None] // s % 2 == 0) & (a[None, :] // s % 2 == 1)
                   for s in LEVELS], 1).astype(f)
    return {"c_ident": np.eye(P, dtype=f), "c_rope": rope, "c_rope_c": rope_c, "c_mask": c_mask, "c_valid": c_valid,
            "c_tri": tri, "c_levels": lm}


def kernel(x, norm_w, nsa_w_in, nsa_pe_k, nsa_pe_v, nsa_wk1, nsa_wk2, nsa_wv1, nsa_wv2, nsa_w_out,
           hg_w_in, hg_lb_logits, hg_norm, hg_w_out, final_norm):
    import concourse.bacc as bacc
    from concourse.bass_utils import run_bass_kernel_spmd

    lay = np.ascontiguousarray
    pe_of = lambda pe: np.asarray(pe)[0].reshape(2, CS, HD).transpose(0, 2, 1).reshape(P, CS)
    arrays = {
        "x": np.asarray(x)[0], "norm_w": norm_w, "nsa": np.asarray(nsa_w_in)[0], "nsa_out": np.asarray(nsa_w_out)[0],
        "hg": np.asarray(hg_w_in)[0], "hg_out": np.asarray(hg_w_out)[0],
        "w1k": np.asarray(nsa_wk1)[0], "w1v": np.asarray(nsa_wv1)[0],
        "w2k": np.asarray(nsa_wk2)[0], "w2v": np.asarray(nsa_wv2)[0],
        "pe": np.stack([pe_of(nsa_pe_k), pe_of(nsa_pe_v)], 1),
        "lb": np.asarray(hg_lb_logits).reshape(2, HH, P).transpose(2, 0, 1),
        "hg_norm": np.asarray(hg_norm)[0], "final_norm": final_norm,
    } | shape_constants()
    arrays = {f"in_{k}": lay(v) for k, v in arrays.items()}
    nc = bacc.Bacc("TRN2", target_bir_lowering=False, num_devices=1)
    t_in = {k[3:]: nc.dram_tensor(k, v.shape, mybir.dt.from_np(v.dtype), kind="ExternalInput").ap() for k, v in arrays.items()}
    t_in["ident"] = t_in["c_ident"]
    out = nc.dram_tensor("out", (S, D), F32, kind="ExternalOutput").ap()
    program(nc, t_in, out)
    got = run_bass_kernel_spmd(nc, [arrays], core_ids=[0])
    return got.results[0]["out"].reshape(1, S, D)
```

```python
from contextlib import ExitStack

import numpy as np

import concourse.bass as bass
from concourse import mybir

P = 128
D = 1024
S = 256
KT = D // P
TT = S // P
UW = 512
H, G, R, HD = 16, 4, 4, 64
CB, CS, NC, NP_ = 32, 16, 15, 32
CH = 256
HH = 8
EPS = 1e-6
NEG = -1e30
NQ = 4
LEVELS = [1, 2, 4, 8, 16, 32, 64]

F32 = mybir.dt.float32
FR = mybir.dt.float32r
BF16 = mybir.dt.bfloat16
U8 = mybir.dt.uint8
ALU = mybir.AluOpType
ACT = mybir.ActivationFunctionType
AX = mybir.AxisListType

NSA_Q, NSA_KC, NSA_KS, NSA_KW, NSA_GL, NSA_Z = 0, 1024, 1536, 2048, 2560, 2608
UNITS = [("nsa", NSA_KC), ("nsa", NSA_KS), ("nsa", NSA_KW), ("nsa", NSA_Q), ("nsa", NSA_Q + UW),
         ("nsa", NSA_Z), ("nsa", NSA_Z + UW), ("nsa_out", 0), ("nsa_out", UW),
         ("hg", 2048), ("hg", 2560), ("hg", 1024), ("hg", 0), ("hg", 1536), ("hg", 512),
         ("hg", 3072), ("hg", 3584), ("hg_out", 0), ("hg_out", UW)]
U_KC, U_KS, U_KW, U_Q0, U_Q1, U_Z0, U_Z1, U_O0, U_O1 = range(9)
V_V0, V_V1, V_F0, V_Q0, V_F1, V_Q1, V_Z0, V_Z1, V_O0, V_O1 = range(9, 19)
NRAW = 2
NS = 3

ITEMS = [(0, gp, 2 * gp + g2, rp, None) for gp in range(2) for g2 in range(2) for rp in range(2)]
ITEMS += [(1, gp, 2 * gp + g2, rp, b) for gp in range(2) for g2 in range(2) for rp in range(2)
          for b in range(2)]
NI = len(ITEMS)
JOBS = [(i, gp) for i in range(2) for gp in range(2)]
ITEM_JOB = [JOBS.index((it[0], it[1])) for it in ITEMS]
JOB_LAST = [max(n for n in range(NI) if ITEM_JOB[n] == j) for j in range(4)]
JOB_FIRST = [min(n for n in range(NI) if ITEM_JOB[n] == j) for j in range(4)]
Z_ORDER = [(V_Z0, 0), (V_Z1, 0), (V_Z0, 1), (V_Z1, 1)]
STEPS_L = ["diag"] + LEVELS


def schedule():
    out = []

    def add(*step, banks=()):
        out.append((step, tuple(banks)))

    def pa(u, t, bank, slices=range(4)):
        for sl in slices:
            add("pa", u, t, sl, banks=(bank,))

    def pb(u, m2, bank, slices=range(4)):
        for sl in slices:
            add("pb", u, m2, sl, banks=(bank,))

    def stage(j):
        for half in range(2):
            add("stage", j, half, banks=(4 + half,))

    for t in range(TT):
        for q in range(2):
            add("hT", 0, t, q, banks=(4 + 2 * t + q,))
    pb(U_KC, 0, 0)
    pb(U_KC, 1, 1)
    pa(U_KS, 0, 2)
    pa(U_KS, 1, 3)
    stage(0)
    add("cmp1", 0, banks=(6,))
    pa(U_KW, 0, 0)
    stage(1)
    add("gl", banks=(7,))
    add("cmpT", 0, banks=(6,))
    pa(U_KW, 1, 1)
    stage(2)
    add("glT", banks=(7,))
    add("cmp2", 0, banks=(6,))
    pa(U_Q0, 0, 2)
    stage(3)
    add("cmp1", 1, banks=(6,))
    pa(U_Q0, 1, 3)
    add("kcT", banks=(7,))
    stage(4)
    add("cmpT", 1, banks=(6,))
    pa(U_Q1, 0, 0)
    stage(5)
    add("cmp2", 1, banks=(6,))
    pa(U_Q1, 1, 1)
    stage(6)
    z = [(u, m2, sl) for u in (U_Z0, U_Z1) for m2 in range(2) for sl in range(4)]
    fill = [(("pb",) + s, 2 + s[1]) for s in z]
    fill += [(("pa", u, 0, sl), 2 + (u - U_O0)) for u in (U_O0, U_O1) for sl in range(4)]

    def filler(n):
        for _ in range(n):
            if fill:
                step, bank = fill.pop(0)
                add(*step, banks=(bank,))

    filler(6)
    stage(7)
    filler(2)
    for i in range(2):
        add("sc", i, banks=(7,))
        filler(2 - i)
        add("scT", i, banks=(7,))
        filler(1)
    for n in range(NS):
        add("s", n, banks=(4 + n,))
    filler(1)
    add("pcT", 0, banks=(7,))
    filler(1)
    add("pcT", 1, banks=(7,))
    filler(1)
    assert len(fill) == 8
    for n in range(NI):
        add("pt", n, banks=(7,))
        if n + NS < NI:
            add("s", n + NS, banks=(4 + n % NS,))
        if n >= 1:
            add("pv", n - 1, banks=(ITEM_JOB[n - 1] % 2,))
        if n >= 10 and n % 2 == 0:
            filler(1)
    add("pv", NI - 1, banks=(ITEM_JOB[NI - 1] % 2,))
    filler(len(fill))
    pa(U_O0, 1, 4)
    pa(U_O1, 1, 5, range(0, 2))
    add("hT", 1, 0, 0, banks=(0,))
    add("hT", 1, 0, 1, banks=(1,))
    pa(U_O1, 1, 5, range(2, 4))
    pa(V_V0, 0, 2)
    pa(V_V1, 0, 3)
    add("hT", 1, 1, 0, banks=(6,))
    add("hT", 1, 1, 1, banks=(7,))
    pa(V_V0, 1, 0)
    pa(V_V1, 1, 1)
    for hh, (uf, uq) in enumerate(((V_F0, V_Q0), (V_F1, V_Q1))):
        pb(uf, 0, 2)
        pb(uf, 1, 3)
        pb(uq, 0, 0)
        pb(uq, 1, 1)
    zs = [(("pa", u, t, sl), 2 * (u - V_Z0) + t) for u, t in Z_ORDER for sl in range(4)]
    slot = 0
    for lv in range(len(STEPS_L)):
        for hh in range(2):
            for c in range(TT):
                add("lev", lv, hh, c, banks=(4 + 2 * hh + c,))
            if slot % 4 != 3:
                step, bank = zs.pop(0)
                add(*step, banks=(bank,))
            slot += 1
    for hh in range(2):
        add("cross", hh, banks=(4 + 2 * hh,))
    for hh in range(2):
        add("o", 0, hh, banks=(hh,))
    for step, bank in zs:
        add(*step, banks=(bank,))
    for q in range(2):
        add("yT", 0, q, banks=(4 + q,))
    for hh in range(2):
        add("o", 1, hh, banks=(2 + hh,))
    pa(V_O0, 0, 0)
    pa(V_O1, 0, 1, range(0, 2))
    for q in range(2):
        add("yT", 1, q, banks=(6 + q,))
    pa(V_O1, 0, 1, range(2, 4))
    pa(V_O0, 1, 2)
    pa(V_O1, 1, 3)
    return out


def bank_key(step):
    if step[0] in ("pa", "pb"):
        return step[:3]
    if step[0] == "pv":
        return ("pv", ITEM_JOB[step[1]])
    return step


SCHEDULE = schedule()


def bank_uses():
    uses, filled, last = {}, [0] * 8, {}
    open_ = {}
    for n, (step, banks) in enumerate(SCHEDULE):
        for b in banks:
            key = bank_key(step)
            if key not in uses:
                uses[key] = (b, filled[b])
                filled[b] += 1
            assert uses[key][0] == b and (b not in open_ or open_[b] == key or filled[b] == uses[key][1] + 1), step
            assert filled[b] == uses[key][1] + 1, step
            open_[b] = key
            last[key] = n
    return uses, last


USES, LAST = bank_uses()
UNIT_FIRST, UNIT_LAST = {}, {}
for _n, (_step, _) in enumerate(SCHEDULE):
    if _step[0] in ("pa", "pb"):
        UNIT_FIRST.setdefault(_step[1], _n)
        UNIT_LAST[_step[1]] = _n


def split_places():
    places, before = {}, 0
    for u in range(2, len(UNITS)):
        free, used = UNIT_LAST[u - 2], UNIT_FIRST[u]
        for q in range(NQ):
            before = n = max(before, free + min(used - free, SPAN) * SPREAD[q] // 8)
            assert n < used
            places.setdefault(n, []).append((u, q))
    return places


SPAN, SPREAD = 12, (1, 3, 5, 7)
SPLIT_AT = split_places()


def program(nc, t_in, out):
    with ExitStack() as ctx:
        def sb(name, shape, dt=F32, scope=ctx):
            return scope.enter_context(nc.sbuf_tensor(name, shape, dt))

        raw = sb("raw", [P, NRAW, KT, UW])
        w_hi = sb("w_hi", [P, 2, KT, UW], FR)
        w_lo = sb("w_lo", [P, 2, KT, UW], FR)
        x = sb("x_res", [P, TT, D])
        h_hi = sb("h_hi", [P, KT, S], FR)
        h_lo = sb("h_lo", [P, KT, S], FR)
        g_row = sb("g_row", [P, D])
        ident = sb("ident", [P, P])
        ident_r = sb("ident_r", [P, P], FR)
        ident_b = sb("ident_b", [P, P], BF16)
        tri_b = sb("tri_b", [P, P], BF16)
        rope = sb("rope", [P, 4, TT, HD])
        rope_c = sb("rope_c", [P, 2, HD])
        c_mask = sb("c_mask", [P, TT, NP_])
        c_valid = sb("c_valid", [P, TT])
        l_mask = sb("l_mask", [P, len(LEVELS), P], U8)
        pe_t = sb("pe_t", [P, 2, CS])
        w2 = sb("w2", [P, 2, 2, HD])
        lbl = sb("lbl", [P, 2, HH])
        lb = sb("lb", [P, 6, HH])
        stat = sb("stat", [P, 3, 3, TT])
        eps_t = sb("eps_t", [P, 1])
        nmax = sb("nmax", [P, NI, 4])
        rsum = sb("rsum", [P, NI, 4])
        rrec = sb("rrec", [P, NI, 4])
        scl = sb("scl", [P, NI, 4])
        gate = sb("gate", [P, TT, 48])
        ostat = sb("ostat", [P, 4, 4, 4])

        nsa = ExitStack()
        cw = ExitStack()
        w1 = sb("w1", [P, CS, CH], F32, cw)
        cw.close()
        q2 = sb("q2", [P, H, S], FR, nsa)
        k2 = sb("k2", [P, 2, 2, G, S], FR, nsa)
        v_tok = sb("v_tok", [P, TT, 2, G, HD], F32, nsa)
        l_land = v_tok[:].rearrange("p t b g d -> p (t b g d)")[:, 0:len(LEVELS) * P]
        kc_pad = sb("kc_pad", [P, 2, G, P], FR, nsa)
        vc_bd = sb("vc_bd", [P, 2, P], F32, nsa)
        zT = sb("zT", [P, KT, S], F32, nsa)
        xn = zT[:].rearrange("p k s -> p (k s)").rearrange("p (t d) -> p t d", t=TT)
        flat = zT[:].rearrange("p k s -> p (k s)").rearrange("p (v j g n) -> p v j g n", v=2, j=CS, g=G)
        pre = ExitStack()
        stg = sb("stg", [P, 2, 8, P], FR, pre)
        rp = sb("rp", [P, 3, UW], F32, pre)
        hid = sb("hid", [G * CS, CH], F32, pre)
        hidT = sb("hidT", [P, 2, 2, P], F32, pre)
        kcr = sb("kcr", [P, 3, HD], F32, pre)
        tri = kcr[:, 0:2].rearrange("p a d -> p (a d)")
        kcs = sb("kcs", [P, 2, P], FR, pre)
        wg = sb("wg", [P, KT, 48], F32, pre)
        wg_hi = sb("wg_hi", [P, KT, 48], FR, pre)
        wg_lo = sb("wg_lo", [P, KT, 48], FR, pre)
        gT = sb("gT", [48, S], F32, pre)
        pre.close()
        att = ExitStack()
        prob = sb("prob", [P, NS + 1, 512], F32, att)
        prob_t = sb("prob_t", [P, 2, 512], F32, att)
        oT = sb("oT", [P, KT, S], F32, att)
        p_ct = sb("p_ct", [P, 2, 512], F32, att)
        xn_1 = p_ct[:].rearrange("p i c -> p (i c)")
        cst = sb("cst", [P, 2, 3, 16], F32, att)
        att.close()
        s_ct = oT[:].rearrange("p k s -> p (k s)")[:, 0:512]
        s_c = oT[:].rearrange("p k s -> p (k s)")[:, 512:1536].rearrange("p (i c) -> p i c", i=TT)
        nsa.close()

        hg = ExitStack()
        qa = sb("qa", [P, HH, S], F32, hg)
        kb = sb("kb", [P, HH, S], F32, hg)
        fg = sb("fg", [P, HH, S], F32, hg)
        ft = sb("ft", [P, HH, S], F32, hg)
        attn = sb("attn", [P, TT, HH, P], F32, hg)
        attx = sb("attx", [P, HH, P], F32, hg)
        v_hg = sb("v_hg", [P, TT, D], F32, hg)
        z_hg = sb("z_hg", [P, TT, D], F32, hg)
        y_hg = sb("y_hg", [P, TT, D], F32, hg)
        junk = sb("junk", [P, D], BF16, hg)
        hg.close()

        bank = [ctx.enter_context(nc.psum_tensor(f"bank{b}", [P, 512], F32)) for b in range(8)]

        def sem(name):
            return ctx.enter_context(nc.semaphore(name))

        raw_in = [sem(f"raw_in{i}") for i in range(NRAW)]
        first_in = [sem(f"first_in{q}") for q in range(NQ)]
        w1_in = [sem(f"w1_in{kv}") for kv in range(2)]
        x_in = [sem(f"x_in{t}") for t in range(TT)]
        const_in = sem("const_in")
        wg_in = sem("wg_in")
        g_in = [sem(f"g_in{i}") for i in range(4)]
        hi_done = sem("hi_done")
        lo_done = sem("lo_done")
        ident_in = sem("ident_in")
        pv_done = sem("pv_done")
        vec_step = sem("vec_step")
        act_step = sem("act_step")
        pool_step = sem("pool_step")
        filled = [sem(f"filled{b}") for b in range(8)]
        drained = [sem(f"drained{b}") for b in range(8)]
        taken_hi = sem("taken_hi")
        idents = sem("idents")
        eps_set = sem("eps_set")
        sumsq = sem("sumsq")
        root = sem("root")
        rstd = sem("rstd")
        normed = sem("normed")
        r_ab = sem("r_ab")
        r_sum = sem("r_sum")
        r_hi = sem("r_hi")
        r_lo = sem("r_lo")
        flat_zero = sem("flat_zero")
        hid_done = sem("hid_done")
        kc_v = sem("kc_v")
        zeros = sem("zeros")
        wg_hi_d = sem("wg_hi_d")
        wg_lo_d = sem("wg_lo_d")
        gate_v = sem("gate_v")
        cmp_v = sem("cmp_v")
        cmp_exp = sem("cmp_exp")
        cmp_scaled = sem("cmp_scaled")
        rowmax = sem("rowmax")
        expd = sem("expd")
        recip_d = sem("recip_d")
        scale_d = sem("scale_d")
        scaled = sem("scaled")
        z_silu = sem("z_silu")
        y_hi = sem("y_hi")
        y_lo = sem("y_lo")
        lb_v = sem("lb_v")
        lb_e = sem("lb_e")
        f_lin = sem("f_lin")
        k_lin = sem("k_lin")
        q_f = sem("q_f")
        qa_up = sem("qa_up")
        kb_up = sem("kb_up")
        ft_up = sem("ft_up")
        z_g = sem("z_g")
        o_sq = sem("o_sq")
        o_sum = sem("o_sum")
        o_root = sem("o_root")
        o_rstd = sem("o_rstd")
        o_norm = sem("o_norm")
        done_row = sem("done_row")
        out_done = sem("out_done")

        def wait_full(eng, key):
            b, k = USES[key]
            eng.wait_ge(filled[b], k + 1)

        def wait_taken(eng, key):
            b, k = USES[key]
            eng.wait_ge(drained[b], k + 1)

        def full(key):
            return filled[USES[key][0]]

        def taken(key):
            return drained[USES[key][0]]

        def bk(key):
            return bank[USES[key][0]]

        def wait_residual(eng, u, t):
            wait_taken(eng, ("pa", u, t))
            wait_taken(eng, ("pa", u + 1, t))

        def wait_unit_used(eng, u):
            wait_full(eng, bank_key(SCHEDULE[UNIT_LAST[u]][0]))

        def wait_pv(eng, it):
            if it == JOB_LAST[ITEM_JOB[it]]:
                wait_full(eng, ("pv", ITEM_JOB[it]))
            else:
                eng.wait_ge(pv_done, it + 1 - sum(j < it for j in JOB_LAST))

        def bc(ap, n, at):
            shape = list(ap.shape)
            return ap.unsqueeze(at).broadcast_to(shape[:at] + [n] + shape[at:])


        def level_totals(s, hh):
            hs = slice(4 * hh, 4 * hh + 4)
            if s == 1:
                return fg[:, hs]
            at = S - 2 * S // s
            return ft[:, hs, at:at + S // s]

        def totals(s, hh):
            return level_totals(s, hh).rearrange("p h (b u) -> p h b u", u=2)

        def scale_item(pool, it):
            pool.wait_ge(scale_d, it + 1)
            nb = 4 if ITEMS[it][0] == 0 else 2
            v = lambda ap: ap.rearrange("p (a b) -> p a b", a=nb)
            pb_ = prob[:, it % (NS + 1)]
            nc.gpsimd.tensor_tensor(v(pb_), v(pb_), bc(scl[:, it, 0:nb], 512 // nb, 2),
                                    ALU.mult).then_inc(scaled, 1)

        def split_parts(u, q):
            if u not in (U_Z0, U_Z1):
                sl = slice(2 * q, 2 * q + 2)
                return [(w_hi[:, u % 2, sl], raw[:, u % NRAW, sl], w_lo[:, u % 2, sl])]
            tile = lambda w, kk: w[:, u % 2, kk].rearrange("p (r g d) -> p r g d", r=R, d=HD)
            return [(tile(w_hi, kk), raw[:, u % NRAW, kk].rearrange("p (g r d) -> p r g d", r=R, d=HD), tile(w_lo, kk))
                    for kk in (2 * q, 2 * q + 1)]

        CONST_LOADS = [(rope[:], t_in["c_rope"]), (rope_c[:], t_in["c_rope_c"]), (c_mask[:], t_in["c_mask"]),
                       (c_valid[:], t_in["c_valid"]), (tri, t_in["c_tri"]), (l_land, t_in["c_levels"].rearrange("p l q -> p (l q)")),
                       (pe_t[:], t_in["pe"]), (lbl[:], t_in["lb"]),
                       (w2[:, 0], t_in["w2k"].rearrange("(c p) d -> p c d", p=P)),
                       (w2[:, 1], t_in["w2v"].rearrange("(c p) d -> p c d", p=P))]
        N_CONST = len(CONST_LOADS)

        STAGE = [(U_KS, 0), (U_KS, 1), (U_KW, 0), (U_KW, 1), (U_Q0, 0), (U_Q0, 1), (U_Q1, 0), (U_Q1, 1)]
        block = ctx.enter_context(nc.Block())

        def load_w1(eng, kv):
            w = t_in["w1" + kv].rearrange("(a j d) h -> a d j h", a=2, d=HD)
            for a in range(2):
                eng.dma_start(w1[a * HD:(a + 1) * HD], w[a]).then_inc(w1_in["kv".index(kv)], 16)

        @block.sync
        def _(sp):
            sp.dma_start(x[:, 0], t_in["x"][0:P, :]).then_inc(x_in[0], 16)
            sp.dma_start(ident[:], t_in["ident"]).then_inc(ident_in, 16)
            sp.dma_start(x[:, 1], t_in["x"][P:2 * P, :]).then_inc(x_in[1], 16)
            for u, (kind, col) in enumerate(UNITS):
                if u == NRAW:
                    sp.dma_start(wg[:], t_in["nsa"][:, NSA_GL:NSA_Z].rearrange("(k p) n -> p k n", p=P)).then_inc(wg_in, 16)
                    for dst, src in CONST_LOADS:
                        sp.dma_start(dst, src).then_inc(const_in, 16)
                    load_w1(sp, "k")
                if u >= NRAW:
                    sp.wait_ge(lo_done, NQ * (u - NRAW + 1))
                dst = raw[:, u % NRAW]
                w = t_in[kind][:, col:col + UW]
                if kind == "nsa_out":
                    w = w.rearrange("(gp g2 r d) n -> g2 d gp r n", gp=2, g2=2, r=R)
                    for g2 in range(2):
                        for gp in range(2):
                            sp.dma_start(dst[g2 * HD:(g2 + 1) * HD, gp * R:(gp + 1) * R], w[g2][:, gp]).then_inc(raw_in[u % NRAW], 16)
                    continue
                w = w.rearrange("(k p) n -> p k n", p=P)
                if u == 0:
                    for q in range(NQ):
                        sp.dma_start(dst[:, 2 * q:2 * q + 2], w[:, 2 * q:2 * q + 2]).then_inc(first_in[q], 16)
                    continue
                for half in range(2):
                    sp.dma_start(dst[:, 4 * half:4 * half + 4], w[:, 4 * half:4 * half + 4]).then_inc(raw_in[u % NRAW], 16)
            for t in range(TT):
                sp.wait_ge(done_row, t + 1)
                sp.dma_start(out[t * P:(t + 1) * P, :], y_hg[:, t]).then_inc(out_done, 16)
            sp.wait_ge(out_done, 16 * TT)

        def raw_count(u):
            return 16 * sum(4 if UNITS[m][0] == "nsa_out" else 2 for m in range(u % NRAW, u + 1, NRAW) if m)

        @block.tensor
        def _(pe):
            def mm(o, lhsT, rhs, start, stop):
                return nc.tensor.matmul(o, lhsT, rhs, start=start, stop=stop, skip_group_check=True)

            def parts(u, sl_first, kk):
                pe.wait_ge(lo_done, NQ * u + kk // 2 + 1)

            def act_ready(L, t, u):
                if u in (U_O0, U_O1):
                    pe.wait_ge(y_lo, 2 * t + 2)
                elif u in (V_O0, V_O1):
                    for q in range(2):
                        wait_taken(pe, ("yT", t, q))
                else:
                    for q in range(2):
                        wait_taken(pe, ("hT", L, t, q))

            for n, (step, banks) in enumerate(SCHEDULE):
                kind = step[0]
                key = bank_key(step)
                b, k = USES[key]
                ps = bank[b]
                first = not any(bank_key(s) == key for s, _ in SCHEDULE[:n])
                last_of_bank = LAST[key] == n
                if first and k > 0:
                    pe.wait_ge(drained[b], k)
                if kind == "hT":
                    _, L, t, q = step
                    pe.wait_ge(normed, TT * L + t + 1)
                    if n == 0:
                        pe.wait_ge(ident_in, 16)
                    src = xn[:, t] if L == 0 else xn_1 if t == 0 else y_hg[:, t]
                    for j in range(4):
                        c = (4 * q + j) * P
                        m = nc.tensor.transpose(ps[:, j * P:(j + 1) * P], src[:, c:c + P], ident[:])
                elif kind == "pa":
                    _, u, t, sl = step
                    if sl == 0:
                        act_ready(0 if u <= U_O1 else 1, t, u)
                    for kk in (2 * sl, 2 * sl + 1):
                        parts(u, sl, kk)
                        hi = h_hi[:, kk, t * P:(t + 1) * P]
                        mm(ps[:], hi, w_hi[:, u % 2, kk], kk == 0, False)
                        mm(ps[:], hi, w_lo[:, u % 2, kk], False, False)
                        m = mm(ps[:], h_lo[:, kk, t * P:(t + 1) * P], w_hi[:, u % 2, kk], False, kk == KT - 1)
                elif kind == "pb":
                    _, u, m2, sl = step
                    if m2 == 0 and sl == 0:
                        for t in range(TT):
                            act_ready(0 if u <= U_O1 else 1, t, u)
                    j = 2 * m2 + sl // 2
                    for kk in range(4 * (sl % 2), 4 * (sl % 2) + 4):
                        parts(u, sl, kk)
                        o = ps[:, (j % 2) * S:(j % 2 + 1) * S]
                        cols = lambda w: w[:, u % 2, kk, j * P:(j + 1) * P]
                        mm(o, cols(w_hi), h_hi[:, kk], kk == 0, False)
                        mm(o, cols(w_hi), h_lo[:, kk], False, False)
                        m = mm(o, cols(w_lo), h_hi[:, kk], False, kk == KT - 1)
                elif kind == "stage":
                    _, j, half = step
                    pe.wait_ge(r_lo, j + 1)
                    if j == 0 and half == 0:
                        pe.wait_ge(idents, 1)
                    for c in range(4):
                        m = nc.tensor.transpose(ps[:, c * P:(c + 1) * P].bitcast(FR), stg[:, j % 2, 4 * half + c], ident_r[:])
                elif kind == "cmp1":
                    kv = step[1]
                    wait_taken(pe, ("pb", U_KC, kv))
                    pe.wait_ge(flat_zero, 1)
                    pe.wait_ge(w1_in[kv], 32)
                    for j in range(CS):
                        m = mm(ps[0:G * CS, 0:CH], flat[:, kv, j].rearrange("p g n -> p (g n)"), w1[:, j], j == 0, j == CS - 1)
                elif kind == "cmpT":
                    kv = step[1]
                    wait_taken(pe, ("cmp1", kv))
                    for c in range(2):
                        m = nc.tensor.transpose(ps[:, c * HD:(c + 1) * HD], hid[:, c * P:(c + 1) * P], ident[0:HD, 0:HD])
                elif kind == "cmp2":
                    kv = step[1]
                    if kv == 0:
                        pe.wait_ge(const_in, 16 * N_CONST)
                    wait_taken(pe, ("cmpT", kv))
                    for c in range(2):
                        m = mm(ps[:, 0:HD], hidT[:, kv, c], w2[:, kv, c], c == 0, c == 1)
                elif kind == "kcT":
                    pe.wait_ge(kc_v, 1)
                    for c in range(2):
                        m = nc.tensor.transpose(ps[:, c * P:(c + 1) * P].bitcast(FR), kcs[:, c], ident_r[:])
                elif kind == "gl":
                    pe.wait_ge(wg_lo_d, 1)
                    for kk in range(KT):
                        mm(ps[0:48, 0:S], wg_hi[:, kk], h_hi[:, kk], kk == 0, False)
                        mm(ps[0:48, 0:S], wg_hi[:, kk], h_lo[:, kk], False, False)
                        m = mm(ps[0:48, 0:S], wg_lo[:, kk], h_hi[:, kk], False, kk == KT - 1)
                elif kind == "glT":
                    wait_taken(pe, ("gl",))
                    for t in range(TT):
                        m = nc.tensor.transpose(ps[:, t * 48:(t + 1) * 48], gT[:, t * P:(t + 1) * P], ident[0:48, 0:48])
                elif kind == "sc":
                    i = step[1]
                    wait_taken(pe, ("kcT",))
                    for j in range(4 + i, 8, 2):
                        for half in range(2):
                            wait_taken(pe, ("stage", j, half))
                    for g in range(G):
                        for part in range(2):
                            m = mm(ps[:], kc_pad[:, part, g], q2[:, g * R:(g + 1) * R, i * P:(i + 1) * P],
                                   g == 0 and part == 0, g == G - 1 and part == 1)
                elif kind == "scT":
                    i = step[1]
                    wait_taken(pe, ("sc", i))
                    for r in range(R):
                        m = nc.tensor.transpose(ps[:, r * P:(r + 1) * P], s_ct[:, r * P:(r + 1) * P], ident[:])
                elif kind == "pcT":
                    i = step[1]
                    pe.wait_ge(cmp_scaled, i + 1)
                    for r in range(R):
                        m = nc.tensor.transpose(ps[:, r * P:(r + 1) * P], s_c[:, i, r * P:(r + 1) * P], ident[:])
                elif kind == "s":
                    i, gp, g, rp_, br = ITEMS[step[1]]
                    if step[1] == 0:
                        for half in range(2):
                            wait_taken(pe, ("stage", 7, half))
                        pe.wait_ge(idents, 3)
                    for r2 in range(2):
                        h = g * R + 2 * rp_ + r2
                        for part in range(2):
                            keys = k2[:, part, :, g, 0:P] if i == 0 else k2[:, part, br, g]
                            mm(ps[:, r2 * S:(r2 + 1) * S], q2[:, h, i * P:(i + 1) * P], keys, r2 == 0 and part == 0, False)
                    if i == 0:
                        m = mm(ps[:], ident_b[:], bc(tri_b[:], 4, 1), False, True)
                    else:
                        m = mm(ps[:].rearrange("p (r k q) -> p r k q", r=2, k=2)[:, :, 1], ident_b[:], bc(tri_b[:], 2, 1), False, True)
                elif kind == "pt":
                    it = step[1]
                    pe.wait_ge(scaled, it + 1)
                    for c in range(4):
                        m = nc.tensor.transpose(ps[:, c * P:(c + 1) * P], prob[:, it % (NS + 1), c * P:(c + 1) * P], ident[:])
                elif kind == "pv":
                    it = step[1]
                    i, gp, g, rp_, br = ITEMS[it]
                    if first:
                        wait_taken(pe, ("cmp2", 1))
                        wait_taken(pe, ("pcT", i))
                        mm(ps[:], vc_bd[:, gp], p_ct[:, i], True, False)
                    wait_taken(pe, ("pt", it))
                    for c in range(4):
                        r2, c2 = c // 2, c % 2
                        vb, kt = (c2, 0) if i == 0 else (br, c2)
                        r = 2 * rp_ + r2
                        o = ps[(g % 2) * HD:(g % 2 + 1) * HD, r * P:(r + 1) * P]
                        m = mm(o, v_tok[:, kt, vb, g], prob_t[:, it % 2, c * P:(c + 1) * P], False, last_of_bank)
                elif kind == "lev":
                    _, lv, hh, c = step
                    if lv == 0:
                        for m2 in range(2):
                            wait_taken(pe, ("pb", (V_Q0, V_Q1)[hh], m2))
                        pe.wait_ge(k_lin, hh + 1)
                    elif lv == 1:
                        pe.wait_ge(q_f, hh + 1)
                    else:
                        pe.wait_ge(qa_up, 2 * (lv - 2) + hh + 1)
                        pe.wait_ge(kb_up, 2 * (lv - 2) + hh + 1)
                    for j in range(4):
                        h = 4 * hh + j
                        m = mm(ps[:, j * P:(j + 1) * P], kb[:, h, c * P:(c + 1) * P], qa[:, h, c * P:(c + 1) * P], j == 0, j == 3)
                elif kind == "cross":
                    hh = step[1]
                    lv = len(STEPS_L)
                    pe.wait_ge(qa_up, 2 * (lv - 2) + hh + 1)
                    pe.wait_ge(kb_up, 2 * (lv - 2) + hh + 1)
                    for j in range(4):
                        h = 4 * hh + j
                        m = mm(ps[:, j * P:(j + 1) * P], kb[:, h, 0:P], qa[:, h, P:2 * P], j == 0, j == 3)
                elif kind == "o":
                    _, c, hh = step
                    wait_taken(pe, ("lev", len(STEPS_L) - 1, hh, c))
                    if c == 1:
                        wait_taken(pe, ("cross", hh))
                    for j in range(4):
                        h = 4 * hh + j
                        o = ps[:, j * P:(j + 1) * P]
                        m = mm(o, attn[:, c, h], v_hg[:, c, h * P:(h + 1) * P], j == 0, c == 0 and j == 3)
                        if c == 1:
                            m = mm(o, attx[:, h], v_hg[:, 0, h * P:(h + 1) * P], False, j == 3)
                elif kind == "yT":
                    _, c, q = step
                    pe.wait_ge(o_norm, 2 * c + q + 1)
                    for j in range(4):
                        col = (4 * q + j) * P
                        m = nc.tensor.transpose(ps[:, j * P:(j + 1) * P], y_hg[:, c, col:col + P], ident[:])
                if last_of_bank:
                    m.then_inc(filled[b], 1)
                elif kind == "pv":
                    m.then_inc(pv_done, 1)

        HI_KEYS = [step for step, _ in SCHEDULE if step[0] in ("hT", "yT")]

        def squares(act, norm, t):
            unused = stg[:, 0].rearrange("p c q -> p (c q)") if norm == 0 else xn_1 if (norm, t) == (1, 0) else junk[:]
            nc.scalar.activation(unused, x[:, t], ACT.Square, accum_out=stat[:, norm, 0, t:t + 1]).then_inc(sumsq, 1)
            act.wait_ge(sumsq, TT * norm + t + 1)
            act.wait_ge(eps_set, 1)
            nc.scalar.activation(stat[:, norm, 1, t:t + 1], stat[:, norm, 0, t:t + 1], ACT.Sqrt,
                                 scale=1.0 / D, bias=eps_t[:]).then_inc(root, 1)

        @block.scalar
        def _(act):
            def split_hi(u, quarters=range(NQ)):
                if u >= 2:
                    wait_unit_used(act, u - 2)
                if u:
                    act.wait_ge(raw_in[u % NRAW], raw_count(u))
                for q in quarters:
                    if u == 0:
                        act.wait_ge(first_in[q], 16)
                    for dst, src, _ in split_parts(u, q):
                        m = nc.scalar.activation(dst, src, ACT.Copy)
                    m.then_inc(hi_done, 1)

            for t in range(TT):
                act.wait_ge(x_in[t], 16)
                if t:
                    act.wait_ge(root, t)
                squares(act, 0, t)
            split_hi(0, range(0, 2))

            for n, (step, _) in enumerate(SCHEDULE):
                kind, key = step[0], bank_key(step)
                if LAST[key] == n:
                    ps = bk(key)
                    if kind == "hT" or kind == "yT":
                        t, q = (step[2], step[3]) if kind == "hT" else (step[1], step[2])
                        wait_full(act, key)
                        nc.scalar.activation(h_hi[:, 4 * q:4 * q + 4, t * P:(t + 1) * P],
                                             ps[:].rearrange("p (k s) -> p k s", k=4), ACT.Copy).then_inc(taken_hi, 1)
                        if step == ("hT", 0, 1, 1):
                            split_hi(0, range(2, NQ))
                            act.wait_ge(ident_in, 16)
                            nc.scalar.activation(ident_r[:], ident[:], ACT.Copy).then_inc(idents, 1)
                            nc.scalar.activation(ident_b[:], ident[:], ACT.Copy).then_inc(idents, 1)
                            split_hi(1)
                            act.wait_ge(wg_in, 16)
                            nc.scalar.activation(wg_hi[:], wg[:], ACT.Copy).then_inc(wg_hi_d, 1)
                            act.wait_ge(const_in, 16 * N_CONST)
                            nc.scalar.activation(tri_b[:], tri, ACT.Copy).then_inc(idents, 1)
                            nc.scalar.activation(l_mask[:].rearrange("p l q -> p (l q)"), l_land, ACT.Copy).then_inc(idents, 1)
                    elif kind == "pa" and step[1] in (U_KS, U_KW, U_Q0, U_Q1):
                        j = STAGE.index(step[1:3])
                        if j >= 2:
                            wait_full(act, ("stage", j - 2, 1))
                        act.wait_ge(r_sum, j + 1)
                        if step[1] in (U_KS, U_KW):
                            nc.scalar.activation(stg[:, j % 2, 0:4].rearrange("p g (u d) -> p g u d", u=2),
                                                 bc(rp[:, 2, 0:G * HD].rearrange("p (g d) -> p g d", d=HD), 2, 2), ACT.Copy).then_inc(r_hi, 1)
                        else:
                            nc.scalar.activation(stg[:, j % 2, :, 0:HD], rp[:, 2].rearrange("p (h d) -> p h d", d=HD), ACT.Copy).then_inc(r_hi, 1)
                    elif kind == "stage":
                        _, j, half = step
                        u, t = STAGE[j]
                        wait_full(act, key)
                        if u in (U_KS, U_KW):
                            dst = k2[:, half, (U_KS, U_KW).index(u), :, t * P:(t + 1) * P]
                        else:
                            h0 = 8 * (u - U_Q0) + 4 * half
                            dst = q2[:, h0:h0 + 4, t * P:(t + 1) * P]
                        nc.scalar.activation(dst, ps[:].rearrange("p (k s) -> p k s", k=4), ACT.Copy).then_inc(taken(key), 1)
                    elif kind == "cmp1":
                        if step[1]:
                            wait_full(act, ("cmpT", 0))
                        wait_full(act, key)
                        nc.scalar.activation(hid[:], ps[0:G * CS, 0:CH], ACT.Silu).then_inc(taken(key), 1)
                        if step[1] == 0:
                            load_w1(act, "v")
                    elif kind == "cmpT":
                        act.wait_ge(zeros, 3)
                        wait_full(act, key)
                        nc.scalar.activation(hidT[:, step[1]].rearrange("p c (g n) -> p (c g) n", g=G)[:, :, 0:CS],
                                             ps[:, 0:2 * HD].rearrange("p (c n) -> p c n", n=CS), ACT.Copy).then_inc(taken(key), 1)
                    elif kind == "gl":
                        wait_full(act, key)
                        nc.scalar.activation(gT[:], ps[0:48, 0:S], ACT.Sigmoid).then_inc(taken(key), 1)
                    elif kind == "glT":
                        wait_full(act, key)
                        nc.scalar.activation(gate[:], ps[:, 0:TT * 48].rearrange("p (t c) -> p t c", t=TT), ACT.Copy).then_inc(taken(key), 1)
                    elif kind == "kcT":
                        act.wait_ge(zeros, 3)
                        wait_full(act, key)
                        for part in range(2):
                            for g in range(G):
                                m = nc.scalar.activation(kc_pad[:, part, g, g * NP_:(g + 1) * NP_],
                                                         ps[:, part * P + g * NP_:part * P + (g + 1) * NP_], ACT.Copy)
                                if part == 1 and g == G - 1:
                                    m.then_inc(taken(key), 1)
                    elif kind == "sc":
                        wait_full(act, key)
                        nc.scalar.activation(s_ct, ps[:], ACT.Copy).then_inc(taken(key), 1)
                        if step[1] == 0:
                            act.wait_ge(lb_v, 1)
                            nc.scalar.activation(lb[:, 1:3], lb[:, 1:3], ACT.Exp).then_inc(lb_e, 1)
                    elif kind == "scT":
                        act.wait_ge(cmp_v, step[1] + 1)
                        nc.scalar.activation(s_c[:, step[1]], s_c[:, step[1]], ACT.Exp).then_inc(cmp_exp, 1)
                    elif kind == "pcT":
                        wait_full(act, key)
                        nc.scalar.activation(p_ct[:, step[1]], ps[:], ACT.Copy).then_inc(taken(key), 1)
                    elif kind == "s":
                        it = step[1]
                        i = ITEMS[it][0]
                        if it >= NS + 1:
                            wait_full(act, ("pt", it - NS - 1))
                        act.wait_ge(rowmax, it + 1)
                        nb = 4 if i == 0 else 2
                        w = 512 // nb
                        for c in range(nb):
                            m = nc.scalar.activation(prob[:, it % (NS + 1), c * w:(c + 1) * w], ps[:, c * w:(c + 1) * w], ACT.Exp,
                                                     bias=nmax[:, it, c:c + 1], accum_out=rsum[:, it, c:c + 1])
                        m.then_inc(taken(key), 1)
                    elif kind == "pb" and step[1] in (U_Z0, U_Z1):
                        u, m2 = step[1], step[2]
                        if u == U_Z0 and m2 == 0:
                            wait_full(act, ("hT", 0, 1, 1))
                        wait_full(act, key)
                        r0 = 4 * (u - U_Z0) + 2 * m2
                        z_rows = lambda r: zT[:, r:r + 2].rearrange("p k s -> p (k s)")
                        held = u == U_Z1 and m2 == 0
                        nc.scalar.activation(z_rows(r0), ps[:], ACT.Copy if held else ACT.Silu).then_inc(taken(key), 1)
                        if u == U_Z1 and m2 == 1:
                            wait_taken(act, ("pb", U_Z1, 0))
                            nc.scalar.activation(z_rows(r0 - 2), z_rows(r0 - 2), ACT.Silu).then_inc(z_silu, 1)
                    elif kind == "pa" and step[1] in (V_V0, V_V1):
                        u, t = step[1], step[2]
                        wait_full(act, key)
                        nc.scalar.activation(v_hg[:, t, (u - V_V0) * UW:(u - V_V0 + 1) * UW], ps[:], ACT.Copy).then_inc(taken(key), 1)
                    elif kind == "pb" and step[1] in (V_F0, V_F1, V_Q0, V_Q1):
                        u, m2 = step[1], step[2]
                        is_f = u in (V_F0, V_F1)
                        h0 = 4 * (u in (V_F1, V_Q1)) + 2 * m2
                        wait_full(act, key)
                        nc.scalar.activation((fg if is_f else qa)[:, h0:h0 + 2], ps[:].rearrange("p (k s) -> p k s", k=2),
                                             ACT.Sigmoid if is_f else ACT.Silu).then_inc(taken(key), 1)
                    elif kind == "pa" and step[1] in (V_Z0, V_Z1):
                        u, t = step[1], step[2]
                        wait_full(act, key)
                        nc.scalar.activation(z_hg[:, t, (u - V_Z0) * UW:(u - V_Z0 + 1) * UW], ps[:], ACT.Silu).then_inc(taken(key), 1)
                    elif kind == "o":
                        _, c, hh = step
                        o = 2 * c + hh
                        wait_full(act, key)
                        sq = fg[:].rearrange("p h s -> p (h s)")[:, o * 512:(o + 1) * 512]
                        nc.scalar.activation(sq, ps[:], ACT.Square).then_inc(o_sq, 1)
                        act.wait_ge(o_sum, o + 1)
                        nc.scalar.activation(ostat[:, o, 1], ostat[:, o, 0], ACT.Sqrt, scale=1.0 / P, bias=eps_t[:]).then_inc(o_root, 1)
                    elif kind == "pv":
                        i, gp = JOBS[key[1]]
                        half = (slice(None), slice(4 * gp, 4 * gp + 4), slice(i * P, (i + 1) * P))
                        wait_taken(act, key)
                        nc.scalar.activation(h_hi[half], oT[half], ACT.Copy).then_inc(y_hi, 1)
                    if key == ("pa", U_O1, 0):
                        wait_residual(act, U_O0, 0)
                        squares(act, 1, 0)
                        act.wait_ge(y_lo, 4)
                    if key == ("pa", U_O1, 1):
                        act.wait_ge(root, TT + 1)
                        wait_residual(act, U_O0, 1)
                        squares(act, 1, 1)
                    if kind == "pa" and step[1] == V_O1:
                        t = step[2]
                        act.wait_ge(root, 2 * TT + t)
                        wait_residual(act, V_O0, t)
                        squares(act, 2, t)
                for u, q in SPLIT_AT.get(n, []):
                    split_hi(u, [q])

        @block.vector
        def _(dve):
            steps = [0]

            def step_(ins):
                ins.then_inc(vec_step, 1)
                steps[0] += 1

            def settled():
                dve.wait_ge(vec_step, steps[0])

            V = nc.vector

            def split_lo(u, quarters=range(NQ)):
                for q in quarters:
                    dve.wait_ge(hi_done, NQ * u + q + 1)
                    for hi, src, lo in split_parts(u, q):
                        m = V.tensor_tensor(lo, src, hi.bitcast(F32), ALU.subtract)
                    m.then_inc(lo_done, 1)

            def norm(nrm, t, dst, g_n, sig):
                dve.wait_ge(root, TT * nrm + t + 1)
                V.reciprocal(stat[:, nrm, 2, t:t + 1], stat[:, nrm, 1, t:t + 1]).then_inc(rstd, 1)
                dve.wait_ge(rstd, TT * nrm + t + 1)
                dve.wait_ge(g_in[g_n], 16)
                V.scalar_tensor_tensor(dst, x[:, t], stat[:, nrm, 2, t:t + 1], g_row[:], ALU.mult, ALU.mult).then_inc(sig, 1)

            def item_scale(it):
                i, gp, g, rp_, br = ITEMS[it]
                nb = 4 if i == 0 else 2
                wait_taken(dve, ("s", it))
                V.reciprocal(rrec[:, it, 0:nb], rsum[:, it, 0:nb]).then_inc(recip_d, 1)
                dve.wait_ge(recip_d, it + 1)
                h0 = g * R + 2 * rp_
                gv = gate[:, i].rearrange("p (h b) -> p h b", b=3)[:, h0:h0 + 2]
                if i == 0:
                    V.tensor_tensor(scl[:, it].rearrange("p (r b) -> p r b", r=2), rrec[:, it].rearrange("p (r b) -> p r b", r=2),
                                    gv[:, :, 1:3], ALU.mult).then_inc(scale_d, 1)
                else:
                    V.tensor_tensor(scl[:, it, 0:2], rrec[:, it, 0:2], gv[:, :, 1 + br], ALU.mult).then_inc(scale_d, 1)

            V.memset(eps_t[:], EPS).then_inc(eps_set, 1)
            for t in range(TT):
                norm(0, t, xn[:, t], 0, normed)
            split_lo(0, range(0, 2))
            for n, (step, _) in enumerate(SCHEDULE):
                kind, key = step[0], bank_key(step)
                if LAST[key] == n:
                    ps = bk(key)
                    if kind == "hT" or kind == "yT":
                        t, q = (step[2], step[3]) if kind == "hT" else (step[1], step[2])
                        dve.wait_ge(taken_hi, HI_KEYS.index(step) + 1)
                        hs = (slice(None), slice(4 * q, 4 * q + 4), slice(t * P, (t + 1) * P))
                        V.tensor_tensor(h_lo[hs], ps[:].rearrange("p (k s) -> p k s", k=4), h_hi[hs].bitcast(F32),
                                        ALU.subtract).then_inc(taken(key), 1)
                        if step == ("hT", 0, 1, 1):
                            V.memset(flat[HD:P, :, :, :, NC:CS], 0.0).then_inc(flat_zero, 1)
                            split_lo(0, range(2, NQ))
                            split_lo(1)
                            dve.wait_ge(wg_hi_d, 1)
                            V.tensor_tensor(wg_lo[:], wg[:], wg_hi[:].bitcast(F32), ALU.subtract).then_inc(wg_lo_d, 1)
                            dve.wait_ge(const_in, 16 * N_CONST)
                            step_(V.tensor_tensor(lb[:, 0], lbl[:, 0], lbl[:, 1], ALU.max))
                            settled()
                            V.tensor_tensor(lb[:, 1:3], lbl[:], bc(lb[:, 0], 2, 1), ALU.subtract).then_inc(lb_v, 1)
                    elif kind == "pa" and step[1] in (U_KS, U_KW, U_Q0, U_Q1):
                        u, t = step[1], step[2]
                        j = STAGE.index((u, t))
                        is_k = u in (U_KS, U_KW)
                        nh = G if is_k else 8
                        if j == 0:
                            dve.wait_ge(const_in, 16 * N_CONST)
                        else:
                            dve.wait_ge(r_sum, j)
                        wait_full(dve, key)
                        xin = ps[:, 0:nh * HD].rearrange("p (h d) -> p h d", d=HD)
                        a = rp[:, 0, 0:nh * HD].rearrange("p (h d) -> p h d", d=HD)
                        b_ = rp[:, 1, 0:nh * HD].rearrange("p (h d) -> p h d", d=HD)
                        co, si = (rope[:, 2, t], rope[:, 3, t]) if is_k else (rope[:, 0, t], rope[:, 1, t])
                        hf = HD // 2
                        V.tensor_tensor(a, xin, bc(co, nh, 1), ALU.mult)
                        V.tensor_tensor(b_[:, :, 0:hf], xin[:, :, hf:HD], bc(si[:, 0:hf], nh, 1), ALU.mult)
                        if is_k:
                            V.tensor_tensor(b_[:, :, hf:HD], xin[:, :, 0:hf], bc(si[:, hf:HD], nh, 1), ALU.mult).then_inc(r_ab, 1)
                            dve.wait_ge(idents, 4)
                            V.tensor_copy(v_tok[:, t, (U_KS, U_KW).index(u)].rearrange("p g d -> p (g d)"), ps[:, G * HD:UW]).then_inc(taken(key), 1)
                        else:
                            V.tensor_tensor(b_[:, :, hf:HD], xin[:, :, 0:hf], bc(si[:, hf:HD], nh, 1), ALU.mult).then_inc(taken(key), 1)
                    elif key[0:2] == ("pb", U_KC):
                        kv = step[2]
                        wait_full(dve, key)
                        for g in range(G):
                            src = ps[(g % 2) * HD:(g % 2 + 1) * HD, (g // 2) * S:(g // 2 + 1) * S].rearrange("p (n j) -> p j n", j=CS)
                            V.tensor_tensor(flat[0:HD, kv, :, g], src, bc(pe_t[0:HD, kv], CS, 2), ALU.add)
                            m = V.tensor_tensor(flat[HD:P, kv, :, g, 0:NC], src[:, :, 1:CS], bc(pe_t[HD:P, kv], NC, 2), ALU.add)
                        m.then_inc(taken(key), 1)
                    elif kind == "cmp2" and step[1] == 0:
                        wait_full(dve, key)
                        hf = HD // 2
                        dve.wait_ge(idents, 3)
                        step_(V.tensor_tensor(kcr[:, 0], ps[:, 0:HD], rope_c[:, 0], ALU.mult))
                        step_(V.tensor_tensor(kcr[:, 1, 0:hf], ps[:, hf:HD], rope_c[:, 1, 0:hf], ALU.mult))
                        V.tensor_tensor(kcr[:, 1, hf:HD], ps[:, 0:hf], rope_c[:, 1, hf:HD], ALU.mult).then_inc(taken(key), 1)
                        wait_taken(dve, key)
                        step_(V.tensor_tensor(kcr[:, 2], kcr[:, 0], kcr[:, 1], ALU.add))
                        settled()
                        hi2 = kcs[:, 0].rearrange("p (u d) -> p u d", u=2)
                        lo2 = kcs[:, 1].rearrange("p (u d) -> p u d", u=2)
                        step_(V.tensor_copy(hi2, bc(kcr[:, 2], 2, 1)))
                        settled()
                        V.tensor_tensor(lo2, bc(kcr[:, 2], 2, 1), hi2.bitcast(F32), ALU.subtract).then_inc(kc_v, 1)
                    elif kind == "cmp2":
                        dve.wait_ge(zeros, 3)
                        wait_full(dve, key)
                        for g in range(G):
                            m = V.tensor_copy(vc_bd[g * NP_:(g + 1) * NP_, g // 2, (g % 2) * HD:(g % 2 + 1) * HD],
                                              ps[g * NP_:(g + 1) * NP_, 0:HD])
                        m.then_inc(taken(key), 1)
                    elif kind == "glT":
                        wait_taken(dve, key)
                        gc = gate[:].rearrange("p t (h b) -> p t h b", b=3)[:, :, :, 0]
                        V.tensor_tensor(gc, gc, bc(c_valid[:], H, 2), ALU.mult).then_inc(gate_v, 1)
                    elif kind == "scT":
                        i = step[1]
                        sc = s_c[:, i].rearrange("p (a n) -> p a n", n=NP_)
                        wait_full(dve, key)
                        V.tensor_tensor(sc, ps[:].rearrange("p (a n) -> p a n", n=NP_), bc(c_mask[:, i], H, 1), ALU.add).then_inc(taken(key), 1)
                        wait_taken(dve, key)
                        step_(V.tensor_reduce(cst[:, i, 0], sc, AX.X, ALU.max, negate=True))
                        settled()
                        V.tensor_tensor(sc, sc, bc(cst[:, i, 0], NP_, 2), ALU.add).then_inc(cmp_v, 1)
                        dve.wait_ge(cmp_exp, i + 1)
                        step_(V.tensor_reduce(cst[:, i, 1], sc, AX.X, ALU.add))
                        settled()
                        step_(V.reciprocal(cst[:, i, 2], cst[:, i, 1]))
                        settled()
                        dve.wait_ge(gate_v, 1)
                        gc = gate[:, i].rearrange("p (g r b) -> p r g b", g=G, b=3)[:, :, :, 0]
                        step_(V.tensor_tensor(cst[:, i, 0].rearrange("p (r g) -> p r g", g=G),
                                              cst[:, i, 2].rearrange("p (r g) -> p r g", g=G), gc, ALU.mult))
                        settled()
                        V.tensor_tensor(sc, sc, bc(cst[:, i, 0], NP_, 2), ALU.mult).then_inc(cmp_scaled, 1)
                        if i == 1:
                            dve.wait_ge(lb_e, 1)
                            for ins in (lambda: V.tensor_tensor(lb[:, 0], lb[:, 1], lb[:, 2], ALU.add),
                                        lambda: V.reciprocal(lb[:, 3], lb[:, 0]),
                                        lambda: V.tensor_tensor(lb[:, 1:3], lb[:, 1:3], bc(lb[:, 3], 2, 1), ALU.mult),
                                        lambda: V.tensor_tensor(lb[:, 3], lb[:, 1], lb[:, 2], ALU.add),
                                        lambda: V.tensor_tensor(lb[:, 4], lb[:, 3], lb[:, 1], ALU.subtract),
                                        lambda: V.tensor_scalar(lb[:, 5], lb[:, 4], -1.0, 1.0, ALU.mult, ALU.add)):
                                step_(ins())
                                settled()
                    elif kind == "s":
                        it = step[1]
                        nb = 4 if ITEMS[it][0] == 0 else 2
                        wait_full(dve, key)
                        V.tensor_reduce(nmax[:, it, 0:nb], ps[:].rearrange("p (a b) -> p a b", a=nb), AX.X, ALU.max,
                                        negate=True).then_inc(rowmax, 1)
                        if it >= 1:
                            item_scale(it - 1)
                    elif kind == "pt":
                        it = step[1]
                        if it == NI - NS:
                            item_scale(NI - 1)
                        if it >= 2:
                            wait_pv(dve, it - 2)
                        wait_full(dve, key)
                        V.tensor_copy(prob_t[:, it % 2], ps[:]).then_inc(taken(key), 1)
                    elif kind == "pv":
                        job = key[1]
                        i, gp = JOBS[job]
                        half = (slice(None), slice(4 * gp, 4 * gp + 4), slice(i * P, (i + 1) * P))
                        wait_full(dve, key)
                        dve.wait_ge(z_silu, 1)
                        for m2 in range(2):
                            wait_taken(dve, ("pb", U_Z1, m2))
                        V.tensor_tensor(oT[half], ps[:].rearrange("p (k s) -> p k s", k=4), zT[half], ALU.mult).then_inc(taken(key), 1)
                        dve.wait_ge(y_hi, job + 1)
                        V.tensor_tensor(h_lo[half], oT[half], h_hi[half].bitcast(F32), ALU.subtract).then_inc(y_lo, 1)
                    elif kind == "pa" and step[1] in (U_O0, U_O1, V_O0, V_O1):
                        u, t = step[1], step[2]
                        c = (u - (U_O0 if u <= U_O1 else V_O0)) * UW
                        wait_full(dve, key)
                        V.tensor_tensor(x[:, t, c:c + UW], x[:, t, c:c + UW], ps[:], ALU.add).then_inc(taken(key), 1)
                    elif kind == "pb" and step[1] in (V_F0, V_F1) and step[2] == 1:
                        hh = int(step[1] == V_F1)
                        for m2 in range(2):
                            wait_taken(dve, ("pb", step[1], m2))
                        for h in range(4 * hh, 4 * hh + 4):
                            m = V.tensor_scalar(fg[:, h], fg[:, h], lb[:, 5, h:h + 1], lb[:, 4, h:h + 1], ALU.mult, ALU.add)
                        m.then_inc(f_lin, 1)
                        dve.wait_ge(f_lin, hh + 1)
                        V.tensor_scalar(kb[:, 4 * hh:4 * hh + 4], fg[:, 4 * hh:4 * hh + 4], -1.0, 1.0, ALU.mult, ALU.add).then_inc(k_lin, 1)
                    elif kind == "lev":
                        _, lv, hh, c = step
                        dst = attn[:, c, 4 * hh:4 * hh + 4]
                        src = ps[:].rearrange("p (h t) -> p h t", h=4)
                        wait_full(dve, key)
                        if lv == 0:
                            V.tensor_tensor(dst, src, bc(ident[:], 4, 1), ALU.mult).then_inc(taken(key), 1)
                        else:
                            s = LEVELS[lv - 1]
                            cut = lambda ap: ap.rearrange("p h (b u s) -> p h b u s", u=2, s=s)[:, :, :, 1]
                            dve.wait_ge(idents, 4)
                            V.copy_predicated(cut(dst), cut(bc(l_mask[:, lv - 1], 4, 1)), cut(src)).then_inc(taken(key), 1)
                        if c == 1:
                            hs = slice(4 * hh, 4 * hh + 4)
                            if lv == 0:
                                V.tensor_tensor(qa[:, hs], qa[:, hs], fg[:, hs], ALU.mult).then_inc(q_f, 1)
                            else:
                                half = qa[:, hs].rearrange("p h (b u s) -> p h b u s", u=2, s=s)[:, :, :, 1]
                                if lv == 1:
                                    dve.wait_ge(q_f, hh + 1)
                                else:
                                    dve.wait_ge(qa_up, 2 * (lv - 2) + hh + 1)
                                    dve.wait_ge(ft_up, 7 * hh + lv - 1)
                                V.tensor_tensor(half, half, bc(totals(s, hh)[:, :, :, 0], s, 3), ALU.mult).then_inc(qa_up, 1)
                    elif kind == "cross":
                        hh = step[1]
                        wait_full(dve, key)
                        V.tensor_copy(attx[:, 4 * hh:4 * hh + 4], ps[:].rearrange("p (h t) -> p h t", h=4)).then_inc(taken(key), 1)
                    elif kind == "o":
                        _, c, hh = step
                        o = 2 * c + hh
                        ys = y_hg[:, c, hh * UW:(hh + 1) * UW]
                        sq = fg[:].rearrange("p h s -> p (h s)")[:, o * 512:(o + 1) * 512]
                        dve.wait_ge(o_sq, o + 1)
                        V.tensor_reduce(ostat[:, o, 0], sq.rearrange("p (h v) -> p h v", h=4), AX.X, ALU.add).then_inc(o_sum, 1)
                        dve.wait_ge(z_g, Z_ORDER.index((V_Z0 + hh, c)) + 1)
                        V.tensor_tensor(ys, ps[:], z_hg[:, c, hh * UW:(hh + 1) * UW], ALU.mult).then_inc(taken(key), 1)
                        dve.wait_ge(o_root, o + 1)
                        V.reciprocal(ostat[:, o, 2], ostat[:, o, 1]).then_inc(o_rstd, 1)
                        dve.wait_ge(o_rstd, o + 1)
                        wait_taken(dve, key)
                        y4 = ys.rearrange("p (h v) -> p h v", h=4)
                        V.tensor_tensor(y4, y4, bc(ostat[:, o, 2], P, 2), ALU.mult).then_inc(o_norm, 1)
                    if key == ("pa", U_O1, 0):
                        norm(1, 0, xn_1, 2, normed)
                    if key == ("pa", U_O1, 1):
                        norm(1, 1, y_hg[:, 1], 2, normed)
                    if kind == "pa" and step[1] == V_O1:
                        norm(2, step[2], y_hg[:, step[2]], 3, done_row)
                for u, q in SPLIT_AT.get(n, []):
                    split_lo(u, [q])

        @block.gpsimd
        def _(pool):
            GP = nc.gpsimd
            row = lambda ap: ap.unsqueeze(0).broadcast_to([P, D])
            pool.dma_start(g_row[:], row(t_in["norm_w"][0])).then_inc(g_in[0], 16)
            GP.memset(hidT[:], 0.0).then_inc(zeros, 1)
            GP.memset(kc_pad[:].bitcast(F32), 0.0).then_inc(zeros, 1)
            GP.memset(vc_bd[:], 0.0).then_inc(zeros, 1)
            pool.wait_ge(normed, TT)
            pool.dma_start(g_row[:], row(t_in["norm_w"][1])).then_inc(g_in[2], 16)

            for n, (step, _) in enumerate(SCHEDULE):
                kind, key = step[0], bank_key(step)
                if LAST[key] == n:
                    if kind == "pa" and step[1] in (U_KS, U_KW, U_Q0, U_Q1):
                        u, t = step[1], step[2]
                        j = STAGE.index((u, t))
                        is_k = u in (U_KS, U_KW)
                        w = (G if is_k else 8) * HD
                        if is_k:
                            pool.wait_ge(r_ab, j + 1)
                        else:
                            wait_taken(pool, key)
                        if j:
                            pool.wait_ge(r_lo, j)
                        GP.tensor_tensor(rp[:, 2, 0:w], rp[:, 0, 0:w], rp[:, 1, 0:w], ALU.add).then_inc(r_sum, 1)
                        pool.wait_ge(r_hi, j + 1)
                        if is_k:
                            v = lambda ap: ap.rearrange("p g (u d) -> p g u d", u=2)
                            GP.tensor_tensor(v(stg[:, j % 2, 4:8]), bc(rp[:, 2, 0:w].rearrange("p (g d) -> p g d", d=HD), 2, 2),
                                             v(stg[:, j % 2, 0:4]).bitcast(F32), ALU.subtract).then_inc(r_lo, 1)
                        else:
                            GP.tensor_tensor(stg[:, j % 2, :, HD:P], rp[:, 2].rearrange("p (h d) -> p h d", d=HD),
                                             stg[:, j % 2, :, 0:HD].bitcast(F32), ALU.subtract).then_inc(r_lo, 1)
                    elif kind == "pt":
                        it = step[1]
                        if it == 0:
                            for first in range(NS):
                                scale_item(pool, first)
                        if it + NS < NI:
                            scale_item(pool, it + NS)
                    elif kind == "pb" and step[1] in (V_F0, V_F1) and step[2] == 1:
                        hh = int(step[1] == V_F1)
                        pool.wait_ge(f_lin, hh + 1)
                        for lv, s in enumerate(LEVELS):
                            if lv:
                                pool.wait_ge(ft_up, 7 * hh + lv)
                            tt = totals(s, hh)
                            GP.tensor_tensor(level_totals(2 * s, hh), tt[:, :, :, 0], tt[:, :, :, 1], ALU.mult).then_inc(ft_up, 1)
                    elif kind == "lev" and step[1] >= 1 and step[3] == 1:
                        _, lv, hh, c = step
                        s = LEVELS[lv - 1]
                        wait_full(pool, key)
                        if lv == 1:
                            pool.wait_ge(k_lin, hh + 1)
                            pool.wait_ge(f_lin, hh + 1)
                        else:
                            pool.wait_ge(kb_up, 2 * (lv - 2) + hh + 1)
                            pool.wait_ge(ft_up, 7 * hh + lv - 1)
                        half = kb[:, 4 * hh:4 * hh + 4].rearrange("p h (b u s) -> p h b u s", u=2, s=s)[:, :, :, 0]
                        GP.tensor_tensor(half, half, bc(totals(s, hh)[:, :, :, 1], s, 3), ALU.mult).then_inc(kb_up, 1)
                    elif kind == "pa" and step[1] in (V_Z0, V_Z1):
                        u, t = step[1], step[2]
                        wait_taken(pool, key)
                        pool.wait_ge(g_in[1], 16)
                        zs = z_hg[:, t, (u - V_Z0) * UW:(u - V_Z0 + 1) * UW]
                        GP.tensor_tensor(zs, zs, g_row[:, (u - V_Z0) * UW:(u - V_Z0 + 1) * UW], ALU.mult).then_inc(z_g, 1)
                        if u == V_Z1 and t == 1:
                            pool.wait_ge(z_g, 4)
                            pool.dma_start(g_row[:], row(t_in["final_norm"])).then_inc(g_in[3], 16)
                    if key == ("hT", 1, 1, 1):
                        pool.wait_ge(normed, 2 * TT)
                        pool.dma_start(g_row[:], row(t_in["hg_norm"])).then_inc(g_in[1], 16)


def shape_constants():
    f = np.float32
    half = HD // 2
    inv = (f(10000.0) ** (-np.arange(half, dtype=f) / f(half))).astype(f)

    def table(pos, scale):
        ang = pos.astype(f)[:, None] * inv[None, :]
        co, si = np.cos(ang), np.sin(ang)
        return np.concatenate([co, co], 1) * f(scale), np.concatenate([-si, si], 1) * f(scale)

    pos = np.arange(S)
    q, k = table(pos, HD ** -0.5), table(pos, 1.0)
    rope = np.stack([q[0], q[1], k[0], k[1]]).astype(f)
    rope = rope.reshape(4, TT, P, HD).transpose(2, 0, 1, 3)
    end = np.arange(NP_) * CS + CB - 1
    c = table(end, 1.0)
    rope_c = np.tile(np.stack(c, 1), (G, 1, 1)).astype(f)
    seen = (end[None, :] <= pos[:, None]) & (np.arange(NP_) < NC)[None, :]
    c_mask = np.where(seen, 0.0, NEG).astype(f).reshape(TT, P, NP_).transpose(1, 0, 2)
    c_valid = seen.any(1).astype(f).reshape(TT, P).T
    a = np.arange(P)
    tri = np.where(a[None, :] <= a[:, None], 0.0, NEG).astype(f)
    lm = np.stack([(a[:, None] // (2 * s) == a[None, :] // (2 * s)) & (a[:, None] // s % 2 == 0) & (a[None, :] // s % 2 == 1)
                   for s in LEVELS], 1).astype(f)
    return {"c_ident": np.eye(P, dtype=f), "c_rope": rope, "c_rope_c": rope_c, "c_mask": c_mask, "c_valid": c_valid,
            "c_tri": tri, "c_levels": lm}


def kernel(x, norm_w, nsa_w_in, nsa_pe_k, nsa_pe_v, nsa_wk1, nsa_wk2, nsa_wv1, nsa_wv2, nsa_w_out,
           hg_w_in, hg_lb_logits, hg_norm, hg_w_out, final_norm):
    import concourse.bacc as bacc
    from concourse.bass_utils import run_bass_kernel_spmd

    lay = np.ascontiguousarray
    pe_of = lambda pe: np.asarray(pe)[0].reshape(2, CS, HD).transpose(0, 2, 1).reshape(P, CS)
    arrays = {
        "x": np.asarray(x)[0], "norm_w": norm_w, "nsa": np.asarray(nsa_w_in)[0], "nsa_out": np.asarray(nsa_w_out)[0],
        "hg": np.asarray(hg_w_in)[0], "hg_out": np.asarray(hg_w_out)[0],
        "w1k": np.asarray(nsa_wk1)[0], "w1v": np.asarray(nsa_wv1)[0],
        "w2k": np.asarray(nsa_wk2)[0], "w2v": np.asarray(nsa_wv2)[0],
        "pe": np.stack([pe_of(nsa_pe_k), pe_of(nsa_pe_v)], 1),
        "lb": np.asarray(hg_lb_logits).reshape(2, HH, P).transpose(2, 0, 1),
        "hg_norm": np.asarray(hg_norm)[0], "final_norm": final_norm,
    } | shape_constants()
    arrays = {f"in_{k}": lay(v) for k, v in arrays.items()}
    nc = bacc.Bacc("TRN2", target_bir_lowering=False, num_devices=1)
    t_in = {k[3:]: nc.dram_tensor(k, v.shape, mybir.dt.from_np(v.dtype), kind="ExternalInput").ap() for k, v in arrays.items()}
    t_in["ident"] = t_in["c_ident"]
    out = nc.dram_tensor("out", (S, D), F32, kind="ExternalOutput").ap()
    program(nc, t_in, out)
    got = run_bass_kernel_spmd(nc, [arrays], core_ids=[0])
    return got.results[0]["out"].reshape(1, S, D)
```

```python
from contextlib import ExitStack

import numpy as np

import concourse.bass as bass
from concourse import mybir

P = 128
D = 1024
S = 256
KT = D // P
TT = S // P
UW = 512
H, G, R, HD = 16, 4, 4, 64
CB, CS, NC, NP_ = 32, 16, 15, 32
CH = 256
HH = 8
EPS = 1e-6
NEG = -1e30
NQ = 4
IDLE = (7, 6)
LEVELS = [1, 2, 4, 8, 16, 32, 64]

F32 = mybir.dt.float32
FR = mybir.dt.float32r
BF16 = mybir.dt.bfloat16
U8 = mybir.dt.uint8
ALU = mybir.AluOpType
ACT = mybir.ActivationFunctionType
AX = mybir.AxisListType

NSA_Q, NSA_KC, NSA_KS, NSA_KW, NSA_GL, NSA_Z = 0, 1024, 1536, 2048, 2560, 2608
UNITS = [("nsa", NSA_KS), ("nsa", NSA_KC), ("nsa", NSA_KW), ("nsa", NSA_Q), ("nsa", NSA_Q + UW),
         ("nsa", NSA_Z), ("nsa", NSA_Z + UW), ("nsa_out", 0), ("nsa_out", UW),
         ("hg", 2048), ("hg", 2560), ("hg", 1024), ("hg", 0), ("hg", 1536), ("hg", 512),
         ("hg", 3072), ("hg", 3584), ("hg_out", 0), ("hg_out", UW)]
U_KS, U_KC, U_KW, U_Q0, U_Q1, U_Z0, U_Z1, U_O0, U_O1 = range(9)
V_V0, V_V1, V_F0, V_Q0, V_F1, V_Q1, V_Z0, V_Z1, V_O0, V_O1 = range(9, 19)
NRAW = 2
NS = 3

ITEMS = [(0, gp, 2 * gp + g2, rp, None) for gp in range(2) for g2 in range(2) for rp in range(2)]
ITEMS += [(1, gp, 2 * gp + g2, rp, b) for gp in range(2) for g2 in range(2) for rp in range(2)
          for b in range(2)]
NI = len(ITEMS)
JOBS = [(i, gp) for i in range(2) for gp in range(2)]
ITEM_JOB = [JOBS.index((it[0], it[1])) for it in ITEMS]
JOB_LAST = [max(n for n in range(NI) if ITEM_JOB[n] == j) for j in range(4)]
Z_ORDER = [(V_Z0, 0), (V_Z1, 0), (V_Z0, 1), (V_Z1, 1)]
STEPS_L = ["diag"] + LEVELS

BEFORE = (3, 3, 2, 0, 0, 0, 5, 0, 3)
AMONG = (13, 15, 16, 21, 22, 23)
ACT_TURNS = (6, 8, 9, 10, 12, 14, 16, 17, 18, 19, 20, 21)


def schedule():
    out = []

    def add(*step, banks=()):
        out.append((step, tuple(banks)))

    def pa(u, t, bank, slices=range(4)):
        for sl in slices:
            add("pa", u, t, sl, banks=(bank,))

    def pb(u, m2, bank, slices=range(4)):
        for sl in slices:
            add("pb", u, m2, sl, banks=(bank,))

    def stage(j):
        for half in range(2):
            add("stage", j, half, banks=(4 + half,))

    add("idle", 0)
    for q in range(2):
        add("hT", 0, 0, q, banks=(4 + q,))
    add("idle", 1)
    pa(U_KS, 0, 2, range(0, 2))
    for q in range(2):
        add("hT", 0, 1, q, banks=(6 + q,))
    pa(U_KS, 0, 2, range(2, 4))
    pa(U_KS, 1, 3)
    pb(U_KC, 0, 0)
    pb(U_KC, 1, 1)
    stage(0)
    add("cmp1", 0, banks=(6,))
    pa(U_KW, 0, 0)
    stage(1)
    add("gl", banks=(7,))
    add("cmpT", 0, banks=(6,))
    pa(U_KW, 1, 1)
    stage(2)
    add("glT", banks=(7,))
    add("cmp2", 0, banks=(6,))
    pa(U_Q0, 0, 2)
    stage(3)
    add("cmp1", 1, banks=(6,))
    pa(U_Q0, 1, 3)
    add("kcT", banks=(7,))
    stage(4)
    add("cmpT", 1, banks=(6,))
    pa(U_Q1, 0, 0)
    stage(5)
    pa(U_Q1, 1, 1)
    z = [(u, m2, sl) for u in (U_Z0, U_Z1) for m2 in range(2) for sl in range(4)]
    fill = [(("pb",) + s, 2 + s[1]) for s in z]
    fill += [(("pa", u, 0, sl), 2 + (u - U_O0)) for u in (U_O0, U_O1) for sl in range(4)]

    def filler(n):
        for _ in range(n):
            if fill:
                step, bank = fill.pop(0)
                add(*step, banks=(bank,))

    filler(BEFORE[0])
    stage(6)
    filler(BEFORE[1])
    stage(7)
    filler(BEFORE[2])
    add("cmp2", 1, banks=(6,))
    add("sc", 0, banks=(7,))
    filler(BEFORE[3])
    add("scT", 0, banks=(7,))
    add("sc", 1, banks=(7,))
    filler(BEFORE[4])
    add("s", 0, banks=(4,))
    add("s", 1, banks=(5,))
    filler(BEFORE[5])
    add("scT", 1, banks=(7,))
    filler(BEFORE[6])
    add("pcT", 0, banks=(7,))
    add("s", 2, banks=(6,))
    filler(BEFORE[7])
    add("pcT", 1, banks=(1,))
    filler(BEFORE[8])
    for n in range(NI):
        add("pt", n, banks=(7,))
        if n + NS < NI:
            add("s", n + NS, banks=(4 + n % NS,))
        if n >= 1:
            add("pv", n - 1, banks=(ITEM_JOB[n - 1] % 2,))
        filler(AMONG.count(n))
    add("pv", NI - 1, banks=(ITEM_JOB[NI - 1] % 2,))
    filler(len(fill))
    pa(U_O0, 1, 4)
    pa(U_O1, 1, 5, range(0, 2))
    add("hT", 1, 0, 0, banks=(0,))
    add("hT", 1, 0, 1, banks=(1,))
    pa(U_O1, 1, 5, range(2, 4))
    pa(V_V0, 0, 2)
    pa(V_V1, 0, 3, range(0, 2))
    add("hT", 1, 1, 0, banks=(6,))
    add("hT", 1, 1, 1, banks=(7,))
    pa(V_V1, 0, 3, range(2, 4))
    pa(V_V0, 1, 0)
    pa(V_V1, 1, 1)
    for hh, (uf, uq) in enumerate(((V_F0, V_Q0), (V_F1, V_Q1))):
        pb(uf, 0, 2)
        pb(uf, 1, 3)
        pb(uq, 0, 0)
        pb(uq, 1, 1)
    zs = [(("pa", u, t, sl), 2 * (u - V_Z0) + t) for u, t in Z_ORDER for sl in range(4)]
    slot = 0
    for lv in range(len(STEPS_L)):
        for hh in range(2):
            for c in range(TT):
                add("lev", lv, hh, c, banks=(4 + 2 * hh + c,))
            if slot % 4 != 3:
                step, bank = zs.pop(0)
                add(*step, banks=(bank,))
            slot += 1
    for hh in range(2):
        add("cross", hh, banks=(4 + 2 * hh,))
        if hh == 0:
            step, bank = zs.pop(0)
            add(*step, banks=(bank,))
    for hh in range(2):
        add("o", 0, hh, banks=(hh,))
    for step, bank in zs:
        add(*step, banks=(bank,))
    for q in range(2):
        add("yT", 0, q, banks=(4 + q,))
    for hh in range(2):
        add("o", 1, hh, banks=(2 + hh,))
    pa(V_O0, 0, 0)
    pa(V_O1, 0, 1, range(0, 2))
    for q in range(2):
        add("yT", 1, q, banks=(6 + q,))
    pa(V_O1, 0, 1, range(2, 4))
    pa(V_O0, 1, 2)
    pa(V_O1, 1, 3)
    return out


def bank_key(step):
    if step[0] in ("pa", "pb"):
        return step[:3]
    if step[0] == "pv":
        return ("pv", ITEM_JOB[step[1]])
    return step


SCHEDULE = schedule()


def bank_uses():
    uses, filled, last = {}, [0] * 8, {}
    open_ = {}
    for n, (step, banks) in enumerate(SCHEDULE):
        for b in banks:
            key = bank_key(step)
            if key not in uses:
                uses[key] = (b, filled[b])
                filled[b] += 1
            assert uses[key][0] == b and (b not in open_ or open_[b] == key or filled[b] == uses[key][1] + 1), step
            assert filled[b] == uses[key][1] + 1, step
            open_[b] = key
            last[key] = n
    return uses, last


USES, LAST = bank_uses()
UNIT_FIRST, UNIT_LAST = {}, {}
for _n, (_step, _) in enumerate(SCHEDULE):
    if _step[0] in ("pa", "pb"):
        UNIT_FIRST.setdefault(_step[1], _n)
        UNIT_LAST[_step[1]] = _n


def split_places():
    places, before = ({}, {}), 0
    for u in range(2, len(UNITS)):
        free, used = UNIT_LAST[u - 2], UNIT_FIRST[u]
        for q in range(NQ):
            before = n = max(before, min(used - 1, free + SPREAD[u][q]))
            assert n < used
            places[0].setdefault(n, []).append((u, q))
            places[1].setdefault(min(used - 1, n + LAG), []).append((u, q))
    return places


SPREAD = {U_KW: (3, 3, 4, 5), U_Q0: (0, 2, 3, 3), U_Q1: (3, 3, 8, 13), U_Z0: (0, 6, 7, 7),
          U_Z1: (1, 2, 4, 11), U_O0: (12, 18, 32, 39), U_O1: (32, 38, 46, 54), V_V0: (0, 0, 0, 2),
          V_V1: (0, 0, 1, 1), V_F0: (0, 0, 0, 0), V_Q0: (0, 0, 1, 3), V_F1: (0, 4, 4, 5),
          V_Q1: (1, 2, 2, 4), V_Z0: (0, 0, 2, 3), V_Z1: (3, 4, 11, 23), V_O0: (0, 3, 5, 8),
          V_O1: (4, 5, 5, 6)}
GATED_LAG = 2
LAG = 2
SPLIT_HI_AT, SPLIT_LO_AT = split_places()


def program(nc, t_in, out):
    with ExitStack() as ctx:
        def sb(name, shape, dt=F32, scope=ctx):
            return scope.enter_context(nc.sbuf_tensor(name, shape, dt))

        raw = sb("raw", [P, NRAW, KT, UW])
        w_hi = sb("w_hi", [P, 2, KT, UW], FR)
        w_lo = sb("w_lo", [P, 2, KT, UW], FR)
        x = sb("x_res", [P, TT, D])
        h_hi = sb("h_hi", [P, KT, S], FR)
        h_lo = sb("h_lo", [P, KT, S], FR)
        g_row = sb("g_row", [P, D])
        ident = sb("ident", [P, P])
        ident_r = sb("ident_r", [P, P], FR)
        ident_b = sb("ident_b", [P, P], BF16)
        tri_b = sb("tri_b", [P, P], BF16)
        rope = sb("rope", [P, 4, TT, HD])
        rope_c = sb("rope_c", [P, 2, HD])
        c_mask = sb("c_mask", [P, TT, NP_])
        c_valid = sb("c_valid", [P, TT])
        l_mask = sb("l_mask", [P, len(LEVELS), P], U8)
        pe_t = sb("pe_t", [P, 2, CS])
        w2 = sb("w2", [P, 2, 2, HD])
        lbl = sb("lbl", [P, 2, HH])
        lb = sb("lb", [P, 6, HH])
        stat = sb("stat", [P, 3, 5, TT])
        eps_t = sb("eps_t", [P, 1])
        nmax = sb("nmax", [P, NI, 4])
        rsum = sb("rsum", [P, NI, 4])
        rrec = sb("rrec", [P, NI, 4])
        scl = sb("scl", [P, NI, 4])
        gate = sb("gate", [P, TT, 48])
        ostat = sb("ostat", [P, TT, 3, 8])

        nsa = ExitStack()
        cw = ExitStack()
        w1 = sb("w1", [P, CS, CH], F32, cw)
        cw.close()
        q2 = sb("q2", [P, H, S], FR, nsa)
        k2 = sb("k2", [P, 2, 2, G, S], FR, nsa)
        v_tok = sb("v_tok", [P, TT, 2, G, HD], F32, nsa)
        kc_pad = sb("kc_pad", [P, 2, G, P], FR, nsa)
        vc_bd = sb("vc_bd", [P, 2, P], F32, nsa)
        zT = sb("zT", [P, KT, S], F32, nsa)
        xn = zT[:].rearrange("p k s -> p (k s)").rearrange("p (t d) -> p t d", t=TT)
        flat = zT[:].rearrange("p k s -> p (k s)").rearrange("p (v j g n) -> p v j g n", v=2, j=CS, g=G)
        pre = ExitStack()
        stg = sb("stg", [P, 2, 8, P], FR, pre)
        rp = sb("rp", [P, 3, UW], F32, pre)
        hid = sb("hid", [G * CS, CH], F32, pre)
        hidT = sb("hidT", [P, 2, 2, P], F32, pre)
        kcr = sb("kcr", [P, 3, HD], F32, pre)
        tri = kcr[:, 0:2].rearrange("p a d -> p (a d)")
        kcs = sb("kcs", [P, 2, P], FR, pre)
        wg = sb("wg", [P, KT, 48], F32, pre)
        wg_hi = sb("wg_hi", [P, KT, 48], FR, pre)
        wg_lo = sb("wg_lo", [P, KT, 48], FR, pre)
        gT = sb("gT", [48, S], F32, pre)
        pre.close()
        att = ExitStack()
        prob = sb("prob", [P, NS + 1, 512], F32, att)
        prob_t = sb("prob_t", [P, 2, 512], F32, att)
        oT = sb("oT", [P, KT, S], F32, att)
        p_ct = sb("p_ct", [P, 2, 512], F32, att)
        xn_1 = p_ct[:].rearrange("p i c -> p (i c)")
        cst = sb("cst", [P, 2, 3, 16], F32, att)
        att.close()
        s_ct = oT[:].rearrange("p k s -> p (k s)")[:, 0:512]
        s_c = oT[:].rearrange("p k s -> p (k s)")[:, 512:1536].rearrange("p (i c) -> p i c", i=TT)
        nsa.close()

        hg = ExitStack()
        qa = sb("qa", [P, HH, S], F32, hg)
        kb = sb("kb", [P, HH, S], F32, hg)
        fg = sb("fg", [P, HH, S], F32, hg)
        ft = sb("ft", [P, HH, S], F32, hg)
        attn = sb("attn", [P, TT, HH, P], F32, hg)
        l_land = attn[:].rearrange("p t h q -> p (t h q)")[:, 0:len(LEVELS) * P]
        attx = sb("attx", [P, HH, P], F32, hg)
        v_hg = sb("v_hg", [P, TT, D], F32, hg)
        z_hg = sb("z_hg", [P, TT, D], F32, hg)
        y_hg = sb("y_hg", [P, TT, D], F32, hg)
        junk = sb("junk", [P, D], BF16, hg)
        hg.close()

        bank = [ctx.enter_context(nc.psum_tensor(f"bank{b}", [P, 512], F32)) for b in range(8)]

        def sem(name):
            return ctx.enter_context(nc.semaphore(name))

        raw_in = [sem(f"raw_in{i}") for i in range(NRAW)]
        first_in = [sem(f"first_in{q}") for q in range(NQ)]
        w1_in = [sem(f"w1_in{kv}") for kv in range(2)]
        x_in = [sem(f"x_in{t}") for t in range(TT)]
        const_in = sem("const_in")
        rope_in = sem("rope_in")
        levels_in = sem("levels_in")
        masks_cast = sem("masks_cast")
        wg_in = sem("wg_in")
        g_in = [sem(f"g_in{i}") for i in range(4)]
        hi_done = sem("hi_done")
        lo_done = sem("lo_done")
        ident_in = sem("ident_in")
        pv_done = sem("pv_done")
        vec_step = sem("vec_step")
        act_step = sem("act_step")
        filled = [sem(f"filled{b}") for b in range(8)]
        drained = [sem(f"drained{b}") for b in range(8)]
        taken_hi = sem("taken_hi")
        idents = sem("idents")
        eps_set = sem("eps_set")
        sumsq = sem("sumsq")
        root = sem("root")
        rp_zero = sem("rp_zero")
        x_g = sem("x_g")
        rstd = sem("rstd")
        normed = sem("normed")
        x_w = sem("x_w")
        normed_b = sem("normed_b")
        r_ab = sem("r_ab")
        r_sum = sem("r_sum")
        r_hi = sem("r_hi")
        r_lo = sem("r_lo")
        flat_zero = sem("flat_zero")
        kc_v = sem("kc_v")
        zeros = sem("zeros")
        wg_hi_d = sem("wg_hi_d")
        wg_lo_d = sem("wg_lo_d")
        gate_v = sem("gate_v")
        cmp_v = sem("cmp_v")
        cmp_exp = sem("cmp_exp")
        cmp_scaled = sem("cmp_scaled")
        rowmax = sem("rowmax")
        recip_d = sem("recip_d")
        scale_d = sem("scale_d")
        scaled = sem("scaled")
        z_silu = sem("z_silu")
        y_hi = sem("y_hi")
        y_lo = sem("y_lo")
        lb_v = sem("lb_v")
        lb_e = sem("lb_e")
        f_lin = sem("f_lin")
        k_lin = sem("k_lin")
        q_f = sem("q_f")
        qa_up = sem("qa_up")
        kb_up = sem("kb_up")
        ft_up = sem("ft_up")
        z_g = sem("z_g")
        o_sq = sem("o_sq")
        o_sum = sem("o_sum")
        o_root = sem("o_root")
        o_rstd = sem("o_rstd")
        o_norm = sem("o_norm")
        done_row = sem("done_row")
        out_done = sem("out_done")

        def wait_full(eng, key):
            b, k = USES[key]
            eng.wait_ge(filled[b], k + 1)

        def wait_taken(eng, key):
            b, k = USES[key]
            eng.wait_ge(drained[b], k + 1)

        def taken(key):
            return drained[USES[key][0]]

        def bk(key):
            return bank[USES[key][0]]

        def wait_residual(eng, u, t):
            wait_taken(eng, ("pa", u, t))
            wait_taken(eng, ("pa", u + 1, t))

        def wait_unit_used(eng, u):
            wait_full(eng, bank_key(SCHEDULE[UNIT_LAST[u]][0]))

        def wait_pv(eng, it):
            if it == JOB_LAST[ITEM_JOB[it]]:
                wait_full(eng, ("pv", ITEM_JOB[it]))
            else:
                eng.wait_ge(pv_done, it + 1 - sum(j < it for j in JOB_LAST))

        def bc(ap, n, at):
            shape = list(ap.shape)
            return ap.unsqueeze(at).broadcast_to(shape[:at] + [n] + shape[at:])

        def level_totals(s, hh):
            hs = slice(4 * hh, 4 * hh + 4)
            if s == 1:
                return fg[:, hs]
            at = S - 2 * S // s
            return ft[:, hs, at:at + S // s]

        def skipped(lv):
            return LEVELS[lv - 1] if lv and LEVELS[lv - 1] >= 16 else 0

        def totals(s, hh):
            return level_totals(s, hh).rearrange("p h (b u) -> p h b u", u=2)

        def scale_item(pool, it):
            pool.wait_ge(scale_d, it + 1)
            nb = 4 if ITEMS[it][0] == 0 else 2
            v = lambda ap: ap.rearrange("p (a b) -> p a b", a=nb)
            pb_ = prob[:, it % (NS + 1)]
            nc.gpsimd.tensor_tensor(v(pb_), v(pb_), bc(scl[:, it, 0:nb], 512 // nb, 2),
                                    ALU.mult).then_inc(scaled, 1)

        def split_parts(u, q):
            if u not in (U_Z0, U_Z1):
                sl = slice(2 * q, 2 * q + 2)
                return [(w_hi[:, u % 2, sl], raw[:, u % NRAW, sl], w_lo[:, u % 2, sl])]
            tile = lambda w, kk: w[:, u % 2, kk].rearrange("p (r g d) -> p r g d", r=R, d=HD)
            return [(tile(w_hi, kk), raw[:, u % NRAW, kk].rearrange("p (g r d) -> p r g d", r=R, d=HD), tile(w_lo, kk))
                    for kk in (2 * q, 2 * q + 1)]

        CONST_LOADS = [(rope_c[:], t_in["c_rope_c"]), (c_mask[:], t_in["c_mask"]),
                       (c_valid[:], t_in["c_valid"]), (tri, t_in["c_tri"]),
                       (pe_t[:], t_in["pe"]), (lbl[:], t_in["lb"]),
                       (w2[:, 0], t_in["w2k"].rearrange("(c p) d -> p c d", p=P)),
                       (w2[:, 1], t_in["w2v"].rearrange("(c p) d -> p c d", p=P))]
        N_CONST = len(CONST_LOADS)

        STAGE = [(U_KS, 0), (U_KS, 1), (U_KW, 0), (U_KW, 1), (U_Q0, 0), (U_Q0, 1), (U_Q1, 0), (U_Q1, 1)]
        block = ctx.enter_context(nc.Block())

        def load_w1(eng, kv):
            w = t_in["w1" + kv].rearrange("(a j d) h -> a d j h", a=2, d=HD)
            for a in range(2):
                eng.dma_start(w1[a * HD:(a + 1) * HD], w[a]).then_inc(w1_in["kv".index(kv)], 16)

        @block.sync
        def _(sp):
            sp.dma_start(x[:, 0], t_in["x"][0:P, :]).then_inc(x_in[0], 16)
            sp.dma_start(ident[:], t_in["ident"]).then_inc(ident_in, 16)
            for u, (kind, col) in enumerate(UNITS):
                if u == 1:
                    sp.dma_start(rope[:], t_in["c_rope"]).then_inc(rope_in, 16)
                if u == NRAW:
                    sp.dma_start(wg[:], t_in["nsa"][:, NSA_GL:NSA_Z].rearrange("(k p) n -> p k n", p=P)).then_inc(wg_in, 16)
                    for dst, src in CONST_LOADS:
                        sp.dma_start(dst, src).then_inc(const_in, 16)
                    load_w1(sp, "k")
                if u >= NRAW:
                    sp.wait_ge(lo_done, NQ * (u - NRAW + 1))
                dst = raw[:, u % NRAW]
                w = t_in[kind][:, col:col + UW]
                if kind == "nsa_out":
                    w = w.rearrange("(gp g2 r d) n -> g2 d gp r n", gp=2, g2=2, r=R)
                    for g2 in range(2):
                        for gp in range(2):
                            sp.dma_start(dst[g2 * HD:(g2 + 1) * HD, gp * R:(gp + 1) * R], w[g2][:, gp]).then_inc(raw_in[u % NRAW], 16)
                    continue
                w = w.rearrange("(k p) n -> p k n", p=P)
                if u == 0:
                    for q in range(NQ):
                        sp.dma_start(dst[:, 2 * q:2 * q + 2], w[:, 2 * q:2 * q + 2]).then_inc(first_in[q], 16)
                    continue
                for half in range(2):
                    sp.dma_start(dst[:, 4 * half:4 * half + 4], w[:, 4 * half:4 * half + 4]).then_inc(raw_in[u % NRAW], 16)
            for t in range(TT):
                for half in range(2):
                    c = slice(half * UW, (half + 1) * UW)
                    sp.wait_ge(done_row, 2 * t + half + 1)
                    sp.dma_start(out[t * P:(t + 1) * P, c], y_hg[:, t, c]).then_inc(out_done, 16)
            sp.wait_ge(out_done, 32 * TT)

        def raw_count(u):
            return 16 * sum(4 if UNITS[m][0] == "nsa_out" else 2 for m in range(u % NRAW, u + 1, NRAW) if m)

        @block.tensor
        def _(pe):
            def mm(o, lhsT, rhs, start, stop):
                return nc.tensor.matmul(o, lhsT, rhs, start=start, stop=stop, skip_group_check=True)

            def parts(u, kk):
                pe.wait_ge(lo_done, NQ * u + kk // 2 + 1)

            def act_ready(L, t, u):
                if u in (U_O0, U_O1):
                    pe.wait_ge(y_lo, 2 * t + 2)
                elif u in (V_O0, V_O1):
                    for q in range(2):
                        wait_taken(pe, ("yT", t, q))
                else:
                    for q in range(2):
                        wait_taken(pe, ("hT", L, t, q))

            for n, (step, banks) in enumerate(SCHEDULE):
                kind = step[0]
                key = bank_key(step)
                if kind == "idle":
                    if step[1] == 0:
                        pe.wait_ge(rp_zero, 1)
                    for _ in range(IDLE[step[1]]):
                        mm(bank[0][:, 0:S], rp[:, 0, 0:P], rp[:, 0, 0:S], True, True)
                    continue
                b, k = USES[key]
                ps = bank[b]
                first = not any(bank_key(s) == key for s, _ in SCHEDULE[:n])
                last_of_bank = LAST[key] == n
                if first and k > 0:
                    pe.wait_ge(drained[b], k)
                if kind == "hT":
                    _, L, t, q = step
                    if (L, t) == (0, 1):
                        pe.wait_ge(normed_b, 1)
                    else:
                        pe.wait_ge(normed, t + 1 + L)
                    if step == ("hT", 0, 0, 0):
                        pe.wait_ge(ident_in, 16)
                    src = xn[:, t] if L == 0 else xn_1 if t == 0 else y_hg[:, t]
                    for j in range(4):
                        c = (4 * q + j) * P
                        m = nc.tensor.transpose(ps[:, j * P:(j + 1) * P], src[:, c:c + P], ident[:])
                elif kind == "pa":
                    _, u, t, sl = step
                    if sl == 0:
                        act_ready(0 if u <= U_O1 else 1, t, u)
                    for kk in (2 * sl, 2 * sl + 1):
                        parts(u, kk)
                        hi = h_hi[:, kk, t * P:(t + 1) * P]
                        mm(ps[:], hi, w_hi[:, u % 2, kk], kk == 0, False)
                        mm(ps[:], hi, w_lo[:, u % 2, kk], False, False)
                        m = mm(ps[:], h_lo[:, kk, t * P:(t + 1) * P], w_hi[:, u % 2, kk], False, kk == KT - 1)
                elif kind == "pb":
                    _, u, m2, sl = step
                    if m2 == 0 and sl == 0:
                        for t in range(TT):
                            act_ready(0 if u <= U_O1 else 1, t, u)
                    j = 2 * m2 + sl // 2
                    for kk in range(4 * (sl % 2), 4 * (sl % 2) + 4):
                        parts(u, kk)
                        o = ps[:, (j % 2) * S:(j % 2 + 1) * S]
                        cols = lambda w: w[:, u % 2, kk, j * P:(j + 1) * P]
                        mm(o, cols(w_hi), h_hi[:, kk], kk == 0, False)
                        mm(o, cols(w_hi), h_lo[:, kk], False, False)
                        m = mm(o, cols(w_lo), h_hi[:, kk], False, kk == KT - 1)
                elif kind == "stage":
                    _, j, half = step
                    pe.wait_ge(r_lo, j + 1)
                    if j == 0 and half == 0:
                        pe.wait_ge(idents, 1)
                    for c in range(4):
                        m = nc.tensor.transpose(ps[:, c * P:(c + 1) * P].bitcast(FR), stg[:, j % 2, 4 * half + c], ident_r[:])
                elif kind == "cmp1":
                    kv = step[1]
                    wait_taken(pe, ("pb", U_KC, kv))
                    pe.wait_ge(flat_zero, 1)
                    pe.wait_ge(w1_in[kv], 32)
                    for j in range(CS):
                        m = mm(ps[0:G * CS, 0:CH], flat[:, kv, j].rearrange("p g n -> p (g n)"), w1[:, j], j == 0, j == CS - 1)
                elif kind == "cmpT":
                    kv = step[1]
                    wait_taken(pe, ("cmp1", kv))
                    for c in range(2):
                        m = nc.tensor.transpose(ps[:, c * HD:(c + 1) * HD], hid[:, c * P:(c + 1) * P], ident[0:HD, 0:HD])
                elif kind == "cmp2":
                    kv = step[1]
                    if kv == 0:
                        pe.wait_ge(const_in, 16 * N_CONST)
                    wait_taken(pe, ("cmpT", kv))
                    for c in range(2):
                        m = mm(ps[:, 0:HD], hidT[:, kv, c], w2[:, kv, c], c == 0, c == 1)
                elif kind == "kcT":
                    pe.wait_ge(kc_v, 1)
                    for c in range(2):
                        m = nc.tensor.transpose(ps[:, c * P:(c + 1) * P].bitcast(FR), kcs[:, c], ident_r[:])
                elif kind == "gl":
                    pe.wait_ge(wg_lo_d, 1)
                    for kk in range(KT):
                        mm(ps[0:48, 0:S], wg_hi[:, kk], h_hi[:, kk], kk == 0, False)
                        mm(ps[0:48, 0:S], wg_hi[:, kk], h_lo[:, kk], False, False)
                        m = mm(ps[0:48, 0:S], wg_lo[:, kk], h_hi[:, kk], False, kk == KT - 1)
                elif kind == "glT":
                    wait_taken(pe, ("gl",))
                    for t in range(TT):
                        m = nc.tensor.transpose(ps[:, t * 48:(t + 1) * 48], gT[:, t * P:(t + 1) * P], ident[0:48, 0:48])
                elif kind == "sc":
                    i = step[1]
                    wait_taken(pe, ("kcT",))
                    for j in range(4 + i, 8, 2):
                        for half in range(2):
                            wait_taken(pe, ("stage", j, half))
                    for g in range(G):
                        for part in range(2):
                            m = mm(ps[:], kc_pad[:, part, g], q2[:, g * R:(g + 1) * R, i * P:(i + 1) * P],
                                   g == 0 and part == 0, g == G - 1 and part == 1)
                elif kind == "scT":
                    i = step[1]
                    wait_taken(pe, ("sc", i))
                    for r in range(R):
                        m = nc.tensor.transpose(ps[:, r * P:(r + 1) * P], s_ct[:, r * P:(r + 1) * P], ident[:])
                elif kind == "pcT":
                    i = step[1]
                    pe.wait_ge(cmp_scaled, i + 1)
                    for r in range(R):
                        m = nc.tensor.transpose(ps[:, r * P:(r + 1) * P], s_c[:, i, r * P:(r + 1) * P], ident[:])
                elif kind == "s":
                    i, gp, g, rp_, br = ITEMS[step[1]]
                    if step[1] == 0:
                        for half in range(2):
                            wait_taken(pe, ("stage", 7, half))
                        pe.wait_ge(idents, 3)
                    for r2 in range(2):
                        h = g * R + 2 * rp_ + r2
                        for part in range(2):
                            keys = k2[:, part, :, g, 0:P] if i == 0 else k2[:, part, br, g]
                            mm(ps[:, r2 * S:(r2 + 1) * S], q2[:, h, i * P:(i + 1) * P], keys, r2 == 0 and part == 0, False)
                    if i == 0:
                        m = mm(ps[:], ident_b[:], bc(tri_b[:], 4, 1), False, True)
                    else:
                        m = mm(ps[:].rearrange("p (r k q) -> p r k q", r=2, k=2)[:, :, 1], ident_b[:], bc(tri_b[:], 2, 1), False, True)
                elif kind == "pt":
                    it = step[1]
                    pe.wait_ge(scaled, it + 1)
                    for c in range(4):
                        m = nc.tensor.transpose(ps[:, c * P:(c + 1) * P], prob[:, it % (NS + 1), c * P:(c + 1) * P], ident[:])
                elif kind == "pv":
                    it = step[1]
                    i, gp, g, rp_, br = ITEMS[it]
                    if first:
                        wait_taken(pe, ("cmp2", 1))
                        wait_taken(pe, ("pcT", i))
                        mm(ps[:], vc_bd[:, gp], p_ct[:, i], True, False)
                    wait_taken(pe, ("pt", it))
                    for c in range(4):
                        r2, c2 = c // 2, c % 2
                        vb, kt = (c2, 0) if i == 0 else (br, c2)
                        r = 2 * rp_ + r2
                        o = ps[(g % 2) * HD:(g % 2 + 1) * HD, r * P:(r + 1) * P]
                        m = mm(o, v_tok[:, kt, vb, g], prob_t[:, it % 2, c * P:(c + 1) * P], False, last_of_bank)
                elif kind == "lev":
                    _, lv, hh, c = step
                    if lv == 0:
                        for m2 in range(2):
                            wait_taken(pe, ("pb", (V_Q0, V_Q1)[hh], m2))
                        pe.wait_ge(k_lin, hh + 1)
                    elif lv == 1:
                        pe.wait_ge(q_f, hh + 1)
                    else:
                        pe.wait_ge(qa_up, 2 * (lv - 2) + hh + 1)
                        pe.wait_ge(kb_up, 2 * (lv - 2) + hh + 1)
                    for j in range(4):
                        h = 4 * hh + j
                        s = skipped(lv)
                        m = mm(ps[0:P - s, j * P + s:(j + 1) * P], kb[:, h, c * P:(c + 1) * P - s], qa[:, h, c * P + s:(c + 1) * P],
                               True, True)
                elif kind == "cross":
                    hh = step[1]
                    lv = len(STEPS_L)
                    pe.wait_ge(qa_up, 2 * (lv - 2) + hh + 1)
                    pe.wait_ge(kb_up, 2 * (lv - 2) + hh + 1)
                    for j in range(4):
                        h = 4 * hh + j
                        m = mm(ps[:, j * P:(j + 1) * P], kb[:, h, 0:P], qa[:, h, P:2 * P], j == 0, j == 3)
                elif kind == "o":
                    _, c, hh = step
                    wait_taken(pe, ("lev", len(STEPS_L) - 1, hh, c))
                    if c == 1:
                        wait_taken(pe, ("cross", hh))
                    for j in range(4):
                        h = 4 * hh + j
                        o = ps[:, j * P:(j + 1) * P]
                        m = mm(o, attn[:, c, h], v_hg[:, c, h * P:(h + 1) * P], j == 0, c == 0 and j == 3)
                        if c == 1:
                            m = mm(o, attx[:, h], v_hg[:, 0, h * P:(h + 1) * P], False, j == 3)
                elif kind == "yT":
                    _, c, q = step
                    pe.wait_ge(o_norm, 2 * c + q + 1)
                    for j in range(4):
                        col = (4 * q + j) * P
                        m = nc.tensor.transpose(ps[:, j * P:(j + 1) * P], y_hg[:, c, col:col + P], ident[:])
                if last_of_bank:
                    m.then_inc(filled[b], 1)
                elif kind == "pv":
                    m.then_inc(pv_done, 1)

        HI_KEYS = [step for step, _ in SCHEDULE if step[0] in ("hT", "yT")]

        def squares(act, norm, t):
            unused = stg[:, 0].rearrange("p c q -> p (c q)") if norm == 0 else xn_1 if (norm, t) == (1, 0) else junk[:]
            nc.scalar.activation(unused, x[:, t], ACT.Square, accum_out=stat[:, norm, 0, t:t + 1]).then_inc(sumsq, 1)
            act.wait_ge(sumsq, TT * norm + t + 1)
            act.wait_ge(eps_set, 1)
            nc.scalar.activation(stat[:, norm, 1, t:t + 1], stat[:, norm, 0, t:t + 1], ACT.Sqrt,
                                 scale=1.0 / D, bias=eps_t[:]).then_inc(root, 1)

        @block.scalar
        def _(act):
            def split_hi(u, quarters=range(NQ)):
                if u >= 2:
                    wait_unit_used(act, u - 2)
                if u:
                    act.wait_ge(raw_in[u % NRAW], raw_count(u))
                for q in quarters:
                    if u == 0:
                        act.wait_ge(first_in[q], 16)
                    for dst, src, _ in split_parts(u, q):
                        m = nc.scalar.activation(dst, src, ACT.Copy)
                    m.then_inc(hi_done, 1)

            act.dma_start(x[:, 1], t_in["x"][P:2 * P, :]).then_inc(x_in[1], 16)
            act.wait_ge(eps_set, 1)
            nc.scalar.activation(rsum[:, 0, 0:1], eps_t[:], ACT.Sqrt).then_inc(act_step, 1)
            for t in range(TT):
                act.wait_ge(x_in[t], 16)
                if t:
                    act.wait_ge(root, t)
                squares(act, 0, t)
            for n, (step, _) in enumerate(SCHEDULE):
                kind, key = step[0], bank_key(step)
                if LAST.get(key) == n:
                    ps = bk(key)
                    if kind == "hT" or kind == "yT":
                        t, q = (step[2], step[3]) if kind == "hT" else (step[1], step[2])
                        wait_full(act, key)
                        nc.scalar.activation(h_hi[:, 4 * q:4 * q + 4, t * P:(t + 1) * P],
                                             ps[:].rearrange("p (k s) -> p k s", k=4), ACT.Copy).then_inc(taken_hi, 1)
                        if step == ("hT", 0, 0, 1):
                            split_hi(0)
                        if step == ("hT", 0, 1, 1):
                            act.wait_ge(ident_in, 16)
                            nc.scalar.activation(ident_r[:], ident[:], ACT.Copy).then_inc(idents, 1)
                            nc.scalar.activation(ident_b[:], ident[:], ACT.Copy).then_inc(idents, 1)
                            split_hi(1)
                    elif kind == "pa" and step[1] in (U_KS, U_KW, U_Q0, U_Q1):
                        j = STAGE.index(step[1:3])
                        if j >= 2:
                            wait_full(act, ("stage", j - 2, 1))
                        act.wait_ge(r_sum, j + 1)
                        if step[1] in (U_KS, U_KW):
                            nc.scalar.activation(stg[:, j % 2, 0:4].rearrange("p g (u d) -> p g u d", u=2),
                                                 bc(rp[:, 2, 0:G * HD].rearrange("p (g d) -> p g d", d=HD), 2, 2), ACT.Copy).then_inc(r_hi, 1)
                        else:
                            nc.scalar.activation(stg[:, j % 2, :, 0:HD], rp[:, 2].rearrange("p (h d) -> p h d", d=HD), ACT.Copy).then_inc(r_hi, 1)
                        if key == ("pa", U_KS, 1):
                            act.wait_ge(wg_in, 16)
                            nc.scalar.activation(wg_hi[:], wg[:], ACT.Copy).then_inc(wg_hi_d, 1)
                            act.wait_ge(const_in, 16 * N_CONST)
                            nc.scalar.activation(tri_b[:], tri, ACT.Copy).then_inc(idents, 1)
                    elif kind == "stage":
                        _, j, half = step
                        u, t = STAGE[j]
                        wait_full(act, key)
                        if u in (U_KS, U_KW):
                            dst = k2[:, half, (U_KS, U_KW).index(u), :, t * P:(t + 1) * P]
                        else:
                            h0 = 8 * (u - U_Q0) + 4 * half
                            dst = q2[:, h0:h0 + 4, t * P:(t + 1) * P]
                        nc.scalar.activation(dst, ps[:].rearrange("p (k s) -> p k s", k=4), ACT.Copy).then_inc(taken(key), 1)
                    elif kind == "cmp1":
                        if step[1]:
                            wait_full(act, ("cmpT", 0))
                        wait_full(act, key)
                        nc.scalar.activation(hid[:], ps[0:G * CS, 0:CH], ACT.Silu).then_inc(taken(key), 1)
                        if step[1] == 0:
                            load_w1(act, "v")
                    elif kind == "cmpT":
                        act.wait_ge(zeros, 3)
                        wait_full(act, key)
                        nc.scalar.activation(hidT[:, step[1]].rearrange("p c (g n) -> p (c g) n", g=G)[:, :, 0:CS],
                                             ps[:, 0:2 * HD].rearrange("p (c n) -> p c n", n=CS), ACT.Copy).then_inc(taken(key), 1)
                    elif kind == "gl":
                        wait_full(act, key)
                        nc.scalar.activation(gT[:], ps[0:48, 0:S], ACT.Sigmoid).then_inc(taken(key), 1)
                    elif kind == "glT":
                        wait_full(act, key)
                        nc.scalar.activation(gate[:], ps[:, 0:TT * 48].rearrange("p (t c) -> p t c", t=TT), ACT.Copy).then_inc(taken(key), 1)
                    elif kind == "kcT":
                        act.wait_ge(zeros, 3)
                        wait_full(act, key)
                        for part in range(2):
                            for g in range(G):
                                m = nc.scalar.activation(kc_pad[:, part, g, g * NP_:(g + 1) * NP_],
                                                         ps[:, part * P + g * NP_:part * P + (g + 1) * NP_], ACT.Copy)
                                if part == 1 and g == G - 1:
                                    m.then_inc(taken(key), 1)
                    elif kind == "sc":
                        wait_full(act, key)
                        nc.scalar.activation(s_ct, ps[:], ACT.Copy).then_inc(taken(key), 1)
                        if step[1] == 0:
                            act.wait_ge(lb_v, 1)
                            nc.scalar.activation(lb[:, 1:3], lb[:, 1:3], ACT.Exp).then_inc(lb_e, 1)
                    elif kind == "scT":
                        act.wait_ge(cmp_v, step[1] + 1)
                        nc.scalar.activation(s_c[:, step[1]], s_c[:, step[1]], ACT.Exp).then_inc(cmp_exp, 1)
                    elif kind == "pcT":
                        wait_full(act, key)
                        nc.scalar.activation(p_ct[:, step[1]], ps[:], ACT.Copy).then_inc(taken(key), 1)
                    elif kind == "pt" and step[1] in ACT_TURNS:
                        it = step[1]
                        wait_pv(act, it - 2)
                        wait_full(act, key)
                        nc.scalar.activation(prob_t[:, it % 2], ps[:], ACT.Copy).then_inc(taken(key), 1)
                    elif kind == "s":
                        it = step[1]
                        i = ITEMS[it][0]
                        if it >= NS + 1:
                            wait_full(act, ("pt", it - NS - 1))
                        act.wait_ge(rowmax, it + 1)
                        nb = 4 if i == 0 else 2
                        w = 512 // nb
                        for c in range(nb):
                            m = nc.scalar.activation(prob[:, it % (NS + 1), c * w:(c + 1) * w], ps[:, c * w:(c + 1) * w], ACT.Exp,
                                                     bias=nmax[:, it, c:c + 1], accum_out=rsum[:, it, c:c + 1])
                        m.then_inc(taken(key), 1)
                    elif kind == "pb" and step[1] in (U_Z0, U_Z1):
                        u, m2 = step[1], step[2]
                        if u == U_Z0 and m2 == 0:
                            wait_full(act, ("hT", 0, 1, 1))
                        wait_full(act, key)
                        r0 = 4 * (u - U_Z0) + 2 * m2
                        z_rows = lambda r: zT[:, r:r + 2].rearrange("p k s -> p (k s)")
                        held = u == U_Z1 and m2 == 0
                        nc.scalar.activation(z_rows(r0), ps[:], ACT.Copy if held else ACT.Silu).then_inc(taken(key), 1)
                        if u == U_Z1 and m2 == 1:
                            wait_taken(act, ("pb", U_Z1, 0))
                            nc.scalar.activation(z_rows(r0 - 2), z_rows(r0 - 2), ACT.Silu).then_inc(z_silu, 1)
                    elif kind == "pa" and step[1] in (V_V0, V_V1):
                        u, t = step[1], step[2]
                        wait_full(act, key)
                        nc.scalar.activation(v_hg[:, t, (u - V_V0) * UW:(u - V_V0 + 1) * UW], ps[:], ACT.Copy).then_inc(taken(key), 1)
                    elif kind == "pb" and step[1] in (V_F0, V_F1, V_Q0, V_Q1):
                        u, m2 = step[1], step[2]
                        is_f = u in (V_F0, V_F1)
                        h0 = 4 * (u in (V_F1, V_Q1)) + 2 * m2
                        wait_full(act, key)
                        nc.scalar.activation((fg if is_f else qa)[:, h0:h0 + 2], ps[:].rearrange("p (k s) -> p k s", k=2),
                                             ACT.Sigmoid if is_f else ACT.Silu).then_inc(taken(key), 1)
                    elif kind == "pa" and step[1] in (V_Z0, V_Z1):
                        u, t = step[1], step[2]
                        wait_full(act, key)
                        nc.scalar.activation(z_hg[:, t, (u - V_Z0) * UW:(u - V_Z0 + 1) * UW], ps[:], ACT.Silu).then_inc(taken(key), 1)
                    elif kind == "o":
                        _, c, hh = step
                        o = 2 * c + hh
                        wait_full(act, key)
                        sq = fg[:].rearrange("p h s -> p (h s)")[:, o * 512:(o + 1) * 512]
                        nc.scalar.activation(sq, ps[:], ACT.Square).then_inc(o_sq, 1)
                        if hh == 1:
                            act.wait_ge(o_sum, 2 * c + 2)
                            nc.scalar.activation(ostat[:, c, 1], ostat[:, c, 0], ACT.Sqrt, scale=1.0 / P, bias=eps_t[:]).then_inc(o_root, 1)
                    elif kind == "pv":
                        i, gp = JOBS[key[1]]
                        half = (slice(None), slice(4 * gp, 4 * gp + 4), slice(i * P, (i + 1) * P))
                        wait_taken(act, key)
                        nc.scalar.activation(h_hi[half], oT[half], ACT.Copy).then_inc(y_hi, 1)
                    if key == ("pb", V_F0, 0):
                        act.wait_ge(levels_in, 16)
                        nc.scalar.activation(l_mask[:].rearrange("p l q -> p (l q)"), l_land, ACT.Copy).then_inc(masks_cast, 1)
                    if key == ("pa", U_O1, 0):
                        wait_residual(act, U_O0, 0)
                        squares(act, 1, 0)
                        act.wait_ge(y_lo, 4)
                    if key == ("pa", U_O1, 1):
                        act.wait_ge(root, TT + 1)
                        wait_residual(act, U_O0, 1)
                        squares(act, 1, 1)
                    if kind == "pa" and step[1] == V_O0:
                        t = step[2]
                        wait_taken(act, key)
                        st = lambda k: stat[:, 2, k, t:t + 1]
                        nc.scalar.activation(junk[:, 0:UW], x[:, t, 0:UW], ACT.Square, accum_out=st(3)).then_inc(act_step, 1)
                        act.wait_ge(act_step, 2 + 2 * t)
                        nc.scalar.activation(st(4), st(3), ACT.Identity, scale=1.0 / D, bias=eps_t[:]).then_inc(act_step, 1)
                    if kind == "pa" and step[1] == V_O1:
                        t = step[2]
                        wait_taken(act, key)
                        nc.scalar.activation(junk[:, UW:D], x[:, t, UW:D], ACT.Square, accum_out=st(0)).then_inc(sumsq, 1)
                        act.wait_ge(sumsq, 2 * TT + t + 1)
                        act.wait_ge(act_step, 3 + 2 * t)
                        nc.scalar.activation(st(1), st(0), ACT.Sqrt, scale=1.0 / D, bias=st(4)).then_inc(root, 1)
                for u, q in SPLIT_HI_AT.get(n, []):
                    split_hi(u, [q])

        @block.vector
        def _(dve):
            steps = [0]

            def step_(ins):
                ins.then_inc(vec_step, 1)
                steps[0] += 1

            def settled():
                dve.wait_ge(vec_step, steps[0])

            V = nc.vector

            def split_lo(u, quarters=range(NQ)):
                for q in quarters:
                    dve.wait_ge(hi_done, NQ * u + q + 1)
                    for hi, src, lo in split_parts(u, q):
                        m = V.tensor_tensor(lo, src, hi.bitcast(F32), ALU.subtract)
                    m.then_inc(lo_done, 1)

            def gated_lo(job):
                i, gp = JOBS[job]
                half = (slice(None), slice(4 * gp, 4 * gp + 4), slice(i * P, (i + 1) * P))
                dve.wait_ge(y_hi, job + 1)
                V.tensor_tensor(h_lo[half], oT[half], h_hi[half].bitcast(F32), ALU.subtract).then_inc(y_lo, 1)

            def norm(nrm, t, dst, g_n, sig):
                dve.wait_ge(root, TT * nrm + t + 1)
                V.reciprocal(stat[:, nrm, 2, t:t + 1], stat[:, nrm, 1, t:t + 1]).then_inc(rstd, 1)
                dve.wait_ge(rstd, TT * nrm + t + 1)
                dve.wait_ge(g_in[g_n], 16)
                V.scalar_tensor_tensor(dst, x[:, t], stat[:, nrm, 2, t:t + 1], g_row[:], ALU.mult, ALU.mult).then_inc(sig, 1)

            def item_scale(it):
                i, gp, g, rp_, br = ITEMS[it]
                nb = 4 if i == 0 else 2
                wait_taken(dve, ("s", it))
                V.reciprocal(rrec[:, it, 0:nb], rsum[:, it, 0:nb]).then_inc(recip_d, 1)
                dve.wait_ge(recip_d, it + 1)
                h0 = g * R + 2 * rp_
                gv = gate[:, i].rearrange("p (h b) -> p h b", b=3)[:, h0:h0 + 2]
                if i == 0:
                    V.tensor_tensor(scl[:, it].rearrange("p (r b) -> p r b", r=2), rrec[:, it].rearrange("p (r b) -> p r b", r=2),
                                    gv[:, :, 1:3], ALU.mult).then_inc(scale_d, 1)
                else:
                    V.tensor_tensor(scl[:, it, 0:2], rrec[:, it, 0:2], gv[:, :, 1 + br], ALU.mult).then_inc(scale_d, 1)

            V.memset(eps_t[:], EPS).then_inc(eps_set, 1)
            V.memset(rp[:, 0, 0:S], 0.0).then_inc(rp_zero, 1)
            norm(0, 0, xn[:, 0], 0, normed)
            dve.wait_ge(root, 2)
            V.reciprocal(stat[:, 0, 2, 1:2], stat[:, 0, 1, 1:2]).then_inc(rstd, 1)
            for n, (step, _) in enumerate(SCHEDULE):
                kind, key = step[0], bank_key(step)
                if LAST.get(key) == n:
                    ps = bk(key)
                    if kind == "hT" or kind == "yT":
                        t, q = (step[2], step[3]) if kind == "hT" else (step[1], step[2])
                        dve.wait_ge(taken_hi, HI_KEYS.index(step) + 1)
                        hs = (slice(None), slice(4 * q, 4 * q + 4), slice(t * P, (t + 1) * P))
                        V.tensor_tensor(h_lo[hs], ps[:].rearrange("p (k s) -> p k s", k=4), h_hi[hs].bitcast(F32),
                                        ALU.subtract).then_inc(taken(key), 1)
                        if step == ("hT", 0, 1, 1):
                            V.memset(flat[HD:P, :, :, :, NC:CS], 0.0).then_inc(flat_zero, 1)
                        if step == ("hT", 0, 0, 1):
                            split_lo(0)
                    elif kind == "pa" and step[1] in (U_KS, U_KW, U_Q0, U_Q1):
                        u, t = step[1], step[2]
                        j = STAGE.index((u, t))
                        is_k = u in (U_KS, U_KW)
                        nh = G if is_k else 8
                        if j == 0:
                            dve.wait_ge(rope_in, 16)
                            dve.wait_ge(rp_zero, 1)
                        else:
                            dve.wait_ge(r_sum, j)
                        wait_full(dve, key)
                        xin = ps[:, 0:nh * HD].rearrange("p (h d) -> p h d", d=HD)
                        a = rp[:, 0, 0:nh * HD].rearrange("p (h d) -> p h d", d=HD)
                        b_ = rp[:, 1, 0:nh * HD].rearrange("p (h d) -> p h d", d=HD)
                        co, si = (rope[:, 2, t], rope[:, 3, t]) if is_k else (rope[:, 0, t], rope[:, 1, t])
                        hf = HD // 2
                        V.tensor_tensor(a, xin, bc(co, nh, 1), ALU.mult)
                        V.tensor_tensor(b_[:, :, 0:hf], xin[:, :, hf:HD], bc(si[:, 0:hf], nh, 1), ALU.mult)
                        if is_k:
                            V.tensor_tensor(b_[:, :, hf:HD], xin[:, :, 0:hf], bc(si[:, hf:HD], nh, 1), ALU.mult).then_inc(r_ab, 1)
                            V.tensor_copy(v_tok[:, t, (U_KS, U_KW).index(u)].rearrange("p g d -> p (g d)"), ps[:, G * HD:UW]).then_inc(taken(key), 1)
                            if j == 0:
                                split_lo(1)
                            if j == 1:
                                dve.wait_ge(wg_hi_d, 1)
                                V.tensor_tensor(wg_lo[:], wg[:], wg_hi[:].bitcast(F32), ALU.subtract).then_inc(wg_lo_d, 1)
                                dve.wait_ge(const_in, 16 * N_CONST)
                                step_(V.tensor_tensor(lb[:, 0], lbl[:, 0], lbl[:, 1], ALU.max))
                                settled()
                                V.tensor_tensor(lb[:, 1:3], lbl[:], bc(lb[:, 0], 2, 1), ALU.subtract).then_inc(lb_v, 1)
                        else:
                            V.tensor_tensor(b_[:, :, hf:HD], xin[:, :, 0:hf], bc(si[:, hf:HD], nh, 1), ALU.mult).then_inc(taken(key), 1)
                    elif key[0:2] == ("pb", U_KC):
                        kv = step[2]
                        wait_full(dve, key)
                        for g in range(G):
                            src = ps[(g % 2) * HD:(g % 2 + 1) * HD, (g // 2) * S:(g // 2 + 1) * S].rearrange("p (n j) -> p j n", j=CS)
                            V.tensor_tensor(flat[0:HD, kv, :, g], src, bc(pe_t[0:HD, kv], CS, 2), ALU.add)
                            m = V.tensor_tensor(flat[HD:P, kv, :, g, 0:NC], src[:, :, 1:CS], bc(pe_t[HD:P, kv], NC, 2), ALU.add)
                        m.then_inc(taken(key), 1)
                    elif kind == "cmp2" and step[1] == 0:
                        wait_full(dve, key)
                        hf = HD // 2
                        dve.wait_ge(idents, 3)
                        step_(V.tensor_tensor(kcr[:, 0], ps[:, 0:HD], rope_c[:, 0], ALU.mult))
                        step_(V.tensor_tensor(kcr[:, 1, 0:hf], ps[:, hf:HD], rope_c[:, 1, 0:hf], ALU.mult))
                        V.tensor_tensor(kcr[:, 1, hf:HD], ps[:, 0:hf], rope_c[:, 1, hf:HD], ALU.mult).then_inc(taken(key), 1)
                        wait_taken(dve, key)
                        step_(V.tensor_tensor(kcr[:, 2], kcr[:, 0], kcr[:, 1], ALU.add))
                        settled()
                        hi2 = kcs[:, 0].rearrange("p (u d) -> p u d", u=2)
                        lo2 = kcs[:, 1].rearrange("p (u d) -> p u d", u=2)
                        step_(V.tensor_copy(hi2, bc(kcr[:, 2], 2, 1)))
                        settled()
                        V.tensor_tensor(lo2, bc(kcr[:, 2], 2, 1), hi2.bitcast(F32), ALU.subtract).then_inc(kc_v, 1)
                    elif kind == "cmp2":
                        dve.wait_ge(zeros, 3)
                        wait_full(dve, key)
                        for g in range(G):
                            m = V.tensor_copy(vc_bd[g * NP_:(g + 1) * NP_, g // 2, (g % 2) * HD:(g % 2 + 1) * HD],
                                              ps[g * NP_:(g + 1) * NP_, 0:HD])
                        m.then_inc(taken(key), 1)
                    elif kind == "glT":
                        wait_taken(dve, key)
                        gc = gate[:].rearrange("p t (h b) -> p t h b", b=3)[:, :, :, 0]
                        V.tensor_tensor(gc, gc, bc(c_valid[:], H, 2), ALU.mult).then_inc(gate_v, 1)
                    elif kind == "scT":
                        i = step[1]
                        sc = s_c[:, i].rearrange("p (a n) -> p a n", n=NP_)
                        wait_full(dve, key)
                        V.tensor_tensor(sc, ps[:].rearrange("p (a n) -> p a n", n=NP_), bc(c_mask[:, i], H, 1), ALU.add).then_inc(taken(key), 1)
                        wait_taken(dve, key)
                        step_(V.tensor_reduce(cst[:, i, 0], sc, AX.X, ALU.max, negate=True))
                        settled()
                        V.tensor_tensor(sc, sc, bc(cst[:, i, 0], NP_, 2), ALU.add).then_inc(cmp_v, 1)
                        dve.wait_ge(cmp_exp, i + 1)
                        step_(V.tensor_reduce(cst[:, i, 1], sc, AX.X, ALU.add))
                        settled()
                        step_(V.reciprocal(cst[:, i, 2], cst[:, i, 1]))
                        settled()
                        dve.wait_ge(gate_v, 1)
                        gc = gate[:, i].rearrange("p (g r b) -> p r g b", g=G, b=3)[:, :, :, 0]
                        step_(V.tensor_tensor(cst[:, i, 0].rearrange("p (r g) -> p r g", g=G),
                                              cst[:, i, 2].rearrange("p (r g) -> p r g", g=G), gc, ALU.mult))
                        settled()
                        V.tensor_tensor(sc, sc, bc(cst[:, i, 0], NP_, 2), ALU.mult).then_inc(cmp_scaled, 1)
                        if i == 1:
                            dve.wait_ge(lb_e, 1)
                            for ins in (lambda: V.tensor_tensor(lb[:, 0], lb[:, 1], lb[:, 2], ALU.add),
                                        lambda: V.reciprocal(lb[:, 3], lb[:, 0]),
                                        lambda: V.tensor_tensor(lb[:, 1:3], lb[:, 1:3], bc(lb[:, 3], 2, 1), ALU.mult),
                                        lambda: V.tensor_tensor(lb[:, 3], lb[:, 1], lb[:, 2], ALU.add),
                                        lambda: V.tensor_tensor(lb[:, 4], lb[:, 3], lb[:, 1], ALU.subtract),
                                        lambda: V.tensor_scalar(lb[:, 5], lb[:, 4], -1.0, 1.0, ALU.mult, ALU.add)):
                                step_(ins())
                                settled()
                    elif kind == "s":
                        it = step[1]
                        nb = 4 if ITEMS[it][0] == 0 else 2
                        wait_full(dve, key)
                        V.tensor_reduce(nmax[:, it, 0:nb], ps[:].rearrange("p (a b) -> p a b", a=nb), AX.X, ALU.max,
                                        negate=True).then_inc(rowmax, 1)
                        if it >= 1:
                            item_scale(it - 1)
                    elif kind == "pt":
                        it = step[1]
                        if it == NI - NS:
                            item_scale(NI - 1)
                        if it not in ACT_TURNS:
                            if it >= 2:
                                wait_pv(dve, it - 2)
                            wait_full(dve, key)
                            V.tensor_copy(prob_t[:, it % 2], ps[:]).then_inc(taken(key), 1)
                    elif kind == "pv":
                        job = key[1]
                        i, gp = JOBS[job]
                        half = (slice(None), slice(4 * gp, 4 * gp + 4), slice(i * P, (i + 1) * P))
                        wait_full(dve, key)
                        dve.wait_ge(z_silu, 1)
                        for m2 in range(2):
                            wait_taken(dve, ("pb", U_Z1, m2))
                        V.tensor_tensor(oT[half], ps[:].rearrange("p (k s) -> p k s", k=4), zT[half], ALU.mult).then_inc(taken(key), 1)
                        if job == 3:
                            gated_lo(job)
                    elif kind == "pa" and step[1] in (U_O0, U_O1, V_O0, V_O1):
                        u, t = step[1], step[2]
                        c = (u - (U_O0 if u <= U_O1 else V_O0)) * UW
                        wait_full(dve, key)
                        V.tensor_tensor(x[:, t, c:c + UW], x[:, t, c:c + UW], ps[:], ALU.add).then_inc(taken(key), 1)
                        if u in (V_O0, V_O1):
                            wait_taken(dve, key)
                            dve.wait_ge(g_in[3], 16)
                            V.tensor_tensor(y_hg[:, t, c:c + UW], x[:, t, c:c + UW], g_row[:, c:c + UW], ALU.mult).then_inc(x_g, 1)
                        if u == V_O1:
                            dve.wait_ge(root, TT * 2 + t + 1)
                            V.reciprocal(stat[:, 2, 2, t:t + 1], stat[:, 2, 1, t:t + 1]).then_inc(rstd, 1)
                            dve.wait_ge(rstd, TT * 2 + t + 1)
                            dve.wait_ge(x_g, 2 * t + 2)
                            for half in (y_hg[:, t, 0:UW], y_hg[:, t, UW:D]):
                                V.tensor_scalar(half, half, stat[:, 2, 2, t:t + 1], None, ALU.mult).then_inc(done_row, 1)
                    elif kind == "pb" and step[1] in (V_F0, V_F1) and step[2] == 1:
                        hh = int(step[1] == V_F1)
                        for m2 in range(2):
                            wait_taken(dve, ("pb", step[1], m2))
                        for h in range(4 * hh, 4 * hh + 4):
                            m = V.tensor_scalar(fg[:, h], fg[:, h], lb[:, 5, h:h + 1], lb[:, 4, h:h + 1], ALU.mult, ALU.add)
                        m.then_inc(f_lin, 1)
                        dve.wait_ge(f_lin, hh + 1)
                        V.tensor_scalar(kb[:, 4 * hh:4 * hh + 4], fg[:, 4 * hh:4 * hh + 4], -1.0, 1.0, ALU.mult, ALU.add).then_inc(k_lin, 1)
                    elif kind == "lev":
                        _, lv, hh, c = step
                        dst = attn[:, c, 4 * hh:4 * hh + 4]
                        src = ps[:].rearrange("p (h t) -> p h t", h=4)
                        wait_full(dve, key)
                        if lv == 0:
                            dve.wait_ge(masks_cast, 1)
                            V.tensor_tensor(dst, src, bc(ident[:], 4, 1), ALU.mult).then_inc(taken(key), 1)
                        else:
                            s = LEVELS[lv - 1]
                            keys = slice(0, P - skipped(lv))
                            cut = lambda ap: ap.rearrange("p h (b u s) -> p h b u s", u=2, s=s)[:, :, :, 1]
                            V.copy_predicated(cut(dst[keys]), cut(bc(l_mask[:, lv - 1], 4, 1)[keys]), cut(src[keys])).then_inc(taken(key), 1)
                        if c == 1:
                            hs = slice(4 * hh, 4 * hh + 4)
                            if lv == 0:
                                V.tensor_tensor(qa[:, hs], qa[:, hs], fg[:, hs], ALU.mult).then_inc(q_f, 1)
                            else:
                                half = qa[:, hs].rearrange("p h (b u s) -> p h b u s", u=2, s=s)[:, :, :, 1]
                                if lv == 1:
                                    dve.wait_ge(q_f, hh + 1)
                                else:
                                    dve.wait_ge(qa_up, 2 * (lv - 2) + hh + 1)
                                    dve.wait_ge(ft_up, 7 * hh + lv - 1)
                                V.tensor_tensor(half, half, bc(totals(s, hh)[:, :, :, 0], s, 3), ALU.mult).then_inc(qa_up, 1)
                    elif kind == "cross":
                        hh = step[1]
                        wait_full(dve, key)
                        V.tensor_copy(attx[:, 4 * hh:4 * hh + 4], ps[:].rearrange("p (h t) -> p h t", h=4)).then_inc(taken(key), 1)
                    elif kind == "o":
                        _, c, hh = step
                        o = 2 * c + hh
                        ys = y_hg[:, c, hh * UW:(hh + 1) * UW]
                        sq = fg[:].rearrange("p h s -> p (h s)")[:, o * 512:(o + 1) * 512]
                        dve.wait_ge(o_sq, o + 1)
                        V.tensor_reduce(ostat[:, c, 0, 4 * hh:4 * hh + 4], sq.rearrange("p (h v) -> p h v", h=4), AX.X, ALU.add).then_inc(o_sum, 1)
                        dve.wait_ge(z_g, Z_ORDER.index((V_Z0 + hh, c)) + 1)
                        V.tensor_tensor(ys, ps[:], z_hg[:, c, hh * UW:(hh + 1) * UW], ALU.mult).then_inc(taken(key), 1)
                        if hh == 1:
                            dve.wait_ge(o_root, c + 1)
                            V.reciprocal(ostat[:, c, 2], ostat[:, c, 1]).then_inc(o_rstd, 1)
                            dve.wait_ge(o_rstd, c + 1)
                            for half in range(2):
                                wait_taken(dve, ("o", c, half))
                                y4 = y_hg[:, c, half * UW:(half + 1) * UW].rearrange("p (h v) -> p h v", h=4)
                                V.tensor_tensor(y4, y4, bc(ostat[:, c, 2, 4 * half:4 * half + 4], P, 2), ALU.mult).then_inc(o_norm, 1)
                    if key == ("pa", U_O1, 0):
                        norm(1, 0, xn_1, 2, normed)
                    if key == ("pa", U_O1, 1):
                        norm(1, 1, y_hg[:, 1], 2, normed)
                for job in range(3):
                    if n == LAST[("pv", job)] + GATED_LAG:
                        gated_lo(job)
                for u, q in SPLIT_LO_AT.get(n, []):
                    split_lo(u, [q])

        @block.gpsimd
        def _(pool):
            GP = nc.gpsimd
            row = lambda ap: ap.unsqueeze(0).broadcast_to([P, D])
            pool.dma_start(g_row[:], row(t_in["norm_w"][0])).then_inc(g_in[0], 16)
            GP.memset(hidT[:], 0.0).then_inc(zeros, 1)
            GP.memset(kc_pad[:].bitcast(F32), 0.0).then_inc(zeros, 1)
            GP.memset(vc_bd[:], 0.0).then_inc(zeros, 1)
            pool.wait_ge(g_in[0], 16)
            pool.wait_ge(x_in[1], 16)
            GP.tensor_tensor(xn[:, 1], x[:, 1], g_row[:], ALU.mult).then_inc(x_w, 1)
            pool.wait_ge(x_w, 1)
            pool.wait_ge(rstd, 2)
            GP.tensor_scalar(xn[:, 1], xn[:, 1], stat[:, 0, 2, 1:2], None, ALU.mult).then_inc(normed_b, 1)
            pool.wait_ge(normed, 1)
            pool.dma_start(g_row[:], row(t_in["norm_w"][1])).then_inc(g_in[2], 16)

            for n, (step, _) in enumerate(SCHEDULE):
                kind, key = step[0], bank_key(step)
                if LAST.get(key) == n:
                    if kind == "pa" and step[1] in (U_KS, U_KW, U_Q0, U_Q1):
                        u, t = step[1], step[2]
                        j = STAGE.index((u, t))
                        is_k = u in (U_KS, U_KW)
                        w = (G if is_k else 8) * HD
                        if is_k:
                            pool.wait_ge(r_ab, j + 1)
                        else:
                            wait_taken(pool, key)
                        if j:
                            pool.wait_ge(r_lo, j)
                        GP.tensor_tensor(rp[:, 2, 0:w], rp[:, 0, 0:w], rp[:, 1, 0:w], ALU.add).then_inc(r_sum, 1)
                        pool.wait_ge(r_hi, j + 1)
                        if is_k:
                            v = lambda ap: ap.rearrange("p g (u d) -> p g u d", u=2)
                            GP.tensor_tensor(v(stg[:, j % 2, 4:8]), bc(rp[:, 2, 0:w].rearrange("p (g d) -> p g d", d=HD), 2, 2),
                                             v(stg[:, j % 2, 0:4]).bitcast(F32), ALU.subtract).then_inc(r_lo, 1)
                        else:
                            GP.tensor_tensor(stg[:, j % 2, :, HD:P], rp[:, 2].rearrange("p (h d) -> p h d", d=HD),
                                             stg[:, j % 2, :, 0:HD].bitcast(F32), ALU.subtract).then_inc(r_lo, 1)
                    elif kind == "pt":
                        it = step[1]
                        if it == 0:
                            for first in range(NS):
                                scale_item(pool, first)
                        if it + NS < NI:
                            scale_item(pool, it + NS)
                    elif kind == "pb" and step[1] in (V_F0, V_F1) and step[2] == 1:
                        hh = int(step[1] == V_F1)
                        pool.wait_ge(f_lin, hh + 1)
                        for lv, s in enumerate(LEVELS):
                            if lv:
                                pool.wait_ge(ft_up, 7 * hh + lv)
                            tt = totals(s, hh)
                            GP.tensor_tensor(level_totals(2 * s, hh), tt[:, :, :, 0], tt[:, :, :, 1], ALU.mult).then_inc(ft_up, 1)
                    elif kind == "lev" and step[1] >= 1 and step[3] == 1:
                        _, lv, hh, c = step
                        s = LEVELS[lv - 1]
                        wait_full(pool, key)
                        if lv == 1:
                            pool.wait_ge(k_lin, hh + 1)
                            pool.wait_ge(f_lin, hh + 1)
                        else:
                            pool.wait_ge(kb_up, 2 * (lv - 2) + hh + 1)
                            pool.wait_ge(ft_up, 7 * hh + lv - 1)
                        half = kb[:, 4 * hh:4 * hh + 4].rearrange("p h (b u s) -> p h b u s", u=2, s=s)[:, :, :, 0]
                        GP.tensor_tensor(half, half, bc(totals(s, hh)[:, :, :, 1], s, 3), ALU.mult).then_inc(kb_up, 1)
                    elif kind == "pa" and step[1] in (V_Z0, V_Z1):
                        u, t = step[1], step[2]
                        wait_taken(pool, key)
                        pool.wait_ge(g_in[1], 16)
                        zs = z_hg[:, t, (u - V_Z0) * UW:(u - V_Z0 + 1) * UW]
                        GP.tensor_tensor(zs, zs, g_row[:, (u - V_Z0) * UW:(u - V_Z0 + 1) * UW], ALU.mult).then_inc(z_g, 1)
                        if u == V_Z1 and t == 1:
                            pool.wait_ge(z_g, 4)
                            pool.dma_start(g_row[:], row(t_in["final_norm"])).then_inc(g_in[3], 16)
                    if key == ("hT", 1, 1, 1):
                        wait_full(pool, key)
                        pool.wait_ge(normed, TT + 1)
                        pool.dma_start(l_land, t_in["c_levels"].rearrange("p l q -> p (l q)")).then_inc(levels_in, 16)
                        pool.dma_start(g_row[:], row(t_in["hg_norm"])).then_inc(g_in[1], 16)


def shape_constants():
    f = np.float32
    half = HD // 2
    inv = (f(10000.0) ** (-np.arange(half, dtype=f) / f(half))).astype(f)

    def table(pos, scale):
        ang = pos.astype(f)[:, None] * inv[None, :]
        co, si = np.cos(ang), np.sin(ang)
        return np.concatenate([co, co], 1) * f(scale), np.concatenate([-si, si], 1) * f(scale)

    pos = np.arange(S)
    q, k = table(pos, HD ** -0.5), table(pos, 1.0)
    rope = np.stack([q[0], q[1], k[0], k[1]]).astype(f)
    rope = rope.reshape(4, TT, P, HD).transpose(2, 0, 1, 3)
    end = np.arange(NP_) * CS + CB - 1
    c = table(end, 1.0)
    rope_c = np.tile(np.stack(c, 1), (G, 1, 1)).astype(f)
    seen = (end[None, :] <= pos[:, None]) & (np.arange(NP_) < NC)[None, :]
    c_mask = np.where(seen, 0.0, NEG).astype(f).reshape(TT, P, NP_).transpose(1, 0, 2)
    c_valid = seen.any(1).astype(f).reshape(TT, P).T
    a = np.arange(P)
    tri = np.where(a[None, :] <= a[:, None], 0.0, NEG).astype(f)
    lm = np.stack([(a[:, None] // (2 * s) == a[None, :] // (2 * s)) & (a[:, None] // s % 2 == 0) & (a[None, :] // s % 2 == 1)
                   for s in LEVELS], 1).astype(f)
    return {"c_ident": np.eye(P, dtype=f), "c_rope": rope, "c_rope_c": rope_c, "c_mask": c_mask, "c_valid": c_valid,
            "c_tri": tri, "c_levels": lm}


def kernel(x, norm_w, nsa_w_in, nsa_pe_k, nsa_pe_v, nsa_wk1, nsa_wk2, nsa_wv1, nsa_wv2, nsa_w_out,
           hg_w_in, hg_lb_logits, hg_norm, hg_w_out, final_norm):
    import concourse.bacc as bacc
    from concourse.bass_utils import run_bass_kernel_spmd

    lay = np.ascontiguousarray
    pe_of = lambda pe: np.asarray(pe)[0].reshape(2, CS, HD).transpose(0, 2, 1).reshape(P, CS)
    arrays = {
        "x": np.asarray(x)[0], "norm_w": norm_w, "nsa": np.asarray(nsa_w_in)[0], "nsa_out": np.asarray(nsa_w_out)[0],
        "hg": np.asarray(hg_w_in)[0], "hg_out": np.asarray(hg_w_out)[0],
        "w1k": np.asarray(nsa_wk1)[0], "w1v": np.asarray(nsa_wv1)[0],
        "w2k": np.asarray(nsa_wk2)[0], "w2v": np.asarray(nsa_wv2)[0],
        "pe": np.stack([pe_of(nsa_pe_k), pe_of(nsa_pe_v)], 1),
        "lb": np.asarray(hg_lb_logits).reshape(2, HH, P).transpose(2, 0, 1),
        "hg_norm": np.asarray(hg_norm)[0], "final_norm": final_norm,
    } | shape_constants()
    arrays = {f"in_{k}": lay(v) for k, v in arrays.items()}
    nc = bacc.Bacc("TRN2", target_bir_lowering=False, num_devices=1)
    t_in = {k[3:]: nc.dram_tensor(k, v.shape, mybir.dt.from_np(v.dtype), kind="ExternalInput").ap() for k, v in arrays.items()}
    t_in["ident"] = t_in["c_ident"]
    out = nc.dram_tensor("out", (S, D), F32, kind="ExternalOutput").ap()
    program(nc, t_in, out)
    got = run_bass_kernel_spmd(nc, [arrays], core_ids=[0])
    return got.results[0]["out"].reshape(1, S, D)
```
